# Optimizing a Trainium2 kernel written in Bass

```python
import math
import jax, jax.numpy as jnp
from jax import lax
import numpy as np

D_MODEL = 1024
BATCH = 1
SEQ = 2048
DEPTH = 1

PL_DIM = 256
MIX_WIDTH = D_MODEL
DIFF_WIDTH = MIX_WIDTH // 2
RWKV_WIDTH = MIX_WIDTH - DIFF_WIDTH
DIFF_HEAD_DIM = 64
DIFF_HEADS = DIFF_WIDTH // (2 * DIFF_HEAD_DIM)
RWKV_HEAD = 64
RWKV_HEADS = RWKV_WIDTH // RWKV_HEAD
D_DECAY_LORA = 64
D_AAA_LORA = 64
D_GATE_LORA = 160
IN_COLS = 3 * DIFF_WIDTH + 3 * RWKV_WIDTH
ROPE_THETA = 10000.0
Q_BLOCK = 128
NORM_EPS = 1e-6
SUBLN_EPS = 1e-5
GN_EPS = 64e-5
N_GROUPS = 4
EXPERTS_PER_GROUP = 8
N_EXPERTS = N_GROUPS * EXPERTS_PER_GROUP
TOP_K = 2
D_EXPERT = 512
MOE_BLOCK = 128
MAX_POS_OFFSET = 1024

kernel_name = "hymba_diffattn_rwkv7_hmoe_block"

def rms_norm(x, g, eps=NORM_EPS):
    xf = x.astype(jnp.float32)
    y = xf * lax.rsqrt(jnp.mean(xf * xf, axis=-1, keepdims=True) + eps)
    return (y * g.astype(jnp.float32)).astype(x.dtype)

def token_shift(z):
    return jnp.pad(z, ((0, 0), (1, 0), (0, 0)))[:, :-1]

def rope_tables(positions):
    half = DIFF_HEAD_DIM // 2
    inv_freq = ROPE_THETA ** (-jnp.arange(half, dtype=jnp.float32) / half)
    ang = positions.astype(jnp.float32)[..., None] * inv_freq
    return jnp.cos(ang), jnp.sin(ang)

def apply_rope(t, cos, sin):
    c = cos[:, :, None, None, :]
    s = sin[:, :, None, None, :]
    t1, t2 = jnp.split(t.astype(jnp.float32), 2, axis=-1)
    return jnp.concatenate([t1 * c - t2 * s, t2 * c + t1 * s], axis=-1).astype(t.dtype)

def diff_attention(q, k, v, lam, out_g, lam_init):
    B, S = q.shape[0], q.shape[1]
    scale = DIFF_HEAD_DIM ** -0.5
    outs = []
    for start in range(0, S, Q_BLOCK):
        end = start + Q_BLOCK
        qb = q[:, start:end]
        kb = k[:, :end]
        vb = v[:, :end]
        s = jnp.einsum('bqhmd,bkhmd->bhmqk', qb, kb,
                       preferred_element_type=jnp.float32) * scale
        causal = jnp.arange(start, end)[:, None] >= jnp.arange(end)[None, :]
        s = jnp.where(causal, s, -jnp.inf)
        prob = jax.nn.softmax(s, axis=-1)
        attn = prob[:, :, 0] - lam * prob[:, :, 1]
        outs.append(jnp.einsum('bhqk,bkhe->bqhe', attn.astype(v.dtype), vb))
    o = jnp.concatenate(outs, axis=1)
    o = rms_norm(o, out_g, SUBLN_EPS) * (1.0 - lam_init)
    return o.reshape(B, S, DIFF_WIDTH)

def rwkv7_scan(r, w, k, v, a, b):
    B, S, H, N = r.shape

    def step(state, inp):
        r_t, w_t, k_t, v_t, a_t, b_t = inp
        sa = jnp.einsum('bhvk,bhk->bhv', state, a_t)
        state = (state * w_t[:, :, None, :] + sa[..., None] * b_t[:, :, None, :]
                 + v_t[..., None] * k_t[:, :, None, :])
        y = jnp.einsum('bhvk,bhk->bhv', state, r_t)
        return state, y

    xs = tuple(jnp.moveaxis(t, 1, 0) for t in (r, w, k, v, a, b))
    s0 = jnp.zeros((B, H, N, N), jnp.float32)
    _, y = lax.scan(step, s0, xs)
    return jnp.moveaxis(y, 0, 1)

def rwkv7_time_mix(h, zr, zk, zv, mu_rkv, mu_wag, w0, w1, w2, a0, a1, a2,
                   g1, g2, k_k, k_a, r_k, gn_w, gn_b):
    B, S, _ = h.shape
    H, N = RWKV_HEADS, RWKV_HEAD
    f32 = jnp.float32
    r = zr + (token_shift(zr) - zr) * mu_rkv[0]
    k = zk + (token_shift(zk) - zk) * mu_rkv[1]
    v = zv + (token_shift(zv) - zv) * mu_rkv[2]
    dh = token_shift(h) - h
    xw = h + dh * mu_wag[0]
    xa = h + dh * mu_wag[1]
    xg = h + dh * mu_wag[2]
    w_log = -jax.nn.softplus(-(w0 + jnp.tanh(xw @ w1) @ w2).astype(f32)) - 0.5
    decay = jnp.exp(-jnp.exp(w_log))
    a = jax.nn.sigmoid((a0 + (xa @ a1) @ a2).astype(f32))
    g = (jax.nn.sigmoid(xg @ g1) @ g2).astype(f32)

    def heads(t):
        return t.reshape(B, S, H, N).astype(f32)

    r, k, v, decay, a = heads(r), heads(k), heads(v), heads(decay), heads(a)
    kk = k * k_k.reshape(H, N).astype(f32)
    kk = kk * lax.rsqrt(jnp.maximum(jnp.sum(kk * kk, axis=-1, keepdims=True), 1e-24))
    k = k * (1.0 + (a - 1.0) * k_a.reshape(H, N).astype(f32))
    y = rwkv7_scan(r, decay, k, v, -kk, kk * a)
    mu = jnp.mean(y, axis=-1, keepdims=True)
    var = jnp.mean(jnp.square(y - mu), axis=-1, keepdims=True)
    y = ((y - mu) * lax.rsqrt(var + GN_EPS)).reshape(B, S, H * N)
    y = y * gn_w.astype(f32) + gn_b.astype(f32)
    bonus = jnp.sum(r * k * r_k.astype(f32), axis=-1, keepdims=True) * v
    y = y + bonus.reshape(B, S, H * N)
    return (y * g).astype(h.dtype)

def hier_moe(h, w_group, w_expert_router, w_gate, w_up, w_down):
    B, S, D = h.shape
    T = B * S
    xt = h.reshape(T, D)
    g_logits = (xt @ w_group).astype(jnp.float32)
    g_prob = jax.nn.softmax(g_logits, axis=-1)
    g_sel = jnp.argmax(g_logits, axis=-1)
    g_w = jnp.take_along_axis(g_prob, g_sel[:, None], axis=1)[:, 0]
    e_logits_all = jnp.einsum('td,gde->tge', xt, w_expert_router).astype(jnp.float32)
    e_logits = jnp.take_along_axis(e_logits_all, g_sel[:, None, None], axis=1)[:, 0]
    top_v, top_i = lax.top_k(e_logits, TOP_K)
    e_w = jax.nn.softmax(top_v, axis=-1) * g_w[:, None]
    expert_id = g_sel[:, None].astype(jnp.int32) * EXPERTS_PER_GROUP + top_i.astype(jnp.int32)

    A = T * TOP_K
    flat_e = expert_id.reshape(A)
    flat_tok = jnp.repeat(jnp.arange(T, dtype=jnp.int32), TOP_K)
    flat_w = e_w.reshape(A)
    order = jnp.argsort(flat_e)
    se = flat_e[order]
    counts = jnp.bincount(flat_e, length=N_EXPERTS)
    starts = jnp.cumsum(counts) - counts
    pcounts = (counts + MOE_BLOCK - 1) // MOE_BLOCK * MOE_BLOCK
    pends = jnp.cumsum(pcounts)
    pstarts = pends - pcounts
    dest = pstarts[se] + (jnp.arange(A) - starts[se])
    n_blocks = -(-A // MOE_BLOCK) + N_EXPERTS
    P = n_blocks * MOE_BLOCK
    buf_tok = jnp.full((P,), T, jnp.int32).at[dest].set(flat_tok[order])
    buf_w = jnp.zeros((P,), jnp.float32).at[dest].set(flat_w[order])
    block_e = jnp.minimum(
        jnp.searchsorted(pends, jnp.arange(n_blocks) * MOE_BLOCK, side='right'),
        N_EXPERTS - 1).astype(jnp.int32)
    x_pad = jnp.concatenate([xt, jnp.zeros((1, D), xt.dtype)], axis=0)
    xb = x_pad[buf_tok].reshape(n_blocks, MOE_BLOCK, D)

    def expert_block(args):
        xblk, e = args
        return (jax.nn.silu(xblk @ w_gate[e]) * (xblk @ w_up[e])) @ w_down[e]

    yb = lax.map(expert_block, (xb, block_e)).reshape(P, D)
    yb = yb.astype(jnp.float32) * buf_w[:, None]
    y = jax.ops.segment_sum(yb, buf_tok, num_segments=T + 1)[:T]
    return y.astype(h.dtype).reshape(B, S, D)

def setup_inputs(seed: int = 0) -> dict:
    key = jax.random.key(seed)
    ks = iter(jax.random.split(key, 48))
    L, D = DEPTH, D_MODEL

    def nrm(shape, scale):
        return jax.random.normal(next(ks), shape, jnp.float32) * scale

    def gain(shape):
        return 1.0 + nrm(shape, 0.02)

    def unif(shape):
        return jax.random.uniform(next(ks), shape, jnp.float32)

    x = nrm((BATCH, SEQ, D), 1.0)
    p = nrm((DEPTH, BATCH, SEQ, PL_DIM), 1.0)
    positions = (jnp.arange(SEQ, dtype=jnp.int32)[None, :]
                 + jax.random.randint(next(ks), (BATCH, 1), 0, MAX_POS_OFFSET, dtype=jnp.int32))
    return {
        "x": x,
        "p": p,
        "positions": positions,
        "attn_norm_g": gain((L, D)),
        "w_in": nrm((L, D, IN_COLS), D ** -0.5),
        "q_norm_g": gain((L, DIFF_HEAD_DIM)),
        "k_norm_g": gain((L, DIFF_HEAD_DIM)),
        "lambda_q1": nrm((L, DIFF_HEAD_DIM), 0.1),
        "lambda_k1": nrm((L, DIFF_HEAD_DIM), 0.1),
        "lambda_q2": nrm((L, DIFF_HEAD_DIM), 0.1),
        "lambda_k2": nrm((L, DIFF_HEAD_DIM), 0.1),
        "diff_out_g": gain((L, 2 * DIFF_HEAD_DIM)),
        "mu_rkv": unif((L, 3, RWKV_WIDTH)),
        "mu_wag": unif((L, 3, D)),
        "w0": jnp.linspace(-6.0, -1.0, RWKV_WIDTH, dtype=jnp.float32)[None, :] + nrm((L, RWKV_WIDTH), 0.1),
        "w_lora_a": nrm((L, D, D_DECAY_LORA), D ** -0.5),
        "w_lora_b": nrm((L, D_DECAY_LORA, RWKV_WIDTH), 0.1 * D_DECAY_LORA ** -0.5),
        "a0": nrm((L, RWKV_WIDTH), 0.1),
        "a_lora_a": nrm((L, D, D_AAA_LORA), D ** -0.5),
        "a_lora_b": nrm((L, D_AAA_LORA, RWKV_WIDTH), 0.5 * D_AAA_LORA ** -0.5),
        "g_lora_a": nrm((L, D, D_GATE_LORA), D ** -0.5),
        "g_lora_b": nrm((L, D_GATE_LORA, RWKV_WIDTH), D_GATE_LORA ** -0.5),
        "k_k": 0.85 + nrm((L, RWKV_WIDTH), 0.02),
        "k_a": 1.0 + nrm((L, RWKV_WIDTH), 0.02),
        "r_k": nrm((L, RWKV_HEADS, RWKV_HEAD), 0.1),
        "gn_w": gain((L, RWKV_WIDTH)),
        "gn_b": nrm((L, RWKV_WIDTH), 0.02),
        "w_out": nrm((L, MIX_WIDTH, D), MIX_WIDTH ** -0.5),
        "moe_norm_g": gain((L, D)),
        "w_group": nrm((L, D, N_GROUPS), D ** -0.5),
        "w_expert_router": nrm((L, N_GROUPS, D, EXPERTS_PER_GROUP), D ** -0.5),
        "w_gate": nrm((L, N_EXPERTS, D, D_EXPERT), D ** -0.5),
        "w_up": nrm((L, N_EXPERTS, D, D_EXPERT), D ** -0.5),
        "w_down": nrm((L, N_EXPERTS, D_EXPERT, D), D_EXPERT ** -0.5),
        "w_pl": nrm((L, PL_DIM, D), PL_DIM ** -0.5),
        "pl_norm_g": gain((L, D)),
        "pl_gate_norm_g": gain((L, D)),
        "w_pl_gate": nrm((L, D, D), D ** -0.5),
    }

def reference(x, p, positions, attn_norm_g, w_in, q_norm_g, k_norm_g, lambda_q1, lambda_k1,
              lambda_q2, lambda_k2, diff_out_g, mu_rkv, mu_wag, w0, w_lora_a, w_lora_b, a0,
              a_lora_a, a_lora_b, g_lora_a, g_lora_b, k_k, k_a, r_k, gn_w, gn_b, w_out,
              moe_norm_g, w_group, w_expert_router, w_gate, w_up, w_down, w_pl, pl_norm_g,
              pl_gate_norm_g, w_pl_gate):
    B, S, _ = x.shape
    cos, sin = rope_tables(positions)
    split_at = [DIFF_WIDTH, 2 * DIFF_WIDTH, 3 * DIFF_WIDTH,
                3 * DIFF_WIDTH + RWKV_WIDTH, 3 * DIFF_WIDTH + 2 * RWKV_WIDTH]
    for i in range(DEPTH):
        lam_init = 0.8 - 0.6 * math.exp(-0.3 * i)
        hn = rms_norm(x, attn_norm_g[i])
        z = hn @ w_in[i]
        dq, dk, dv, zr, zk, zv = jnp.split(z, split_at, axis=-1)
        q = apply_rope(rms_norm(dq.reshape(B, S, DIFF_HEADS, 2, DIFF_HEAD_DIM), q_norm_g[i]), cos, sin)
        k = apply_rope(rms_norm(dk.reshape(B, S, DIFF_HEADS, 2, DIFF_HEAD_DIM), k_norm_g[i]), cos, sin)
        v = dv.reshape(B, S, DIFF_HEADS, 2 * DIFF_HEAD_DIM)
        lam = (jnp.exp(jnp.sum(lambda_q1[i].astype(jnp.float32) * lambda_k1[i].astype(jnp.float32)))
               - jnp.exp(jnp.sum(lambda_q2[i].astype(jnp.float32) * lambda_k2[i].astype(jnp.float32)))
               + lam_init)
        o_diff = diff_attention(q, k, v, lam, diff_out_g[i], lam_init)
        o_rwkv = rwkv7_time_mix(hn, zr, zk, zv, mu_rkv[i], mu_wag[i], w0[i], w_lora_a[i],
                                w_lora_b[i], a0[i], a_lora_a[i], a_lora_b[i], g_lora_a[i],
                                g_lora_b[i], k_k[i], k_a[i], r_k[i], gn_w[i], gn_b[i])
        x = x + jnp.concatenate([o_diff, o_rwkv], axis=-1) @ w_out[i]
        x = x + hier_moe(rms_norm(x, moe_norm_g[i]), w_group[i], w_expert_router[i],
                         w_gate[i], w_up[i], w_down[i])
        gate = jax.nn.sigmoid(rms_norm(x, pl_gate_norm_g[i]) @ w_pl_gate[i])
        x = x + rms_norm(p[i] @ w_pl[i], pl_norm_g[i]) * gate
    return x


_drawn_inputs = setup_inputs


def setup_inputs(seed=0):
    import zlib

    import numpy as np

    out = dict(_drawn_inputs(seed))
    spreads = {}
    factors = {'q_norm_g': 2.943,
     'k_norm_g': 2.819,
     'lambda_q2': 4.537,
     'lambda_k2': 8.0,
     'diff_out_g': 9.477,
     'w_lora_a': 7.415,
     'w_lora_b': 7.273,
     'k_k': 23.039,
     'k_a': 4.166,
     'gn_w': 14.055,
     'gn_b': 16.136,
     'pl_norm_g': 24.354,
     'pl_gate_norm_g': 22.543,
     'lambda_q1': 8.0,
     'lambda_k1': 8.0,
     'moe_norm_g': 4.365}
    for name, (base, spread) in spreads.items():
        noise = np.random.default_rng([zlib.crc32(name.encode()), seed]).standard_normal(out[name].shape)
        drawn = base * np.exp(spread * noise) if base else spread * noise
        out[name] = __import__('jax').numpy.asarray(drawn.astype(out[name].dtype))
    for name, factor in factors.items():
        out[name] = (out[name] * factor).astype(out[name].dtype)
    return out
```

```python
import math
from contextlib import ExitStack
import numpy as np
import concourse.bass as bass
from concourse import mybir

F32 = mybir.dt.float32
I32 = mybir.dt.int32
U32 = mybir.dt.uint32
ALU = mybir.AluOpType
ACT = mybir.ActivationFunctionType
AX = mybir.AxisListType

P = 128
SEQ, D = 2048, 1024
TILES = SEQ // P
KD = D // P
QKV = 1536
RW = 512
NORM_EPS = 1e-6
R_W, R_A, R_G = 64, 64, 160
R_ALL = R_W + R_A + R_G
DH = 64
ROPE_THETA = 10000.0
ROUND = 1.5 * 2.0 ** 23
TWO_PI = (6.28125, 1.9350051879882812e-03, 3.019916050561733e-07)
BANK = 512


def two_by_two(eng, n, body):
    body(0, 0, 0, False)
    body(1, 0, 1, False)
    with eng.Fori(1, n // 2 - 1) as j:
        body(j * 2, j, 0, False)
        body(j * 2 + 1, j, 1, False)
    body(n - 2, n // 2 - 1, 0, False)
    body(n - 1, n // 2 - 1, 1, True)


def phase_project(nc, t, ident):
    with ExitStack() as ctx:
        sb = lambda n, s, d=F32: ctx.enter_context(nc.sbuf_tensor(n, s, d))
        sems = []

        def sem(name):
            sems.append(t["semctx"].enter_context(nc.semaphore(name)))
            return sems[-1]
        w_sb = sb("w_in_sb", [P, KD, 2 * QKV])
        wl = sb("lora_in", [P, KD, 2, R_ALL])
        wab = sb("lora_out_wa", [P, RW])
        wg0 = sb("lora_out_g0", [P, RW])
        wg1 = sb("lora_out_g1", [R_G - P, RW])
        mu = sb("mu_cols", [P, 3, KD])
        gain = sb("attn_gain", [P, D])
        bias = sb("lora_bias", [P, 2, RW])
        x_sb = [sb(f"x_tile{s}", [P, D]) for s in range(2)]
        hn = [sb(f"hn_tile{s}", [P, D]) for s in range(2)]
        hT = [sb(f"hnT{s}", [P, KD, P + 1]) for s in range(2)]
        ss = sb("sumsq", [P, 2])
        rstd = sb("rstd", [P, 2])
        pw = sb("rsqrt_consts", [P, 4, 16])
        ms = sb("meansq", [P, 16])
        l1 = sb("lora_mid", [P, R_ALL])
        l1T = sb("lora_midT", [P, 3, P])
        qk = sb("qk_stage", [P, 2, BANK])
        stage = [qk[:, 0, :], qk[:, 1, :]] + [sb(f"z_stage{c}", [P, BANK])[:] for c in range(2, 9)]
        qk_g = sb("qk_gain", [P, 2, 8, DH])
        qn = sb("qk_normed", [P, 16, DH])
        by_cos = sb("qk_cos", [P, 16, DH])
        by_sin = sb("qk_sin", [P, 16, DH])
        qss = sb("qk_sumsq", [P, 16])
        qrs = sb("qk_rstd", [P, 16])
        qkT = sb("qkT_stage", [P, 8, P])
        cos_t = sb("cos_table", [P, TILES, DH // 2])
        sin_t = sb("sin_table", [P, TILES, DH // 2])
        pos_i = sb("positions_i", [P, TILES], I32)
        pos_f = sb("positions_f", [P, TILES])
        freq = sb("inv_freq", [P, DH // 2])
        turns = by_sin[:, 0:8, :].rearrange("p a b -> p (a b)").rearrange("p (t f) -> p t f", t=TILES)
        ang = by_cos[:, 0:8, :].rearrange("p a b -> p (a b)").rearrange("p (t f) -> p t f", t=TILES)
        half_pi = sb("half_pi", [P, 1])
        ps = lambda n, s: ctx.enter_context(nc.psum_tensor(n, s, F32))
        pT = ps("p_hT", [P, 2, BANK])
        pZ = ps("p_z", [P, 3, BANK])
        pL = ps("p_l1", [P, BANK])
        pLT = ps("p_l1T", [P, BANK])

        x_in = [sem(f"A_x_in{s}") for s in range(2)]
        w_in = [sem(f"A_w_in{c}") for c in range(6)]
        s_par = sem("A_params"); s_wl = sem("A_lora_w_in"); s_wl_rdy = sem("A_lora_scaled")
        s_const = sem("A_const")
        ss_done = sem("A_ss"); rstd_done = sem("A_rstd"); hn_done = sem("A_hn")
        hT_psum = sem("A_hT_psum"); hTa = sem("A_hT_lo"); hTd = sem("A_hT_hi")
        z_done = sem("A_z"); ev = [sem(f"A_evac{c}") for c in range(9)]
        staged = [sem(f"A_staged{c}") for c in range(9)]
        out_dma = [sem(f"A_out{c}") for c in range(9)]
        s_pos = sem("A_positions"); s_freq = sem("A_inv_freq"); s_ang = sem("A_angles"); s_trig = sem("A_trig")
        sq_done = sem("A_qk_sq"); qss_done = sem("A_qk_ss"); qrs_done = sem("A_qk_rstd"); rot_done = sem("A_rot")
        qkT_psum = sem("A_qkT_psum"); qkTa = sem("A_qT"); qkTd = sem("A_kT"); qT_out = sem("A_qT_out"); kT_out = sem("A_kT_out")
        l1_done = sem("A_l1"); l1_act = sem("A_l1_act"); l1T_psum = sem("A_l1T_psum"); l1T_sb = sem("A_l1T")
        block = ctx.enter_context(nc.Block())

        @block.sync
        def _(sp):
            for s in range(2):
                sp.dma_start(x_sb[s][:], t["x"][s * P:(s + 1) * P, :]).then_inc(x_in[s], 16)
            sp.dma_start(gain[:], t["attn_norm_g"].partition_broadcast(P)).then_inc(s_par, 16)
            with nc.allow_non_contiguous_dma(reason="8 KB of positions, once"):
                sp.dma_start(pos_i[:], t["positions"].rearrange("(t p) -> p t", p=P)).then_inc(s_pos, 16)
            for n, name in enumerate(("q_norm_g", "k_norm_g")):
                for g in range(8):
                    sp.dma_start(qk_g[:, n, g, :], t[name].partition_broadcast(P)).then_inc(s_par, 16)
            with nc.allow_non_contiguous_dma(reason="12 KB of per-channel mixes, once"):
                for m in range(3):
                    sp.dma_start(mu[:, m, :], t["mu_wag"][m].rearrange("(k p) -> p k", p=P)).then_inc(s_wl, 16)
            for name, a, b in (("w_lora_a", 0, R_W), ("a_lora_a", R_W, R_W + R_A), ("g_lora_a", R_W + R_A, R_ALL)):
                sp.dma_start(wl[:, :, 0, a:b], t[name].rearrange("(k p) r -> p k r", p=P)).then_inc(s_wl, 16)
            for c in range(6):
                sp.dma_start(w_sb[:, :, c * BANK:(c + 1) * BANK],
                             t["w_in"][:, c * BANK:(c + 1) * BANK].rearrange("(k p) n -> p k n", p=P)).then_inc(w_in[c], 16)
            sp.dma_start(wab[0:R_W, :], t["w_lora_b"]).then_inc(s_par, 16)
            sp.dma_start(wab[R_W:P, :], t["a_lora_b"]).then_inc(s_par, 16)
            sp.dma_start(wg0[:], t["g_lora_b"][0:P, :]).then_inc(s_par, 16)
            sp.dma_start(wg1[:], t["g_lora_b"][P:R_G, :]).then_inc(s_par, 16)
            sp.dma_start(bias[:, 0, :], t["w0"].partition_broadcast(P)).then_inc(s_par, 16)
            sp.dma_start(bias[:, 1, :], t["a0"].partition_broadcast(P)).then_inc(s_par, 16)

            def tile(i, j, s, last, load):
                if load:
                    sp.wait_ge(hn_done, i + 1)
                    sp.dma_start(x_sb[s][:], t["x"][bass.ds(i * P + 2 * P, P), :]).then_inc(x_in[s], 16)
                for c in range(2, 9):
                    if c == 2:
                        dst = t["v"][bass.ds(i * P, P), :]
                    elif c < 6:
                        dst = t["zr"][bass.ds(i * P + 1, P), (c - 3) * BANK:(c - 2) * BANK]
                    else:
                        dst = t["lo"][c - 6, bass.ds(i * P, P), :]
                    sp.wait_ge(staged[c], i + 1)
                    sp.dma_start(dst, stage[c]).then_inc(out_dma[c], 16)
                for n, name, rdy, out in ((0, "qT", qkTa, qT_out), (4, "kT", qkTd, kT_out)):
                    sp.wait_ge(rdy, i + 1)
                    sp.dma_start(t[name][bass.ds(i * P, P), :], qkT[:, n:n + 4, :].rearrange("p h n -> p (h n)")).then_inc(out, 16)
            tile(0, 0, 0, False, True)
            tile(1, 0, 1, False, True)
            with sp.Fori(1, TILES // 2 - 1) as j:
                tile(j * 2, j, 0, False, True)
                tile(j * 2 + 1, j, 1, False, True)
            tile(TILES - 2, None, 0, False, False)
            tile(TILES - 1, None, 1, True, False)
            for c in range(2, 9):
                sp.wait_ge(out_dma[c], 16 * TILES)
            sp.wait_ge(qT_out, 16 * TILES)
            sp.wait_ge(kT_out, 16 * TILES)

        @block.gpsimd
        def _(pool):
            for n, v in enumerate((1.0 / D, 1.0 / DH, NORM_EPS, -0.5)):
                pool.memset(pw[:, n, :], v)
            for n in range(DH // 2):
                pool.memset(freq[:, n:n + 1], float(ROPE_THETA ** (np.float32(-n) / np.float32(DH // 2))))
            pool.memset(half_pi[:], math.pi / 2).then_inc(s_freq, 1)
            pool.memset(hT[1][:], 0.0).then_inc(s_const, 1)
            pool.drain()

            def rsqrt(out, sums, mean):
                n = out.shape[1]
                pool.tensor_tensor(ms[:, 0:n], sums, pw[:, mean, 0:n], ALU.mult)
                pool.drain()
                pool.tensor_tensor(ms[:, 0:n], ms[:, 0:n], pw[:, 2, 0:n], ALU.add)
                pool.drain()
                return pool.tensor_tensor(out, ms[:, 0:n], pw[:, 3, 0:n], ALU.pow)

            def head(i, s):
                pool.wait_ge(ss_done, i + 1)
                rsqrt(rstd[:, s:s + 1], ss[:, s:s + 1], 0).then_inc(rstd_done, 1)
            head(0, 0)

            def tile(i, j, s, last):
                if not last:
                    head(i + 1, 1 - s)
                pool.wait_ge(qss_done, i + 1)
                rsqrt(qrs[:], qss[:], 1).then_inc(qrs_done, 1)
            two_by_two(pool, TILES, tile)

        @block.scalar
        def _(act):
            def square(i, jj, s):
                act.wait_ge(x_in[s], 16 * jj + 16)
                nc.scalar.activation(hn[s][:], x_sb[s][:], ACT.Square, accum_out=ss[:, s:s + 1]).then_inc(ss_done, 1)

            def copy_hT(i, s):
                act.wait_ge(hT_psum, i + 1)
                nc.scalar.copy(hT[s][:, 0:4, 1:P + 1], pT[:, 0, :].rearrange("p (k n) -> p k n", k=4))
                nc.scalar.copy(hT[s][:, 0:4, 0:1], hT[1 - s][:, 0:4, P:P + 1]).then_inc(hTa, 1)

            act.wait_ge(s_const, 1)
            act.wait_ge(s_ang, 1)
            nc.scalar.activation(sin_t[:], ang, ACT.Sin)
            act.wait_ge(s_ang, 2)
            nc.scalar.activation(cos_t[:], turns, ACT.Sin, bias=half_pi[:], scale=-1.0).then_inc(s_trig, 1)
            square(0, 0, 0)
            copy_hT(0, 0)

            def tile(i, j, s, last):
                if not last:
                    square(i + 1, j + s, 1 - s)
                act.wait_ge(l1_done, i + 1)
                act.wait_ge(l1T_psum, i)
                nc.scalar.activation(l1[:, 0:R_W], pL[:, 0:R_W], ACT.Tanh)
                nc.scalar.copy(l1[:, R_W:P], pL[:, R_W:P])
                nc.scalar.activation(l1[:, P:R_ALL], pL[:, P:R_ALL], ACT.Sigmoid).then_inc(l1_act, 1)

                def evac(c):
                    act.wait_ge(z_done, 9 * i + (c + 1))
                    if c >= 2:
                        act.wait_ge(out_dma[c], 16 * i)
                    nc.scalar.copy(stage[c], pZ[:, c % 3, :]).then_inc(ev[c], 1)
                    if c >= 2:
                        act.wait_ge(ev[c], i + 1)
                        act.sem_inc(staged[c], 1)
                evac(0)
                evac(2)
                act.wait_ge(ev[0], i + 1)
                act.wait_ge(ev[1], i + 1)
                nc.scalar.activation(qn[:].rearrange("p g d -> p (g d)"), qk[:].rearrange("p a n -> p (a n)"),
                                     ACT.Square).then_inc(sq_done, 1)
                if not last:
                    copy_hT(i + 1, 1 - s)
                evac(4)
                for c in (6, 7):
                    act.wait_ge(ev[c], i + 1)
                    nc.scalar.activation(stage[c], stage[c], ACT.Sigmoid).then_inc(staged[c], 1)
                evac(8)
                act.wait_ge(qkT_psum, i + 1)
                act.wait_ge(qT_out, 16 * i)
                nc.scalar.copy(qkT[:, 0:4, :], pT[:, 0, :].rearrange("p (k n) -> p k n", k=4)).then_inc(qkTa, 1)
            two_by_two(act, TILES, tile)

        @block.vector
        def _(dve):
            dve.wait_ge(s_pos, 16)
            dve.wait_ge(s_freq, 1)
            nc.vector.tensor_copy(pos_f[:], pos_i[:])
            dve.drain()
            shape = [P, TILES, DH // 2]
            nc.vector.tensor_tensor(ang, pos_f[:].unsqueeze(2).broadcast_to(shape), freq[:].unsqueeze(1).broadcast_to(shape), ALU.mult)
            dve.drain()
            nc.vector.tensor_scalar(turns, ang, 1.0 / (2 * math.pi), ROUND, ALU.mult, ALU.add)
            dve.drain()
            nc.vector.tensor_scalar(turns, turns, ROUND, None, ALU.subtract)
            for part in TWO_PI:
                dve.drain()
                nc.vector.scalar_tensor_tensor(ang, turns, -part, ang, ALU.mult, ALU.add)
            dve.drain()
            nc.vector.tensor_scalar(ang, ang, math.pi, -math.pi, ALU.min, ALU.max).then_inc(s_ang, 1)
            dve.drain()
            nc.vector.scalar_tensor_tensor(turns, ang, -1.0, ang, ALU.mult, ALU.max).then_inc(s_ang, 1)
            dve.wait_ge(s_wl, 6 * 16)
            for k in range(KD):
                for m, (a, b) in enumerate(((0, R_W), (R_W, R_W + R_A), (R_W + R_A, R_ALL))):
                    nc.vector.tensor_scalar(wl[:, k, 1, a:b], wl[:, k, 0, a:b], mu[:, m, k:k + 1], None, ALU.mult)
            dve.drain()
            nc.vector.tensor_tensor(wl[:, :, 0, :], wl[:, :, 0, :], wl[:, :, 1, :], ALU.subtract).then_inc(s_wl_rdy, 1)
            dve.wait_ge(s_par, 23 * 16)
            dve.wait_ge(s_const, 1)
            dve.wait_ge(s_trig, 1)
            nc.vector.tensor_scalar(qk_g[:, 0, :, :], qk_g[:, 0, :, :], float(DH) ** -0.5, None, ALU.mult)
            dve.drain()

            def make_hn(i, jj, s):
                dve.wait_ge(x_in[s], 16 * jj + 16)
                dve.wait_ge(rstd_done, i + 1)
                nc.vector.scalar_tensor_tensor(hn[s][:], x_sb[s][:], rstd[:, s:s + 1], gain[:],
                                               ALU.mult, ALU.mult).then_inc(hn_done, 1)

            def copy_hT(i, s):
                dve.wait_ge(hT_psum, i + 1)
                nc.vector.tensor_copy(hT[s][:, 4:8, 1:P + 1], pT[:, 1, :].rearrange("p (k n) -> p k n", k=4))
                nc.vector.tensor_copy(hT[s][:, 4:8, 0:1], hT[1 - s][:, 4:8, P:P + 1]).then_inc(hTd, 1)
            make_hn(0, 0, 0)
            copy_hT(0, 0)

            def tile(i, j, s, last):
                if not last:
                    make_hn(i + 1, j + s, 1 - s)

                def evac(c):
                    dve.wait_ge(z_done, 9 * i + (c + 1))
                    if c >= 2:
                        dve.wait_ge(out_dma[c], 16 * i)
                    if c < 6:
                        nc.vector.tensor_copy(stage[c], pZ[:, c % 3, :]).then_inc(ev[c], 1)
                        if c >= 2:
                            dve.wait_ge(ev[c], i + 1)
                            dve.sem_inc(staged[c], 1)
                    else:
                        nc.vector.tensor_tensor(stage[c], pZ[:, c % 3, :], bias[:, c - 6, :], ALU.add).then_inc(ev[c], 1)
                evac(1)
                if not last:
                    copy_hT(i + 1, 1 - s)
                dve.wait_ge(l1T_psum, i + 1)
                nc.vector.tensor_copy(l1T[:, 0:2, :], pLT[:, 0:2 * P].rearrange("p (k n) -> p k n", k=2))
                nc.vector.tensor_copy(l1T[0:R_G - P, 2, :], pLT[0:R_G - P, 2 * P:3 * P]).then_inc(l1T_sb, 1)
                dve.wait_ge(sq_done, i + 1)
                nc.vector.tensor_reduce(qss[:], qn[:], AX.X, ALU.add).then_inc(qss_done, 1)
                evac(3)
                dve.wait_ge(qrs_done, i + 1)
                shape = [P, 16, DH]
                nc.vector.tensor_tensor(qn[:], qk[:].rearrange("p a (g d) -> p (a g) d", d=DH),
                                        qrs[:].unsqueeze(2).broadcast_to(shape), ALU.mult)
                dve.drain()
                nc.vector.tensor_tensor(qn[:], qn[:], qk_g[:].rearrange("p a g d -> p (a g) d"), ALU.mult)
                dve.drain()
                half = [P, 32, DH // 2]
                c_t = cos_t[:, bass.ds(i, 1), :].broadcast_to(half)
                s_t = sin_t[:, bass.ds(i, 1), :].broadcast_to(half)
                nc.vector.tensor_tensor(by_cos[:].rearrange("p g (h d) -> p (g h) d", h=2), qn[:].rearrange("p g (h d) -> p (g h) d", h=2), c_t, ALU.mult)
                nc.vector.tensor_tensor(by_sin[:].rearrange("p g (h d) -> p (g h) d", h=2), qn[:].rearrange("p g (h d) -> p (g h) d", h=2), s_t, ALU.mult)
                dve.drain()
                h = DH // 2
                nc.vector.tensor_tensor(qn[:, :, 0:h], by_cos[:, :, 0:h], by_sin[:, :, h:DH], ALU.subtract)
                nc.vector.tensor_tensor(qn[:, :, h:DH], by_cos[:, :, h:DH], by_sin[:, :, 0:h], ALU.add).then_inc(rot_done, 1)
                evac(5)
                evac(6)
                evac(7)
                dve.wait_ge(qkT_psum, i + 1)
                dve.wait_ge(kT_out, 16 * i)
                nc.vector.tensor_copy(qkT[:, 4:8, :], pT[:, 1, :].rearrange("p (k n) -> p k n", k=4)).then_inc(qkTd, 1)
            two_by_two(dve, TILES, tile)

        @block.tensor
        def _(pe):
            def transposes(i, s, first=1):
                pe.wait_ge(hn_done, i + 1)
                pe.wait_ge(qkTa, i - first)
                pe.wait_ge(qkTd, i - first)
                for k in range(KD):
                    last = nc.tensor.transpose(pT[:, k // 4, (k % 4) * P:(k % 4 + 1) * P], hn[s][:, k * P:(k + 1) * P], ident[:])
                last.then_inc(hT_psum, 1)
            transposes(0, 0, 0)
            pe.wait_ge(s_wl_rdy, 1)
            pe.wait_ge(s_par, 23 * 16)

            def tile(i, j, s, last_tile):
                pe.wait_ge(hTa, i + 1)
                pe.wait_ge(hTd, i + 1)
                pe.wait_ge(l1_act, i)
                for shifted in (0, 1):
                    for k in range(KD):
                        last = nc.tensor.matmul(pL[:, 0:R_ALL], hT[s][:, k, 1 - shifted:P + 1 - shifted], wl[:, k, shifted, :],
                                                start=(k == 0 and not shifted), stop=(k == KD - 1 and shifted == 1))
                last.then_inc(l1_done, 1)

                def free_bank(c):
                    if c < 3:
                        pe.wait_ge(ev[c + 6], i)
                    else:
                        pe.wait_ge(ev[c - 3], i + 1)

                def chunk(c):
                    pe.wait_ge(w_in[c], 16)
                    free_bank(c)
                    for k in range(KD):
                        last = nc.tensor.matmul(pZ[:, c % 3, :], hT[s][:, k, 1:P + 1], w_sb[:, k, c * BANK:(c + 1) * BANK],
                                                start=(k == 0), stop=(k == KD - 1))
                    last.then_inc(z_done, 1)
                for c in range(3):
                    chunk(c)
                if not last_tile:
                    transposes(i + 1, 1 - s)
                pe.wait_ge(l1_act, i + 1)
                pe.wait_ge(l1T_sb, i)
                nc.tensor.transpose(pLT[:, 0:P], l1[:, 0:P], ident[:])
                nc.tensor.transpose(pLT[:, P:2 * P], l1[:, P:2 * P], ident[:])
                nc.tensor.transpose(pLT[0:R_G - P, 2 * P:3 * P], l1[:, 2 * P:R_ALL], ident[:]).then_inc(l1T_psum, 1)
                for c in range(3, 6):
                    chunk(c)
                pe.wait_ge(l1T_sb, i + 1)
                free_bank(6)
                nc.tensor.matmul(pZ[:, 0, :], l1T[0:R_W, 0, :], wab[0:R_W, :], start=True, stop=True).then_inc(z_done, 1)
                free_bank(7)
                nc.tensor.matmul(pZ[:, 1, :], l1T[R_W:P, 0, :], wab[R_W:P, :], start=True, stop=True).then_inc(z_done, 1)
                free_bank(8)
                nc.tensor.matmul(pZ[:, 2, :], l1T[:, 1, :], wg0[:], start=True, stop=False)
                nc.tensor.matmul(pZ[:, 2, :], l1T[0:R_G - P, 2, :], wg1[:], start=False, stop=True).then_inc(z_done, 1)
                pe.wait_ge(rot_done, i + 1)
                if not last_tile:
                    pe.wait_ge(hTa, i + 2)
                    pe.wait_ge(hTd, i + 2)
                for g in range(8):
                    last = nc.tensor.transpose(pT[:, g // 4, (g % 4) * P:(g % 4 + 1) * P],
                                               qn[:, 2 * g:2 * g + 2, :].rearrange("p a d -> p (a d)"), ident[:])
                last.then_inc(qkT_psum, 1)
            two_by_two(pe, TILES, tile)
    return sems


def phase_constants(nc, t, ident):
    with ExitStack() as ctx:
        s_id = t["semctx"].enter_context(nc.semaphore("C_ident"))
        s_z = t["semctx"].enter_context(nc.semaphore("C_zero_row"))
        zero = ctx.enter_context(nc.sbuf_tensor("zero_row", [1, QKV], F32))
        block = ctx.enter_context(nc.Block())

        @block.gpsimd
        def _(pool):
            pool.memset(zero[:], 0.0)
            pool.memset(ident[:], 0.0)
            pool.drain()
            pool.affine_select(out=ident[:], in_=ident[:], compare_op=ALU.not_equal, fill=1.0, base=0,
                               pattern=[[-1, P]], channel_multiplier=1).then_inc(s_id, 1)
            pool.drain()
            pool.dma_start(t["zr"][0:1, :], zero[:]).then_inc(s_z, 16)
            pool.wait_ge(s_z, 16)
            pool.wait_ge(s_id, 1)


HEADS = 4
SUBLN_EPS = 1e-5
LAM_INIT = 0.8 - 0.6 * math.exp(0.0)
MASKED = -1e30


def phase_attention(nc, t, ident, spent=()):
    CH = [i // 4 + 1 for i in range(TILES)]
    W = [[min(BANK, (i + 1) * P - c * BANK) for c in range(CH[i])] for i in range(TILES)]
    C0 = [sum(CH[:i]) for i in range(TILES + 1)]
    NCH = C0[TILES]
    with ExitStack() as ctx:
        sb = lambda n, s, d=F32: ctx.enter_context(nc.sbuf_tensor(n, s, d))
        sem = lambda n: t["semctx"].enter_context(nc.semaphore(n))
        ps = lambda n, s: ctx.enter_context(nc.psum_tensor(n, s, F32))
        kT = sb("kT_all", [P, TILES, HEADS * P])
        v = sb("v_all", [P, TILES, HEADS * P])
        qz = [sb(f"q_maps{s}", [P, 2, P]) for s in range(2)]
        prob = [[sb(f"prob{s}{m}", [P, TILES * P]) for m in range(2)] for s in range(2)]
        aT = [sb(f"attnT{s}", [P, BANK]) for s in range(2)]
        o_st = [sb(f"o_stage{s}", [P, P]) for s in range(2)]
        sq_junk = sb("o_sq", [P, 2, P])
        mask = sb("causal_mask", [P, P])
        nmax = [sb(f"neg_max{s}", [P, 2, 4]) for s in range(2)]
        sums = [sb(f"prob_sums{s}", [P, 2, 4]) for s in range(2)]
        nrow = sb("neg_row_max", [P, 2])
        fac = sb("chunk_factor", [P, 2, 4])
        tmp = sb("stat_tmp", [P, 2, 4])
        den = sb("denominator", [P, 2])
        coef = sb("coef", [P, 2, 4])
        oss = sb("o_sumsq", [P, 2]); ors = sb("o_rstd", [P, 2]); oms = sb("o_ms", [P, 1])
        pw = sb("o_consts", [P, 3])
        lamv = sb("lam_sign", [P, 2])
        lp = sb("lam_params", [P, 4, DH]); lprod = sb("lam_prod", [P, 2, DH]); lsum = sb("lam_sum", [P, 2]); lexp = sb("lam_exp", [P, 2])
        og = sb("o_gain", [P, P])
        pS = ps("p_scores", [P, 4, BANK]); pT = ps("p_attnT", [P, 2, BANK]); pO = ps("p_o", [P, 2, BANK])

        kv_in = [sem(f"B_kv{n}") for n in range(4)]; par_in = sem("B_par"); q_in = [sem(f"B_q{s}") for s in range(2)]
        consts = sem("B_consts"); lam_s = sem("B_lam_sum"); lam_e = sem("B_lam_exp")
        s_done = sem("B_scores")
        max_done = sem("B_max"); exp_done = sem("B_exp")
        d_done = sem("B_max_diff"); f_done = sem("B_factor")
        attn_done = sem("B_attn"); T_done = sem("B_attnT_psum"); Tc_done = sem("B_attnT")
        pv_done = sem("B_pv")
        oss_done = sem("B_oss"); ors_done = sem("B_ors"); o_done = sem("B_o")
        o_out = [sem(f"B_out{s}") for s in range(2)]
        block = ctx.enter_context(nc.Block())

        @block.sync
        def _(sp):
            for s in spent:
                sp.sem_clear(s)
            for n in range(4):
                rows = slice(n * 4 * P, (n + 1) * 4 * P)
                sp.dma_start(kT[:, 4 * n:4 * n + 4, :], t["kT"][rows, :].rearrange("(t p) n -> p t n", p=P)).then_inc(kv_in[n], 16)
                sp.dma_start(v[:, 4 * n:4 * n + 4, :], t["v"][rows, :].rearrange("(t p) n -> p t n", p=P)).then_inc(kv_in[n], 16)
                if n == 0:
                    for k, name in enumerate(("lambda_q1", "lambda_k1", "lambda_q2", "lambda_k2")):
                        sp.dma_start(lp[:, k, :], t[name].partition_broadcast(P)).then_inc(par_in, 16)
                    sp.dma_start(og[:], t["diff_out_g"].partition_broadcast(P)).then_inc(par_in, 16)
            sp.wait_ge(consts, 1)
            for s in range(2):
                sp.sem_inc(o_out[s], 16)
            with sp.Fori(0, HEADS) as h:
                def load_q(i):
                    sp.wait_ge(s_done, h * (2 * NCH) + (2 * C0[TILES - 2 + i + 1] if i < 2 else 2 * NCH + 2 * C0[i - 1]))
                    for m in range(2):
                        r = slice(DH * m, DH * m + DH)
                        sp.dma_start(qz[i % 2][r, m, :], t["qT"][i * P + DH * m:i * P + DH * m + DH, bass.ds(h * P, P)]).then_inc(q_in[i % 2], 16)

                def store(i):
                    sp.wait_ge(o_done, h * TILES + (i + 3))
                    sp.dma_start(t["mix"][i * P:(i + 1) * P, bass.ds(h * P, P)], o_st[i % 2][:]).then_inc(o_out[i % 2], 16)
                load_q(0)
                load_q(1)
                for i in range(TILES):
                    if i + 2 < TILES:
                        load_q(i + 2)
                    if i >= 1:
                        store(i - 1)
                store(TILES - 1)
            for s in range(2):
                sp.wait_ge(o_out[s], 16 * (HEADS * TILES // 2 + 1))

        @block.gpsimd
        def _(pool):
            pool.memset(qz[0][:], 0.0)
            pool.memset(qz[1][:], 0.0)
            pool.memset(lamv[:], 1.0)
            for n, c in enumerate((1.0 / P, SUBLN_EPS, -0.5)):
                pool.memset(pw[:, n:n + 1], c)
            pool.memset(mask[:], 0.0)
            pool.drain()
            pool.affine_select(out=mask[:], in_=mask[:], compare_op=ALU.is_ge, fill=MASKED, base=0,
                               pattern=[[-1, P]], channel_multiplier=1).then_inc(consts, 1)
            with pool.Fori(0, HEADS * TILES // 2) as j:
                for s in range(2):
                    pool.wait_ge(oss_done, j * 2 + s + 1)
                    pool.tensor_tensor(oms[:], oss[:, s:s + 1], pw[:, 0:1], ALU.mult)
                    pool.drain()
                    pool.tensor_tensor(oms[:], oms[:], pw[:, 1:2], ALU.add)
                    pool.drain()
                    pool.tensor_tensor(ors[:, s:s + 1], oms[:], pw[:, 2:3], ALU.pow).then_inc(ors_done, 1)
                    pool.drain()

        @block.scalar
        def _(act):
            act.sem_inc(exp_done, 4)
            act.sem_inc(Tc_done, 2)
            act.wait_ge(lam_s, 1)
            nc.scalar.activation(lexp[:], lsum[:], ACT.Exp).then_inc(lam_e, 1)
            with act.Fori(0, HEADS) as h:
                def exp(i, c, m):
                    n = 2 * (C0[i] + c) + m
                    act.wait_ge(max_done, h * (2 * NCH) + n + 1)
                    nc.scalar.activation(prob[i % 2][m][:, c * BANK:c * BANK + W[i][c]], pS[:, n % 4, 0:W[i][c]], ACT.Exp,
                                         bias=nmax[i % 2][:, m, c:c + 1], accum_out=sums[i % 2][:, m, c:c + 1]).then_inc(exp_done, 1)

                def square_o(i):
                    act.wait_ge(pv_done, h * NCH + (C0[i + 1] + 1))
                    nc.scalar.activation(sq_junk[:, i % 2, :], pO[:, i % 2, 0:P], ACT.Square, accum_out=oss[:, i % 2:i % 2 + 1]).then_inc(oss_done, 1)
                for i in range(-1, TILES):
                    if i >= 0:
                        act.wait_ge(d_done, h * TILES + i + 1)
                        nc.scalar.activation(fac[:], tmp[:], ACT.Exp, scale=-1.0).then_inc(f_done, 1)
                    for c in range(max(CH[i] if i >= 0 else 0, CH[i + 1] if i + 1 < TILES else 0)):
                        if i + 1 < TILES and c < CH[i + 1]:
                            exp(i + 1, c, 0)
                            exp(i + 1, c, 1)
                        if i >= 0 and c < CH[i]:
                            n = C0[i] + c
                            act.wait_ge(T_done, h * NCH + n + 1)
                            act.wait_ge(pv_done, h * NCH + n) if n > 0 else None
                            nc.scalar.copy(aT[n % 2][:, 0:W[i][c]], pT[:, n % 2, 0:W[i][c]]).then_inc(Tc_done, 1)
                    if i >= 1:
                        square_o(i - 1)
                square_o(TILES - 1)

        @block.vector
        def _(dve):
            dve.sem_inc(o_done, 2)
            dve.wait_ge(par_in, 16 * 5)
            dve.wait_ge(consts, 1)
            nc.vector.tensor_tensor(lprod[:, 0, :], lp[:, 0, :], lp[:, 1, :], ALU.mult)
            nc.vector.tensor_tensor(lprod[:, 1, :], lp[:, 2, :], lp[:, 3, :], ALU.mult)
            nc.vector.tensor_scalar(og[:], og[:], 1.0 - LAM_INIT, None, ALU.mult)
            nc.vector.memset(nmax[0][:], 0.0)
            nc.vector.memset(nmax[1][:], 0.0)
            nc.vector.memset(tmp[:], 0.0)
            dve.drain()
            nc.vector.tensor_reduce(lsum[:], lprod[:], AX.X, ALU.add).then_inc(lam_s, 1)
            dve.wait_ge(lam_e, 1)
            nc.vector.tensor_tensor(lamv[:, 1:2], lexp[:, 1:2], lexp[:, 0:1], ALU.subtract)
            dve.drain()
            nc.vector.tensor_scalar(lamv[:, 1:2], lamv[:, 1:2], -LAM_INIT, None, ALU.add)
            dve.drain()
            with dve.Fori(0, HEADS) as h:
                def chunk_max(i, c, m):
                    n = 2 * (C0[i] + c) + m
                    dve.wait_ge(s_done, h * (2 * NCH) + 2 * NCH + n + 1)
                    nc.vector.tensor_reduce(nmax[i % 2][:, m, c:c + 1], pS[:, n % 4, 0:W[i][c]], AX.X, ALU.max, negate=True).then_inc(max_done, 1)

                def output(i):
                    dve.wait_ge(ors_done, h * TILES + i + 1)
                    dve.wait_ge(o_out[i % 2], h * (8 * 16) + (i // 2 + 1) * 16)
                    nc.vector.scalar_tensor_tensor(o_st[i % 2][:], pO[:, i % 2, 0:P], ors[:, i % 2:i % 2 + 1], og[:],
                                                   ALU.mult, ALU.mult).then_inc(o_done, 1)
                for i in range(-1, TILES):
                    if i >= 0:
                        k, s = CH[i], i % 2
                        three = [P, 2, k]
                        dve.wait_ge(exp_done, h * (2 * NCH) + 4 + 2 * C0[i + 1])
                        nc.vector.tensor_reduce(nrow[:], nmax[s][:, :, 0:k], AX.X, ALU.min)
                        dve.drain()
                        nc.vector.tensor_tensor(tmp[:, :, 0:k], nmax[s][:, :, 0:k], nrow[:].unsqueeze(2).broadcast_to(three), ALU.subtract).then_inc(d_done, 1)
                        dve.wait_ge(f_done, h * TILES + i + 1)
                        nc.vector.tensor_tensor(coef[:, :, 0:k], fac[:, :, 0:k], sums[s][:, :, 0:k], ALU.mult)
                        dve.drain()
                        nc.vector.tensor_reduce(den[:], coef[:, :, 0:k], AX.X, ALU.add)
                        dve.drain()
                        nc.vector.reciprocal(den[:], den[:])
                        dve.drain()
                        nc.vector.tensor_tensor(den[:], den[:], lamv[:], ALU.mult)
                        dve.drain()
                        nc.vector.tensor_tensor(coef[:, :, 0:k], fac[:, :, 0:k], den[:].unsqueeze(2).broadcast_to(three), ALU.mult)
                        dve.drain()
                    for c in range(max(CH[i] if i >= 0 else 0, CH[i + 1] if i + 1 < TILES else 0)):
                        if i >= 0 and c < CH[i]:
                            cols = slice(c * BANK, c * BANK + W[i][c])
                            p0, p1 = prob[i % 2][0][:, cols], prob[i % 2][1][:, cols]
                            nc.vector.tensor_scalar(p1, p1, coef[:, 1, c:c + 1], None, ALU.mult)
                            dve.drain()
                            nc.vector.scalar_tensor_tensor(p0, p0, coef[:, 0, c:c + 1], p1, ALU.mult, ALU.add).then_inc(attn_done, 1)
                        if i + 1 < TILES and c < CH[i + 1]:
                            chunk_max(i + 1, c, 0)
                            chunk_max(i + 1, c, 1)
                    if i >= 1:
                        output(i - 1)
                output(TILES - 1)

        @block.tensor
        def _(pe):
            pe.sem_inc(s_done, 2 * NCH)
            pe.wait_ge(consts, 1)
            pe.sem_inc(pv_done, 1)
            with pe.Fori(0, HEADS) as h:
                def scores(i, c, m):
                    n = 2 * (C0[i] + c) + m
                    if c == 0 and m == 0:
                        pe.wait_ge(q_in[i % 2], h * (8 * 32) + (i // 2 + 1) * 32)
                        pe.wait_ge(kv_in[i // 4], 32)
                    pe.wait_ge(exp_done, h * (2 * NCH) + n + 1)
                    tiles = W[i][c] // P
                    diag = c == CH[i] - 1
                    last = nc.tensor.matmul(pS[:, n % 4, 0:W[i][c]], qz[i % 2][:, m, :], kT[:, 4 * c:4 * c + tiles, bass.ds(h * P, P)],
                                            start=True, stop=not diag)
                    if diag:
                        last = nc.tensor.matmul(pS[:, n % 4, W[i][c] - P:W[i][c]], ident[:], mask[:], start=False, stop=True)
                    last.then_inc(s_done, 1)

                def turn(i, c):
                    n = C0[i] + c
                    pe.wait_ge(attn_done, h * NCH + n + 1)
                    pe.wait_ge(Tc_done, h * NCH + n + 1)
                    for b in range(W[i][c] // P):
                        last = nc.tensor.transpose(pT[:, n % 2, b * P:(b + 1) * P], prob[i % 2][0][:, c * BANK + b * P:c * BANK + (b + 1) * P], ident[:])
                    last.then_inc(T_done, 1)

                def values(i, c):
                    n = C0[i] + c
                    if c == 0:
                        pe.wait_ge(o_done, h * TILES + i + 1)
                    pe.wait_ge(Tc_done, h * NCH + n + 3)
                    for b in range(W[i][c] // P):
                        kb = 4 * c + b
                        last = nc.tensor.matmul(pO[:, i % 2, 0:P], aT[n % 2][:, b * P:(b + 1) * P], v[:, kb, bass.ds(h * P, P)],
                                                start=(kb == 0), stop=(kb == i))
                    last.then_inc(pv_done, 1)
                for i in range(-1, TILES):
                    k = CH[i] if i >= 0 else 0
                    for c in range(max(k, CH[i + 1] if i + 1 < TILES else 0)):
                        if i + 1 < TILES and c < CH[i + 1]:
                            scores(i + 1, c, 0)
                            scores(i + 1, c, 1)
                        if c < k:
                            turn(i, c)
                            if c > 0:
                                values(i, c - 1)
                    if k:
                        values(i, k - 1)


HV = 8
CK = 64
DECAY = math.exp(-0.5)
GN_EPS = 64e-5
LEVELS = (1, 2, 4, 8, 16, 32)


class Events:

    def __init__(self, sem, names):
        self.sem, self.at = sem, {n: k + 1 for k, n in enumerate(names)}
        assert len(self.at) == len(names)
        self.n, self.seen = len(names), 0

    def value(self, name, step):
        return self.nth(self.at[name], step)

    def nth(self, k, step):
        return step * self.n + (self.n + k)

    def in_order(self, name):
        assert self.at[name] == self.seen % self.n + 1, (name, self.seen % self.n)
        self.seen += 1


AB = "ab"
PE_JOBS = (["cum", "G3a", "G3b", "G1_0", "G1_1", "Tr0a", "G1_2", "G1_3", "Tr0b", "G2_0", "G2_1", "X1a", "X1b", "Wa", "Wb",
            "TX1a", "G2_2", "TX1b", "G2_3", "Tr1a", "MN0", "Tr1b", "MN1", "X2a", "RT", "X2b", "Y0", "TX2a", "S0", "TX2b",
            "Tr2a", "S1", "Tr2b", "X3a", "Ya", "X3b", "Yb", "TX3a", "Da", "TX3b", "Db", "Tr3a", "Tr3b", "pc", "X4a", "X4b", "TX4a", "TX4b",
            "Tr4a", "T0", "Tr4b", "T1", "X5a", "T2", "X5b", "T3", "TX5a", "TX5b", "Tr5a", "Tr5b"])
PREP_JOBS = ("cum", "pc", "T0", "T1", "T2", "T3")
TAIL = ("Wa", "Wb", "MN0", "MN1", "RT", "Y0", "S0", "S1", "Ya", "Yb", "sqy", "s1", "yc", "s2", "yn", "ysum", "rsy", "out")
PREP = PREP_JOBS + ("P", "cumsb", "Pex", "sqk", "vcopy", "kp", "ssk", "kkn", "Ah", "Bh", "bon", "T_init", "rkv", "kk0", "rsk", "ex", "b", "Kh", "Rh", "rk", "bv")
ACT_EV = ["P", "cumsb", "Tr0a", "Tr0b", "X1a", "X1b", "Wa", "Wb", "sqk", "Tr1a", "Tr1b", "Pex", "X2a", "X2b", "Y0", "Tr2a", "Tr2b",
          "X3a", "X3b", "Da", "Db", "Tr3a", "Tr3b", "sqy", "pc", "X4a", "X4b", "vcopy", "Tr4a", "T0", "Tr4b", "T1", "X5a", "T2", "X5b", "T3", "Tr5a", "Tr5b"]
DVE_EV = ["G3a", "G3b", "G1_0", "G1_1", "G1_2", "G1_3", "G2_0", "G2_1", "TX1a", "G2_2", "TX1b", "G2_3", "kp", "ssk", "MN0", "MN1", "kkn", "RT", "TX2a", "S0", "TX2b",
          "S1", "Ya", "Yb", "s1", "yc", "TX3a", "TX3b", "Ah", "Bh", "s2", "TX4a", "TX4b", "bon", "yn", "TX5a", "TX5b"]
POOL_EV = ["rkv", "kk0", "rsk", "ex", "b", "Kh", "Rh", "rk", "T_init", "rsy", "bv", "out"]
MAIN_JOBS = [n for n in PE_JOBS if n not in PREP_JOBS]
BANKS = 6
FIRST_OF = (0, 4, 1, 5)


def phase_rwkv(nc, t, ident):
    with ExitStack() as ctx:
        sb = lambda n, s, d=F32: ctx.enter_context(nc.sbuf_tensor(n, s, d))
        sem = lambda n: t["semctx"].enter_context(nc.semaphore(n))
        two = lambda n, s, d=F32: [sb(f"{n}{k}", s, d) for k in range(2)]
        assert len(MAIN_JOBS) % BANKS == 0
        z = two("c_z", [P, 3 * RW]); rkv = two("c_rkv", [P, 3 * RW])
        sig = two("c_sig", [P, RW]); a = two("c_a", [P, RW]); g = two("c_g", [P, RW])
        mu = sb("c_mu", [P, 3 * RW]); k_k = sb("c_kk", [P, RW]); k_a = sb("c_ka", [P, RW]); r_k = sb("c_rk", [P, RW])
        gn_w = sb("c_gnw", [P, RW]); gn_b = sb("c_gnb", [P, RW])
        Pt = sb("c_P", [P, RW]); iP = sb("c_invP", [P, RW]); cumsb = sb("c_cum", [P, RW]); Pex = sb("c_Pex", [P, RW])
        kk0 = sb("c_kk0", [P, RW]); sq = sb("c_sq", [P, RW]); kp = sb("c_kp", [P, RW]); kkn = sb("c_kkn", [P, RW]); bb = sb("c_b", [P, RW])
        rk = sb("c_rkp", [P, RW]); bon = sb("c_bon", [P, HV]); ssk = sb("c_ssk", [P, HV]); rsk = sb("c_rsk", [P, HV])
        AD = two("c_AD", [P, 2, HV, DH])
        Bh = two("c_Bh", [P, RW]); Kh = two("c_Kh", [P, RW]); Rh = sb("c_Rh", [P, RW]); V = two("c_V", [P, RW]); bv = two("c_bv", [P, RW])
        cT = two("c_cT", [P, 4, 4, P])
        pc = two("c_pc", [P, 4, 2])
        AR1 = two("c_AR1", [P, HV, 2, P]); AR2 = two("c_AR2", [P, HV, 2, P])
        T = two("c_T", [P, HV, CK]); TB = two("c_TB", [P, HV, P])
        TT = two("c_TT", [P, HV, P]); X = sb("c_X", [P, HV, CK])
        WU = sb("c_WU", [P, HV, 2, DH]); RpT = sb("c_RpT", [P, 4, P]); Y0 = sb("c_Y0", [P, RW])
        MT = sb("c_MT", [P, 2, 4, DH]); NN = sb("c_NN", [P, 2, 4, DH]); St = sb("c_Stmp", [P, 4, DH])
        S = [two(f"c_S{k}", [P, 4, DH]) for k in range(2)]
        y = sb("c_y", [P, RW]); s1 = sb("c_s1", [P, HV]); s2 = sb("c_s2", [P, HV]); rsy = sb("c_rsy", [P, HV]); yo = sb("c_yo", [P, RW])
        cst = sb("c_consts", [P, 4, HV]); tiny = sb("c_tiny", [P, HV])
        maskG = sb("c_maskG", [P, 2, P]); i64 = sb("c_i64", [P, CK]); ind = sb("c_ind", [P, 2])
        lv = sb("c_levels", [P, len(LEVELS), CK], I32); bits = sb("c_bits", [P, 3, CK], I32)
        ps = ctx.enter_context(nc.psum_tensor("p_ring", [P, 8, BANK], F32))

        z_in = [sem(f"C_z_in{k}") for k in range(2)]; g_in = [sem(f"C_g_in{k}") for k in range(2)]; par = sem("C_params"); o_out = sem("C_out")
        cs_p = sem("C_masks"); passed = sem("C_passed")
        PE = Events(sem("C_pe"), PE_JOBS); AC = Events(sem("C_act"), ACT_EV)
        DV = Events(sem("C_dve"), DVE_EV); PO = Events(sem("C_pool"), POOL_EV)
        block = ctx.enter_context(nc.Block())

        def bank(name):
            return ps[:, MAIN_JOBS.index(name) % BANKS, :] if name in MAIN_JOBS else ps[:, BANKS + PREP_JOBS.index(name) % 2, :]

        def owner(name):
            ev = {"cum": "cumsb"}.get(name, name)
            return (AC, ev) if ev in AC.at else (DV, ev)

        def steps(eng, body):
            body(-1, 1, {"prep"}, None)
            body(0, 0, {"main", "prep"}, None)
            with eng.Fori(0, (TILES - 2) // 2) as j:
                body(j * 2 + 1, 1, {"main", "tail", "prep"}, j)
                body(j * 2 + 2, 0, {"main", "tail", "prep"}, j)
            body(TILES - 1, 1, {"main", "tail"}, None)
            body(TILES, 0, {"tail"}, None)

        def nth(tile, j, ahead):
            return tile // 2 if isinstance(tile, int) else j + ahead

        def group(name):
            return "tail" if name in TAIL else "prep" if name in PREP else "main"

        def heads(ap):
            return ap.rearrange("p (h d) -> p h d", d=DH)

        @block.sync
        def _(sp):
            sp.dma_start(mu[:], t["mu_rkv"].rearrange("m n -> (m n)").partition_broadcast(P)).then_inc(par, 16)
            for dst, name in ((k_k, "k_k"), (k_a, "k_a"), (r_k, "r_k"), (gn_w, "gn_w"), (gn_b, "gn_b")):
                src = t[name].rearrange("h n -> (h n)") if name == "r_k" else t[name]
                sp.dma_start(dst[:], src.partition_broadcast(P)).then_inc(par, 16)

            def load(i, s):
                sp.dma_start(z[s][:], t["zr"][bass.ds(i * P + 1, P), :]).then_inc(z_in[s], 16)
                sp.dma_start(rkv[s][:], t["zr"][bass.ds(i * P, P), :]).then_inc(z_in[s], 16)
                sp.dma_start(sig[s][:], t["lo"][0, bass.ds(i * P, P), :]).then_inc(z_in[s], 16)
                sp.dma_start(a[s][:], t["lo"][1, bass.ds(i * P, P), :]).then_inc(z_in[s], 16)
            load(0, 0)
            load(1, 1)
            sp.sem_inc(o_out, 16)
            sp.dma_start(g[0][:], t["lo"][2, 0:P, :]).then_inc(g_in[0], 16)
            sp.dma_start(g[1][:], t["lo"][2, P:2 * P, :]).then_inc(g_in[1], 16)

            def step(i, s, what, j):
                if "tail" in what:
                    sp.wait_ge(PO.sem, PO.value("out", i))
                    sp.dma_start(t["mix"][bass.ds((i - 1) * P, P), RW:2 * RW], yo[:]).then_inc(o_out, 16)
                    if "prep" in what:
                        sp.dma_start(g[1 - s][:], t["lo"][2, bass.ds((i + 1) * P, P), :]).then_inc(g_in[1 - s], 16)
            def reload(i, s):
                sp.wait_ge(PO.sem, PO.value("bv", i - 1))
                sp.wait_ge(DV.sem, DV.value("bon", i - 1))
                sp.wait_ge(AC.sem, AC.value("vcopy", i - 1))
                load(i + 2, s)
            reload(0, 0)
            reload(1, 1)
            with sp.Fori(0, (TILES - 2) // 2 - 1) as j:
                step(j * 2 + 1, 1, {"main", "tail", "prep"}, j)
                reload(j * 2 + 2, 0)
                step(j * 2 + 2, 0, {"main", "tail", "prep"}, j)
                reload(j * 2 + 3, 1)
            step(TILES - 3, 1, {"main", "tail", "prep"}, None)
            step(TILES - 2, 0, {"main", "tail", "prep"}, None)
            step(TILES - 1, 1, {"main", "tail"}, None)
            step(TILES, 0, {"tail"}, None)
            sp.wait_ge(o_out, 16 * (TILES + 1))

        @block.gpsimd
        def _(pool):
            for n, c in enumerate((1.0 / DH, GN_EPS, -0.5)):
                pool.memset(cst[:, n, :], c)
            pool.memset(maskG[:], 1.0)
            pool.memset(ind[:], 0.0)
            pool.memset(i64[:], 0.0)
            for k in range(2):
                pool.memset(S[k][0][:], 0.0)
            pool.iota(bits[:, 0, :], pattern=[[0, CK]], base=0, channel_multiplier=1)
            pool.iota(bits[:, 1, :], pattern=[[1, CK]], base=0, channel_multiplier=0)
            pool.drain()
            for c in range(2):
                r = slice(c * CK, c * CK + CK)
                pool.memset(ind[r, c:c + 1], 1.0)
                pool.memset(maskG[r, :, (1 - c) * CK:(1 - c) * CK + CK], 0.0)
                pool.affine_select(out=i64[r, :], in_=i64[r, :], compare_op=ALU.not_equal, fill=1.0, base=0,
                                   pattern=[[-1, CK]], channel_multiplier=1)
            pool.drain()
            for kind in range(2):
                pool.affine_select(out=maskG[:, kind, :], in_=maskG[:, kind, :], compare_op=ALU.is_ge, fill=0.0,
                                   base=kind - 1, pattern=[[1, P]], channel_multiplier=-1)
            pool.drain()
            pool.tensor_copy(tiny[:], cst[:, 0, :]).then_inc(cs_p, 1)
            pool.wait_ge(par, 16 * 6)

            def step(i, s, what, j):
                n = 1 - s

                def ev(name, make):
                    if group(name) in what:
                        PO.in_order(name)
                        make().then_inc(PO.sem, 1)
                    else:
                        PO.in_order(name)
                        pool.drain().then_inc(PO.sem, 1)

                def mul(out, x0, x1, op=ALU.mult):
                    return lambda: pool.tensor_tensor(out, x0, x1, op)
                real = "prep" in what
                if real:
                    pool.wait_ge(z_in[n], nth(i + 1, j, 1) * 64 + 64)
                    pool.tensor_tensor(rkv[n][:], rkv[n][:], z[n][:], ALU.subtract)
                    pool.drain()
                    pool.tensor_tensor(rkv[n][:], rkv[n][:], mu[:], ALU.mult)
                    pool.drain()
                ev("rkv", mul(rkv[n][:], rkv[n][:], z[n][:], ALU.add))
                pool.drain()
                ev("kk0", mul(kk0[:], rkv[n][:, RW:2 * RW], k_k[:]))
                if real:
                    pool.wait_ge(DV.sem, DV.value("ssk", i))
                ev("rsk", mul(rsk[:], ssk[:], cst[:, 2, :], ALU.pow))
                if real:
                    pool.wait_ge(AC.sem, AC.value("cumsb", i))
                ev("ex", mul(cumsb[:], cumsb[:], sig[n][:], ALU.subtract))
                if real:
                    pool.wait_ge(DV.sem, DV.value("kkn", i))
                ev("b", mul(bb[:], kkn[:], a[n][:]))
                if real:
                    pool.wait_ge(DV.sem, DV.value("kp", i))
                    pool.wait_ge(AC.sem, AC.value("P", i))
                    pool.wait_ge(PE.sem, PE.value("MN1", i))
                ev("Kh", mul(Kh[n][:], kp[:], iP[:]))
                ev("Rh", mul(Rh[:], rkv[n][:, 0:RW], Pt[:]))
                if real:
                    pool.tensor_tensor(rk[:], rkv[n][:, 0:RW], kp[:], ALU.mult)
                    pool.drain()
                ev("rk", mul(rk[:], rk[:], r_k[:]))
                if real:
                    pool.wait_ge(PE.sem, PE.value("Tr5b", i - 1)) if not (isinstance(i, int) and i < 0) else None
                    pool.sem_inc(passed, 1)
                    pool.tensor_copy(T[n][:], i64[:].unsqueeze(1).broadcast_to([P, HV, CK]))
                ev("T_init", lambda: pool.tensor_copy(TB[n][:], ident[:].unsqueeze(1).broadcast_to([P, HV, P])))
                if "tail" in what:
                    pool.wait_ge(DV.sem, DV.value("s2", i))
                    pool.tensor_tensor(tiny[:], s2[:], cst[:, 0, :], ALU.mult)
                    pool.drain()
                    pool.tensor_tensor(tiny[:], tiny[:], cst[:, 1, :], ALU.add)
                    pool.drain()
                ev("rsy", mul(rsy[:], tiny[:], cst[:, 2, :], ALU.pow))
                if "tail" in what:
                    pool.wait_ge(DV.sem, DV.value("yn", i))
                    pool.wait_ge(g_in[n], nth(i - 1, j, 0) * 16 + 16)
                    pool.wait_ge(o_out, i * 16)
                    pool.tensor_tensor(yo[:], y[:], gn_w[:], ALU.mult)
                    pool.drain()
                    pool.tensor_tensor(yo[:], yo[:], gn_b[:], ALU.add)
                    pool.drain()
                    pool.tensor_tensor(yo[:], yo[:], bv[n][:], ALU.add)
                    pool.drain()
                if real:
                    pool.wait_ge(DV.sem, DV.value("bon", i))
                ev("bv", lambda: pool.tensor_tensor(heads(bv[n][:]), heads(rkv[n][:, 2 * RW:3 * RW]), bon[:].unsqueeze(2).broadcast_to([P, HV, DH]), ALU.mult))
                ev("out", mul(yo[:], yo[:], g[n][:]))

            steps(pool, step)

        @block.scalar
        def _(act):
            act.wait_ge(cs_p, 1)

            def step(i, s, what, j):
                n = 1 - s

                def ev(name, make, *waits):
                    if group(name) in what:
                        for e, other in waits:
                            act.wait_ge(e.sem, e.value(other, i))
                        AC.in_order(name)
                        make().then_inc(AC.sem, 1)
                    else:
                        AC.in_order(name)
                        act.drain().then_inc(AC.sem, 1)

                def evac(name, out, src=None, waits=()):
                    b = bank(name)
                    ev(name, lambda: nc.scalar.copy(out, src(b) if src else b), (PE, name), *waits)

                def four(b):
                    return b.rearrange("p (h n) -> p h n", h=4)

                def tr(level, f):
                    evac(f"Tr{level}{f}", TT[s][:, half(f), :], four)

                def x_(level, f):
                    evac(f"X{level}{f}", X[:, half(f), :], lambda b: b[:, 0:4 * CK].rearrange("p (h n) -> p h n", h=4))
                if "prep" in what:
                    act.wait_ge(PE.sem, PE.value("cum", i))
                    act.wait_ge(PO.sem, PO.value("Rh", i - 1)) if not (isinstance(i, int) and i < 0) else None
                    act.wait_ge(DV.sem, DV.value("Bh", i - 1)) if not (isinstance(i, int) and i < 0) else None
                    nc.scalar.activation(Pt[:], bank("cum"), ACT.Exp, scale=-DECAY)
                ev("P", lambda: nc.scalar.activation(iP[:], bank("cum"), ACT.Exp, scale=DECAY))
                ev("cumsb", lambda: nc.scalar.copy(cumsb[:], bank("cum")))
                tr(0, "a")
                tr(0, "b")
                x_(1, "a")
                x_(1, "b")
                for f in AB:
                    evac(f"W{f}", WU[:, half(f), :, :].rearrange("p h a d -> p h (a d)"), four)
                ev("sqk", lambda: nc.scalar.activation(sq[:], kk0[:], ACT.Square), (PO, "kk0"))
                tr(1, "a")
                tr(1, "b")
                ev("Pex", lambda: nc.scalar.activation(Pex[:], cumsb[:], ACT.Exp, scale=-DECAY), (PO, "ex"))
                x_(2, "a")
                x_(2, "b")
                evac("Y0", Y0[:])
                tr(2, "a")
                tr(2, "b")
                x_(3, "a")
                x_(3, "b")
                for f in AB:
                    evac(f"D{f}", AD[s][:, 1, half(f), :], lambda b: b[:, 0:4 * DH].rearrange("p (h n) -> p h n", h=4))
                tr(3, "a")
                tr(3, "b")
                ev("sqy", lambda: nc.scalar.activation(sq[:], y[:], ACT.Square), (DV, "yc"))
                ev("pc", lambda: nc.scalar.activation(pc[n][:], bank("pc")[:, 0:8].rearrange("p (a c) -> p a c", c=2), ACT.Exp, scale=-DECAY),
                   (PE, "pc"), (DV, "S1"))
                x_(4, "a")
                x_(4, "b")
                ev("vcopy", lambda: nc.scalar.copy(V[n][:], rkv[n][:, 2 * RW:3 * RW]), (PO, "rkv"), (PE, "Y0"))

                def t_(p):
                    evac(f"T{p}", cT[n][:, p, :, :], lambda b: b.rearrange("p (k n) -> p k n", k=4), ((DV, "RT"),))
                tr(4, "a")
                t_(0)
                tr(4, "b")
                t_(1)
                x_(5, "a")
                t_(2)
                x_(5, "b")
                t_(3)
                tr(5, "a")
                tr(5, "b")
            steps(act, step)

        @block.vector
        def _(dve):
            dve.wait_ge(cs_p, 1)
            nc.vector.tensor_scalar(bits[:, 0, :], bits[:, 0, :], CK - 1, None, ALU.bitwise_and)
            dve.drain()
            nc.vector.tensor_tensor(bits[:, 2, :], bits[:, 0, :], bits[:, 1, :], ALU.bitwise_xor)
            dve.drain()
            for b in range(len(LEVELS)):
                nc.vector.tensor_scalar(lv[:, b, :], bits[:, 2, :], b, None, ALU.logical_shift_right)
                nc.vector.tensor_scalar(bits[:, 1, :], bits[:, 0, :], b, 1, ALU.logical_shift_right, ALU.bitwise_and)
                dve.drain()
                nc.vector.tensor_scalar(lv[:, b, :], lv[:, b, :], 1.0, None, ALU.is_equal)
                dve.drain()
                nc.vector.tensor_tensor(lv[:, b, :], lv[:, b, :], bits[:, 1, :], ALU.mult)
                dve.drain()
            dve.wait_ge(par, 16 * 6)

            def step(i, s, what, j):
                n = 1 - s
                started = not (isinstance(i, int) and i < 0)

                def ev(name, make, *waits):
                    if group(name) in what:
                        for e, other in waits:
                            dve.wait_ge(e.sem, e.value(other, i))
                        if name[:2] in ("G3", "TX"):
                            dve.sem_inc(passed, 1)
                        DV.in_order(name)
                        make().then_inc(DV.sem, 1)
                    else:
                        DV.in_order(name)
                        dve.drain().then_inc(DV.sem, 1)

                def fill_T(name, level, f):
                    def make():
                        src = bank(name)[:, 0:4 * CK].rearrange("p (h n) -> p h n", h=4)
                        m = lv[:, level, :].unsqueeze(1).broadcast_to([P, 4, CK])
                        nc.vector.copy_predicated(T[s][:, half(f), :], m, src)
                        nc.vector.copy_predicated(TB[s][0:CK, half(f), 0:CK], m[0:CK], src[0:CK])
                        return nc.vector.copy_predicated(TB[s][CK:P, half(f), CK:P], m[CK:P], src[CK:P])
                    ev(name, make, (PE, name))

                def masked(name, dst, p):
                    h0 = FIRST_OF[p]
                    ev(name, lambda: nc.vector.tensor_tensor(dst[s][:, h0:h0 + 3:2, :, :].rearrange("p h k n -> p h (k n)"),
                                                             bank(name).rearrange("p (h n) -> p h n", h=2),
                                                             maskG[:].rearrange("p k n -> p (k n)").unsqueeze(1).broadcast_to([P, 2, 2 * P]), ALU.mult),
                       (PE, name))
                if "main" in what:
                    dve.wait_ge(PO.sem, PO.value("T_init", i - 1))
                for f in AB:
                    fill_T(f"G3{f}", 0, f)
                for p in range(4):
                    masked(f"G1_{p}", AR1, p)
                masked("G2_0", AR2, 0)
                masked("G2_1", AR2, 1)
                fill_T("TX1a", 1, "a")
                masked("G2_2", AR2, 2)
                fill_T("TX1b", 1, "b")
                masked("G2_3", AR2, 3)
                if "prep" in what:
                    dve.wait_ge(PO.sem, PO.value("kk0", i))
                    dve.wait_ge(z_in[n], nth(i + 1, j, 1) * 64 + 64)
                    nc.vector.scalar_tensor_tensor(kp[:], a[n][:], -1.0, k_a[:], ALU.add, ALU.mult)
                    dve.drain()
                ev("kp", lambda: nc.vector.scalar_tensor_tensor(kp[:], kp[:], 1.0, rkv[n][:, RW:2 * RW], ALU.add, ALU.mult))
                if "prep" in what:
                    dve.wait_ge(AC.sem, AC.value("sqk", i))
                    nc.vector.tensor_reduce(ssk[:], heads(sq[:]), AX.X, ALU.add)
                    dve.drain()
                ev("ssk", lambda: nc.vector.tensor_scalar(ssk[:], ssk[:], 1e-24, None, ALU.max))
                for c in range(2):
                    def mn():
                        b = bank(f"MN{c}")
                        nc.vector.tensor_tensor(MT[:, c, :, :], b[:, 0:4 * DH].rearrange("p (a d) -> p a d", d=DH),
                                                i64[:].unsqueeze(1).broadcast_to([P, 4, DH]), ALU.add)
                        return nc.vector.tensor_copy(NN[:, c, :, :], b[:, 4 * DH:8 * DH].rearrange("p (a d) -> p a d", d=DH))
                    ev(f"MN{c}", mn, (PE, f"MN{c}"))
                ev("kkn", lambda: nc.vector.tensor_tensor(heads(kkn[:]), heads(kk0[:]), rsk[:].unsqueeze(2).broadcast_to([P, HV, DH]), ALU.mult),
                   (PO, "rsk"))
                ev("RT", lambda: nc.vector.tensor_tensor(RpT[:], bank("RT").rearrange("p (a n) -> p a n", a=4), cT[n][:, :, 1, :], ALU.add), (PE, "RT"))

                def state(c):
                    def make():
                        nc.vector.tensor_tensor(St[:], bank(f"S{c}")[:, 0:4 * DH].rearrange("p (a d) -> p a d", d=DH), NN[:, c, :, :], ALU.add)
                        dve.drain()
                        dst = S[n][1] if c == 0 else S[s][0]
                        return nc.vector.tensor_tensor(dst[:], St[:], pc[n][:, :, c:c + 1].broadcast_to([P, 4, DH]), ALU.mult)
                    ev(f"S{c}", make, (PE, f"S{c}"))
                fill_T("TX2a", 2, "a")
                state(0)
                fill_T("TX2b", 2, "b")
                state(1)
                if "tail" in what:
                    dve.wait_ge(PO.sem, PO.value("out", i - 1))
                for f in AB:
                    ev(f"Y{f}", lambda: nc.vector.tensor_tensor(heads(y[:])[:, half(f), :], bank(f"Y{f}")[:, 0:4 * DH].rearrange("p (h n) -> p h n", h=4),
                                                                heads(Y0[:])[:, half(f), :], ALU.add), (PE, f"Y{f}"), (AC, "Y0"))
                dve.drain()

                def mean():
                    nc.vector.tensor_reduce(s1[:], heads(y[:]), AX.X, ALU.add)
                    dve.drain()
                    return nc.vector.tensor_scalar(s1[:], s1[:], 1.0 / DH, None, ALU.mult)
                ev("s1", mean)
                dve.drain()
                ev("yc", lambda: nc.vector.tensor_tensor(heads(y[:]), heads(y[:]), s1[:].unsqueeze(2).broadcast_to([P, HV, DH]), ALU.subtract))
                fill_T("TX3a", 3, "a")
                fill_T("TX3b", 3, "b")
                ev("Ah", lambda: nc.vector.scalar_tensor_tensor(AD[n][:, 0, :, :], heads(kkn[:]), -1.0, heads(Pex[:]), ALU.mult, ALU.mult), (AC, "Pex"), (PE, "Wb"))
                ev("Bh", lambda: nc.vector.tensor_tensor(Bh[n][:], bb[:], iP[:], ALU.mult), (PO, "b"), (PE, "MN1"))
                ev("s2", lambda: nc.vector.tensor_reduce(s2[:], heads(sq[:]), AX.X, ALU.add), (AC, "sqy"))
                fill_T("TX4a", 4, "a")
                fill_T("TX4b", 4, "b")
                ev("bon", lambda: nc.vector.tensor_reduce(bon[:], heads(rk[:]), AX.X, ALU.add), (PO, "rk"))
                ev("yn", lambda: nc.vector.tensor_tensor(heads(y[:]), heads(y[:]), rsy[:].unsqueeze(2).broadcast_to([P, HV, DH]), ALU.mult), (PO, "rsy"))
                fill_T("TX5a", 5, "a")
                fill_T("TX5b", 5, "b")

            steps(dve, step)

        @block.tensor
        def _(pe):
            pe.wait_ge(cs_p, 1)

            def step(i, s, what, j):
                n = 1 - s
                first = isinstance(i, int) and i < 0

                def job(name, make, *waits):
                    if group(name) not in what:
                        PE.in_order(name)
                        pe.drain().then_inc(PE.sem, 1)
                        return
                    ring, size = (MAIN_JOBS, BANKS) if name in MAIN_JOBS else (PREP_JOBS, 2)
                    k = ring.index(name)
                    e, other = owner(ring[k - size])
                    free = [(e, other, 0 if k >= size else 1)] if k >= size or not first else []
                    for e in (AC, DV, PO):
                        asked = [(-back, e.at[other]) for who, other, back in (*free, *waits) if who is e]
                        if asked:
                            back, at_ = max(asked)
                            pe.wait_ge(e.sem, e.nth(at_, i + back))
                    if name[:2] in ("G3", "MN", "S0", "S1", "Ya", "Yb"):
                        pe.sem_inc(passed, 1)
                    PE.in_order(name)
                    make(bank(name)).then_inc(PE.sem, 1)

                def each(name, hs, mm, *waits):
                    def make(b):
                        for h in hs:
                            last = mm(b, h)
                        return last
                    job(name, make, *waits)

                def cols(b, h, w):
                    return b[:, h * w:(h + 1) * w]

                def at(h):
                    return slice(DH * (h % 2), DH * (h % 2) + DH)

                def cum(b):
                    return nc.tensor.matmul(b, maskG[:, 1, :], sig[n][:], start=True, stop=True)

                def chunk_ends(b):
                    for p in range(4):
                        last = nc.tensor.matmul(b[:, 2 * p:2 * p + 2], sig[n][:, p * P:(p + 1) * P], ind[:], start=True, stop=True)
                    return last
                if "prep" in what:
                    pe.wait_ge(z_in[n], nth(i + 1, j, 1) * 64 + 64)
                job("cum", cum)

                def g3(b, h):
                    for c in range(2):
                        r = slice(c * CK, c * CK + CK)
                        last = nc.tensor.matmul(b[r, (h // 2) * CK:(h // 2 + 1) * CK], cT[s][at(h), h // 2, 0, r], cT[s][at(h), h // 2, 2, r], start=True, stop=True)
                    return last

                def g12(kind):
                    return lambda b, h: nc.tensor.matmul(b[:, (h // 2 % 2) * 2 * P:(h // 2 % 2 + 1) * 2 * P], cT[s][at(h), h // 2, kind, :],
                                                         cT[s][at(h), h // 2, 0:2, :], start=True, stop=True)

                def g1(p):
                    each(f"G1_{p}", (FIRST_OF[p], FIRST_OF[p] + 2), g12(2))

                def g2(p):
                    each(f"G2_{p}", (FIRST_OF[p], FIRST_OF[p] + 2), g12(3))

                def tr(level, f):
                    each(f"Tr{level}{f}", hs_of(f), lambda b, h: nc.tensor.transpose(cols(b, h // 2, P), TB[s][:, h, :], ident[:]),
                         (DV, ("G3" if level == 0 else f"TX{level}") + f, 0))

                def x_(level, f):
                    each(f"X{level}{f}", hs_of(f), lambda b, h: nc.tensor.matmul(cols(b, h // 2, CK), AR1[s][:, h, 0, :], T[s][:, h, :], start=True, stop=True),
                         (DV, ("G3" if level == 1 else f"TX{level - 1}") + f, 0), (DV, "G1_3" if f == "b" else "G1_1", 0))

                def tx(level, f):
                    each(f"TX{level}{f}", hs_of(f), lambda b, h: nc.tensor.matmul(cols(b, h // 2, CK), TT[s][:, h, :], X[:, h, :], start=True, stop=True),
                         (AC, f"X{level}{f}", 0), (AC, f"Tr{level - 1}{f}", 0))

                def w_(f):
                    each(f"W{f}", hs_of(f), lambda b, h: nc.tensor.matmul(cols(b, h // 2, P), TT[n][:, h, :], AD[n][:, :, h, :], start=True, stop=True),
                         (AC, f"Tr5{f}", 1), (AC, "Db", 1))

                def mn(c):
                    r = slice(c * CK, c * CK + CK)

                    def mm(b, h):
                        o, col = at(h), (h // 2) * DH
                        hc = slice(h * DH, h * DH + DH)
                        nc.tensor.matmul(b[o, col:col + DH], WU[r, h, 0, :], Bh[n][r, hc], start=True, stop=True)
                        nc.tensor.matmul(b[o, 4 * DH + col:4 * DH + col + DH], Bh[n][r, hc], WU[r, h, 1, :], start=True, stop=False)
                        return nc.tensor.matmul(b[o, 4 * DH + col:4 * DH + col + DH], Kh[n][r, hc], V[n][r, hc], start=False, stop=True)
                    each(f"MN{c}", range(HV), mm, (AC, "Wb", 0))

                def rt(b, h):
                    return nc.tensor.matmul(b[at(h), (h // 2) * P:(h // 2 + 1) * P], WU[:, h, 0, :], AR1[n][:, h, 1, :], start=True, stop=True)

                def y0(b, h):
                    nc.tensor.matmul(cols(b, h, DH), AR1[n][:, h, 1, :], WU[:, h, 1, :], start=True, stop=False)
                    return nc.tensor.matmul(cols(b, h, DH), AR2[n][:, h, 1, :], V[n][:, h * DH:(h + 1) * DH], start=False, stop=True)

                def s_(c):
                    each(f"S{c}", range(HV), lambda b, h: nc.tensor.matmul(b[at(h), (h // 2) * DH:(h // 2 + 1) * DH], MT[at(h), c, h // 2, :], S[n][c][at(h), h // 2, :], start=True, stop=True),
                         (DV, f"MN{c}", 0), *(((DV, "S0", 0),) if c else ((DV, "S1", 1),)))

                def y_(b, h):
                    for c in range(2):
                        r = slice(c * CK, c * CK + CK)
                        last = nc.tensor.matmul(b[r, (h // 2) * DH:(h // 2 + 1) * DH], RpT[at(h), h // 2, r], S[n][c][at(h), h // 2, :], start=True, stop=True)
                    return last

                def d_(b, h):
                    return nc.tensor.matmul(cols(b, h // 2, DH), AR2[s][:, h, 0, :], V[s][:, h * DH:(h + 1) * DH], start=True, stop=True)

                def t_(p):
                    def make(b):
                        for k, src in enumerate((AD[n][:, 0, 2 * p:2 * p + 2, :].rearrange("p h d -> p (h d)"), Rh[:, p * P:(p + 1) * P], Bh[n][:, p * P:(p + 1) * P], Kh[n][:, p * P:(p + 1) * P])):
                            last = nc.tensor.transpose(b[:, k * P:(k + 1) * P], src, ident[:])
                        return last
                    job(f"T{p}", make, (DV, "Bh", 0), (PO, "Rh", 0))
                each("G3a", hs_of("a"), g3, (AC, "T3", 1))
                each("G3b", hs_of("b"), g3)
                g1(0); g1(1); tr(0, "a"); g1(2); g1(3); tr(0, "b"); g2(0); g2(1)
                x_(1, "a"); x_(1, "b"); w_("a"); w_("b")
                tx(1, "a"); g2(2); tx(1, "b"); g2(3)
                tr(1, "a"); mn(0); tr(1, "b"); mn(1)
                x_(2, "a"); each("RT", range(HV), rt); x_(2, "b"); each("Y0", range(HV), y0); tx(2, "a"); s_(0)
                tx(2, "b"); tr(2, "a"); s_(1); tr(2, "b")
                x_(3, "a"); each("Ya", hs_of("a"), y_, (DV, "RT", 0), (DV, "S0", 0)); x_(3, "b"); each("Yb", hs_of("b"), y_)
                tx(3, "a"); each("Da", hs_of("a"), d_, (DV, "G2_3", 0), (AC, "vcopy", 1)); tx(3, "b"); each("Db", hs_of("b"), d_)
                tr(3, "a"); tr(3, "b")
                job("pc", chunk_ends)
                x_(4, "a"); x_(4, "b"); tx(4, "a"); tx(4, "b")
                tr(4, "a"); t_(0); tr(4, "b"); t_(1)
                x_(5, "a"); t_(2); x_(5, "b"); t_(3); tx(5, "a"); tx(5, "b"); tr(5, "a"); tr(5, "b")
            steps(pe, step)


def half(f):
    return slice(AB.index(f), HV, 2)


def hs_of(f):
    return range(AB.index(f), HV, 2)


GROUPS, PER_GROUP = 4, 8
EXPERTS = GROUPS * PER_GROUP
DX = 512
KX = DX // P
BLOCKS = 2 * SEQ // P + EXPERTS
SLOTS = 3
LOW = -3e38
PL = 256


def first_pairs_last(eng, n, body):
    body(0, 0)
    body(1, 1)
    with eng.Fori(1, n // 2 - 1) as j:
        body(j * 2, 0)
        body(j * 2 + 1, 1)
    body(n - 2, 0)
    body(n - 1, 1)


def known(i):
    return i if isinstance(i, int) else None


def load_expert(sp, t, weights, e, s, w_in):
    for w, name in zip(weights, ("w_gate", "w_up", "w_down")):
        sp.dma_start(w[:, s], t[name][bass.ds(e, 1)].rearrange("o (k p) n -> p (o k) n", p=P)).then_inc(w_in[s], 16)


class Rsqrt:

    def __init__(self, pool, sb, name, widths):
        self.pool, self.row = pool, {w: k for k, w in enumerate(widths)}
        self.c = sb(name + "_consts", [P, len(widths) + 2])
        self.ms = sb(name + "_mean", [P, 1])
        for w, k in self.row.items():
            pool.memset(self.c[:, k:k + 1], 1.0 / w)
        pool.memset(self.c[:, -2:-1], NORM_EPS)
        pool.memset(self.c[:, -1:], -0.5)
        pool.drain()

    def __call__(self, out, total, width):
        k = self.row[width]
        self.pool.tensor_tensor(self.ms[:], total, self.c[:, k:k + 1], ALU.mult)
        self.pool.drain()
        self.pool.tensor_tensor(self.ms[:], self.ms[:], self.c[:, -2:-1], ALU.add)
        self.pool.drain()
        return self.pool.tensor_tensor(out, self.ms[:], self.c[:, -1:], ALU.pow)


def phase_out(nc, t, ident, logits):
    with ExitStack() as ctx:
        sb = lambda n, s, d=F32: ctx.enter_context(nc.sbuf_tensor(n, s, d))
        sem = lambda n: t["semctx"].enter_context(nc.semaphore(n))
        w_sb = sb("d_w_out", [P, KD, D]); wr = sb("d_w_router", [P, KD, GROUPS + EXPERTS]); gain = sb("d_gain", [P, D])
        mix = [sb(f"d_mix{s}", [P, D]) for s in range(2)]; x = [sb(f"d_x{s}", [P, D]) for s in range(2)]
        mixT = sb("d_mixT", [P, KD, P]); h2T = sb("d_h2T", [P, KD, P])
        h2 = [sb(f"d_h2{s}", [P, D]) for s in range(2)]; x1 = [sb(f"d_x1{s}", [P, D]) for s in range(2)]
        zeros = sb("d_zeros", [P, D]); ss = sb("d_ss", [P, 2]); rstd = sb("d_rstd", [P, 2])
        ps = lambda n, s: ctx.enter_context(nc.psum_tensor(n, s, F32))
        p_mT = ps("pd_mixT", [P, 2, BANK]); p_o = ps("pd_out", [P, 2, BANK]); p_hT = ps("pd_h2T", [P, 2, BANK]); p_l = ps("pd_logits", [P, BANK])

        s_w = [sem(f"D_w_out{h}") for h in range(2)]; s_par = sem("D_params")
        mix_in = [sem(f"D_mix_in{s}") for s in range(2)]; x_in = [sem(f"D_x_in{s}") for s in range(2)]
        mT_psum = sem("D_mixT_psum"); mT_a = sem("D_mixT_lo"); mT_d = sem("D_mixT_hi"); out_done = sem("D_out")
        x1_half = [sem(f"D_x1_half{h}") for h in range(2)]; x1_done = sem("D_x1"); ss_done = sem("D_ss"); rstd_done = sem("D_rstd"); h2_done = sem("D_h2"); h2_out = sem("D_h2_store"); x1_out = sem("D_x1_store"); zeroed = sem("D_zeros"); z_out = sem("D_zero_blocks")
        hT_psum = sem("D_h2T_psum"); hT_a = sem("D_h2T_lo"); hT_d = sem("D_h2T_hi"); lg_psum = sem("D_logits_psum"); lg_sb = sem("D_logits")
        passed = sem("D_passed")
        block = ctx.enter_context(nc.Block())

        @block.sync
        def _(sp):
            def load(i, s):
                sp.dma_start(mix[s][:], t["mix"][bass.ds(i * P, P), :]).then_inc(mix_in[s], 16)
                sp.dma_start(x[s][:], t["x"][bass.ds(i * P, P), :]).then_inc(x_in[s], 16)
            load(0, 0)
            for h in range(2):
                sp.dma_start(w_sb[:, :, h * BANK:(h + 1) * BANK],
                             t["w_out"][:, h * BANK:(h + 1) * BANK].rearrange("(k p) n -> p k n", p=P)).then_inc(s_w[h], 16)
            load(1, 1)
            sp.dma_start(gain[:], t["moe_norm_g"].partition_broadcast(P)).then_inc(s_par, 16)
            with nc.allow_non_contiguous_dma(reason="144 KB of router weights, once"):
                sp.dma_start(wr[:, :, 0:GROUPS], t["w_group"].rearrange("(k p) g -> p k g", p=P)).then_inc(s_par, 16)
                for g in range(GROUPS):
                    a = GROUPS + g * PER_GROUP
                    sp.dma_start(wr[:, :, a:a + PER_GROUP], t["w_expert_router"][g].rearrange("(k p) e -> p k e", p=P)).then_inc(s_par, 16)

            def step(i, s):
                sp.dma_start(t["y"][bass.ds(i * 2 * P + BLOCKS // 2 * P, 2 * P), :].rearrange("(b p) n -> p b n", p=P),
                             zeros[:].unsqueeze(1).broadcast_to([P, 2, D])).then_inc(z_out, 16)
                sp.wait_ge(x1_done, i + 1)
                sp.dma_start(t["x1"][bass.ds(i * P, P), :], x1[s][:]).then_inc(x1_out, 16)
                sp.wait_ge(h2_done, i + 1)
                sp.dma_start(t["h2"][bass.ds(i * P, P), :], h2[s][:]).then_inc(h2_out, 16)
                if known(i) is None or i < TILES - 2:
                    load(i + 2, s)
            sp.wait_ge(zeroed, 1)
            first_pairs_last(sp, TILES, step)
            sp.wait_ge(z_out, 16 * TILES)
            sp.wait_ge(h2_out, 16 * TILES)
            sp.wait_ge(x1_out, 16 * TILES)

        @block.gpsimd
        def _(pool):
            pool.memset(zeros[:], 0.0).then_inc(zeroed, 1)
            rsqrt = Rsqrt(pool, sb, "d_rsqrt", (D,))

            def step(i, s):
                pool.wait_ge(ss_done, i + 1)
                pool.sem_inc(passed, 1)
                rsqrt(rstd[:, s:s + 1], ss[:, s:s + 1], D).then_inc(rstd_done, 1)
            first_pairs_last(pool, TILES, step)

        @block.scalar
        def _(act):
            def copy_mT(i):
                act.wait_ge(mT_psum, i + 1)
                nc.scalar.copy(mixT[:, 0:4, :], p_mT[:, 0, :].rearrange("p (k n) -> p k n", k=4)).then_inc(mT_a, 1)

            def copy_hT(i):
                act.wait_ge(hT_psum, i + 1)
                nc.scalar.copy(h2T[:, 0:4, :], p_hT[:, 0, :].rearrange("p (k n) -> p k n", k=4)).then_inc(hT_a, 1)
            copy_mT(0)

            def step(i, s):
                if known(i) != 0:
                    copy_hT(i - 1)
                if known(i) != TILES - 1:
                    copy_mT(i + 1)
                act.wait_ge(x1_done, i + 1)
                if known(i) is None or i >= 2:
                    act.wait_ge(h2_out, i * 16 - 16)
                    act.wait_ge(hT_psum, i - 1)
                nc.scalar.activation(h2[s][:], x1[s][:], ACT.Square, accum_out=ss[:, s:s + 1]).then_inc(ss_done, 1)
            first_pairs_last(act, TILES, step)
            copy_hT(TILES - 1)

        @block.vector
        def _(dve):
            def copy_mT(i):
                dve.wait_ge(mT_psum, i + 1)
                nc.vector.tensor_copy(mixT[:, 4:8, :], p_mT[:, 1, :].rearrange("p (k n) -> p k n", k=4)).then_inc(mT_d, 1)

            def copy_hT(i):
                dve.wait_ge(hT_psum, i + 1)
                nc.vector.tensor_copy(h2T[:, 4:8, :], p_hT[:, 1, :].rearrange("p (k n) -> p k n", k=4)).then_inc(hT_d, 1)

            def copy_logits(i):
                dve.wait_ge(lg_psum, i + 1)
                nc.vector.tensor_copy(logits[:, bass.ds(i, 1), :], p_l[:, 0:GROUPS + EXPERTS].unsqueeze(1)).then_inc(lg_sb, 1)
            copy_mT(0)
            dve.wait_ge(s_par, 16 * (2 + GROUPS))

            def step(i, s):
                if known(i) != 0:
                    copy_hT(i - 1)
                dve.wait_ge(x_in[s], 8 * (i + 2 - s))
                if known(i) is None or i >= 2:
                    dve.wait_ge(x1_out, i * 16 - 16)
                for h in range(2):
                    dve.wait_ge(out_done, i * 2 + (h + 1))
                    half = slice(h * BANK, (h + 1) * BANK)
                    nc.vector.tensor_tensor(x1[s][:, half], p_o[:, h, :], x[s][:, half], ALU.add).then_inc(x1_half[h], 1)
                dve.wait_ge(x1_half[1], i + 1)
                dve.sem_inc(x1_done, 1)
                if known(i) != TILES - 1:
                    copy_mT(i + 1)
                if known(i) != 0:
                    copy_logits(i - 1)
                dve.wait_ge(rstd_done, i + 1)
                nc.vector.scalar_tensor_tensor(h2[s][:], x1[s][:], rstd[:, s:s + 1], gain[:], ALU.mult, ALU.mult).then_inc(h2_done, 1)
            first_pairs_last(dve, TILES, step)
            copy_hT(TILES - 1)
            copy_logits(TILES - 1)

        @block.tensor
        def _(pe):
            def mix_transposes(i, s):
                pe.wait_ge(mix_in[s], 8 * (i + 2 - s))
                for k in range(KD):
                    last = nc.tensor.transpose(p_mT[:, k // 4, (k % 4) * P:(k % 4 + 1) * P], mix[s][:, k * P:(k + 1) * P], ident[:])
                last.then_inc(mT_psum, 1)

            def h2_transposes(i, s):
                pe.wait_ge(h2_done, i + 1)
                for k in range(KD):
                    last = nc.tensor.transpose(p_hT[:, k // 4, (k % 4) * P:(k % 4 + 1) * P], h2[s][:, k * P:(k + 1) * P], ident[:])
                last.then_inc(hT_psum, 1)

            def route(i):
                pe.wait_ge(hT_a, i + 1)
                pe.wait_ge(hT_d, i + 1)
                pe.wait_ge(lg_sb, i)
                for k in range(KD):
                    last = nc.tensor.matmul(p_l[:, 0:GROUPS + EXPERTS], h2T[:, k, :], wr[:, k, :], start=(k == 0), stop=(k == KD - 1))
                last.then_inc(lg_psum, 1)
            mix_transposes(0, 0)
            pe.wait_ge(s_par, 16 * (2 + GROUPS))

            def step(i, s):
                pe.wait_ge(mT_a, i + 1)
                pe.wait_ge(mT_d, i + 1)
                for h in range(2):
                    pe.wait_ge(s_w[h], 16)
                    if known(i) != 0:
                        pe.wait_ge(x1_half[h], i)
                    for k in range(KD):
                        last = nc.tensor.matmul(p_o[:, h, :], mixT[:, k, :], w_sb[:, k, h * BANK:(h + 1) * BANK],
                                                start=(k == 0), stop=(k == KD - 1))
                    last.then_inc(out_done, 1)
                    if h == 0 and known(i) != 0:
                        h2_transposes(i - 1, 1 - s)
                if known(i) != TILES - 1:
                    mix_transposes(i + 1, 1 - s)
                if known(i) != 0:
                    route(i - 1)
            first_pairs_last(pe, TILES, step)
            h2_transposes(TILES - 1, (TILES - 1) % 2)
            route(TILES - 1)


def phase_route(nc, t, logits, wts, dest, ids, tab, ends, weights, w_in):
    with ExitStack() as ctx:
        sb = lambda n, s, d=F32: ctx.enter_context(nc.sbuf_tensor(n, s, d))
        sem = lambda n: t["semctx"].enter_context(nc.semaphore(n))
        E = EXPERTS
        g8 = sb("r_group_logits", [P, TILES, 8]); gmax = sb("r_group_max", [P, TILES, 8]); gidx = sb("r_group_idx", [P, TILES, 8], U32)
        gsel = sb("r_group", [P, TILES]); goh = sb("r_group_onehot", [P, TILES, GROUPS]); goff = sb("r_group_off", [P, TILES, GROUPS])
        iota_i = sb("r_iota_i", [P, BLOCKS], I32); iota = sb("r_iota", [P, BLOCKS])
        gex = sb("r_group_exp", [P, TILES, GROUPS]); gsum = sb("r_group_sum", [P, TILES])
        em = sb("r_masked", [P, TILES, E]); emax = sb("r_top", [P, TILES, 8]); eidx = sb("r_top_idx", [P, TILES, 8], U32)
        esel = sb("r_experts", [P, TILES, 2]); diff = sb("r_diff", [P, TILES]); den = sb("r_den", [P, TILES])
        oh = [sb(f"r_onehot{k}", [P, TILES, E]) for k in range(2)]; both = sb("r_both", [P, TILES, E])
        before = sb("r_before", [P, P]); ones = sb("r_ones", [P, P])
        pos = sb("r_pos", [P, TILES, E]); base = sb("r_base", [P, TILES + 1, E])
        nb_i = sb("r_nblocks_i", [P, E], I32); nb = sb("r_nblocks", [P, E]); bend = sb("r_block_end", [P, E]); pstart = sb("r_row_start", [P, E])
        dest_f = sb("r_dest_f", [P, 2, TILES]); lo = sb("r_dest_lo", [P, 2, TILES], U32); hi = sb("r_dest_hi", [P, 2, TILES], U32)
        cell = sb("r_cell", [P, 2, TILES], U32); half = sb("r_half", [1, 4], I32)
        tok = sb("r_tokens", [P, TILES], U32); zero = sb("r_zero", [P, BLOCKS], U32)
        past = sb("r_past", [1, BLOCKS, E]); be = sb("r_block_expert", [1, BLOCKS]); be_i = sb("r_block_expert_i", [1, BLOCKS], I32)
        ps_r = ctx.enter_context(nc.psum_tensor("pr_rank", [P, BANK], F32)); ps_t = ctx.enter_context(nc.psum_tensor("pr_total", [P, BANK], F32))
        s_c = sem("R_consts"); s_gm = sem("R_group_max"); s_ge = sem("R_group_exp"); s_d = sem("R_diff"); s_de = sem("R_diff_exp")
        s_oh = sem("R_onehots"); s_rk = sem("R_ranks"); s_cell = sem("R_cells"); s_z = sem("R_ids_zero"); s_sc = sem("R_ids_scatter"); s_ids = sem("R_ids")
        block = ctx.enter_context(nc.Block())

        @block.sync
        def _(sp):
            for e in range(SLOTS):
                load_expert(sp, t, weights, e, e, w_in)

        @block.gpsimd
        def _(pool):
            pool.memset(zero[:], 0)
            pool.drain()
            pool.dma_start(t["ids"].rearrange("(p b) o -> p (b o)", p=P), zero[:]).then_inc(s_z, 16)
            pool.iota(iota_i[:], [[1, BLOCKS]], base=0, channel_multiplier=0)
            pool.iota(tok[:], [[P, TILES]], base=0, channel_multiplier=1)
            pool.memset(ones[:], 1.0)
            pool.memset(before[:], 1.0)
            pool.drain()
            pool.affine_select(out=before[:], in_=before[:], compare_op=ALU.is_gt, fill=0.0, base=0,
                               pattern=[[1, P]], channel_multiplier=-1)
            pool.drain()
            pool.sem_inc(s_c, 1)
            pool.wait_ge(s_z, 16)
            pool.wait_ge(s_cell, 1)
            for k in range(2):
                for i in range(TILES):
                    pool.indirect_dma_start(t["ids"], bass.IndirectOffsetOnAxis(ap=cell[:, k, i:i + 1], axis=0),
                                            tok[:, i:i + 1], None).then_inc(s_sc, 16)
            pool.wait_ge(s_sc, 16 * 2 * TILES)
            pool.memset(ids[:, BLOCKS:BLOCKS + 1], 0)
            pool.dma_start(ids[:, 0:BLOCKS], t["ids"].rearrange("(p b) o -> p (b o)", p=P)).then_inc(s_ids, 16)
            pool.wait_ge(s_ids, 16)

        @block.scalar
        def _(act):
            act.wait_ge(s_gm, 1)
            nc.scalar.activation(gex[:], gex[:], ACT.Exp).then_inc(s_ge, 1)
            act.wait_ge(s_d, 1)
            nc.scalar.activation(diff[:], diff[:], ACT.Exp).then_inc(s_de, 1)

        @block.tensor
        def _(pe):
            pe.wait_ge(s_c, 1)
            pe.wait_ge(s_oh, 1)
            flat = both[:].rearrange("p t e -> p (t e)")
            nc.tensor.matmul(ps_t[:], ones[:], flat, start=True, stop=True)
            nc.tensor.matmul(ps_r[:], before[:], flat, start=True, stop=True).then_inc(s_rk, 1)

        @block.vector
        def _(dve):
            v = nc.vector
            tt = lambda o, a, b, op: v.tensor_tensor(o, a, b, op)
            v.memset(g8[:], LOW)
            dve.wait_ge(s_c, 1)
            dve.drain()
            v.tensor_copy(g8[:, :, 0:GROUPS], logits[:, :, 0:GROUPS])
            v.tensor_copy(iota[:], iota_i[:])
            dve.drain()
            for i in range(TILES):
                v.max(gmax[:, i, :], g8[:, i, :])
            dve.drain()
            for i in range(TILES):
                v.max_index(gidx[:, i, :], gmax[:, i, :], g8[:, i, :])
            s4 = [P, TILES, GROUPS]
            tt(gex[:], logits[:, :, 0:GROUPS], gmax[:, :, 0:1].broadcast_to(s4), ALU.subtract).then_inc(s_gm, 1)
            dve.drain()
            v.tensor_copy(gsel[:].unsqueeze(2), gidx[:, :, 0:1])
            dve.drain()
            tt(goh[:], gsel[:].unsqueeze(2).broadcast_to(s4), iota[:, 0:GROUPS].unsqueeze(1).broadcast_to(s4), ALU.is_equal)
            dve.drain()
            v.tensor_scalar(goff[:], goh[:], 1.0, -LOW, ALU.subtract, ALU.mult)
            for g in range(GROUPS):
                a = GROUPS + g * PER_GROUP
                tt(em[:, :, g * PER_GROUP:(g + 1) * PER_GROUP], logits[:, :, a:a + PER_GROUP],
                   goh[:, :, g:g + 1].broadcast_to([P, TILES, PER_GROUP]), ALU.mult)
            dve.drain()
            for g in range(GROUPS):
                part = em[:, :, g * PER_GROUP:(g + 1) * PER_GROUP]
                tt(part, part, goff[:, :, g:g + 1].broadcast_to([P, TILES, PER_GROUP]), ALU.add)
            dve.drain()
            for i in range(TILES):
                v.max(emax[:, i, :], em[:, i, :])
            dve.drain()
            for i in range(TILES):
                v.max_index(eidx[:, i, :], emax[:, i, :], em[:, i, :])
            tt(diff[:].unsqueeze(2), emax[:, :, 1:2], emax[:, :, 0:1], ALU.subtract).then_inc(s_d, 1)
            dve.drain()
            v.tensor_copy(esel[:], eidx[:, :, 0:2])
            dve.drain()
            sE = [P, TILES, E]
            for k in range(2):
                tt(oh[k][:], esel[:, :, k:k + 1].broadcast_to(sE), iota[:, 0:E].unsqueeze(1).broadcast_to(sE), ALU.is_equal)
            dve.drain()
            tt(both[:], oh[0][:], oh[1][:], ALU.add).then_inc(s_oh, 1)
            dve.wait_ge(s_ge, 1)
            v.tensor_reduce(gsum[:], gex[:], AX.X, ALU.add)
            dve.wait_ge(s_de, 1)
            dve.drain()
            v.scalar_tensor_tensor(den[:], diff[:], 1.0, gsum[:], ALU.add, ALU.mult)
            dve.drain()
            v.reciprocal(wts[:, :, 0], den[:])
            dve.drain()
            tt(wts[:, :, 1], wts[:, :, 0], diff[:], ALU.mult)
            v.memset(base[:, 0, :], 0.0)
            dve.wait_ge(s_rk, 1)
            dve.drain()
            for i in range(TILES):
                tt(base[:, i + 1, :], base[:, i, :], ps_t[:, i * E:(i + 1) * E], ALU.add)
                dve.drain()
            v.tensor_copy(nb_i[:], base[:, TILES, :])
            dve.drain()
            v.tensor_scalar(nb_i[:], nb_i[:], P - 1, None, ALU.add)
            dve.drain()
            v.tensor_scalar(nb_i[:], nb_i[:], 7, None, ALU.arith_shift_right)
            dve.drain()
            v.tensor_copy(nb[:], nb_i[:])
            dve.drain()
            v.tensor_tensor_scan(bend[:], ones[:, 0:E], nb[:], 0.0, ALU.mult, ALU.add)
            dve.drain()
            v.tensor_scalar(past[:, 0, :], bend[0:1, :], 1.0, None, ALU.add)
            tt(pstart[:], bend[:], nb[:], ALU.subtract)
            dve.drain()
            v.tensor_copy(ends[0:1, 0:EXPERTS], past[:, 0, :])
            v.tensor_scalar(pstart[:], pstart[:], float(P), None, ALU.mult)
            tt(pos[:], base[:, 0:TILES, :], ps_r[:].rearrange("p (t e) -> p t e", e=E), ALU.add)
            dve.drain()
            tt(pos[:], pos[:], pstart[:].unsqueeze(1).broadcast_to(sE), ALU.add)
            dve.drain()
            for k in range(2):
                tt(oh[k][:], oh[k][:], pos[:], ALU.mult)
            dve.drain()
            for k in range(2):
                v.tensor_reduce(dest_f[:, k, :], oh[k][:], AX.X, ALU.add)
            dve.drain()
            v.tensor_copy(dest[:], dest_f[:])
            dve.drain()
            v.tensor_scalar(lo[:], dest[:], P - 1, 6, ALU.bitwise_and, ALU.logical_shift_left)
            v.tensor_scalar(hi[:], dest[:], 7, None, ALU.logical_shift_right)
            dve.drain()
            tt(cell[:], lo[:], hi[:], ALU.bitwise_or).then_inc(s_cell, 1)
            for s in range(4):
                v.tensor_scalar(half[:, s:s + 1], ends[0:1, EXPERTS - 1:EXPERTS], (0, -1, 2, 1)[s], None, ALU.add)
            dve.drain()
            v.tensor_scalar(half[:], half[:], 1, 4, ALU.arith_shift_right, ALU.logical_shift_left)
            dve.drain()
            v.tensor_copy(ends[0:1, EXPERTS:EXPERTS + 4], half[:])
            sB = [1, BLOCKS, E]
            tt(past[:], bend[0:1, :].unsqueeze(1).broadcast_to(sB), iota[0:1, :].unsqueeze(2).broadcast_to(sB), ALU.is_le)
            dve.drain()
            v.tensor_reduce(be[:], past[:], AX.X, ALU.add)
            dve.drain()
            v.tensor_scalar(be[:], be[:], float(E - 1), None, ALU.min)
            dve.drain()
            v.tensor_copy(be_i[:], be[:])
            dve.drain()
            for s in range(SLOTS):
                v.tensor_scalar(tab[:, 1 + s, :], be_i[:], SLOTS - s, None, ALU.add)
            v.tensor_scalar(tab[:, 0, :], be_i[:], 43, None, ALU.mult)
            dve.drain()
            v.tensor_scalar(tab[:, 1:, :], tab[:, 1:, :], 43, None, ALU.mult)
            v.tensor_scalar(tab[:, 0, :], tab[:, 0, :], 7, None, ALU.arith_shift_right)
            dve.drain()
            v.tensor_scalar(tab[:, 1:, :], tab[:, 1:, :], 7, None, ALU.arith_shift_right)
            v.scalar_tensor_tensor(tab[:, 0, :], tab[:, 0, :], -SLOTS, be_i[:], ALU.mult, ALU.add)
            dve.drain()
            v.tensor_scalar(tab[:, 1:, :], tab[:, 1:, :], 1, 3 * 16, ALU.max, ALU.mult)
            dve.drain()


def phase_experts(nc, t, ident, ids, tab, ends, weights, s_w, w_plg):
    with ExitStack() as ctx:
        sb = lambda n, s, d=F32: ctx.enter_context(nc.sbuf_tensor(n, s, d))
        sem = lambda n: t["semctx"].enter_context(nc.semaphore(n))
        wg, wu, wd = weights
        idx = [sb(f"e_idx{s}", [P, 1], U32) for s in range(2)]
        x = [sb(f"e_x{s}", [P, D]) for s in range(2)]; xT = sb("e_xT", [P, KD, P])
        sg = sb("e_silu", [P, DX]); h = sb("e_h", [P, DX]); hT = sb("e_hT", [P, KX, P]); y = [sb(f"e_y{s}", [P, D]) for s in range(2)]
        ps = lambda n, s: ctx.enter_context(nc.psum_tensor(n, s, F32))
        p_xT = ps("pe_xT", [P, 2, BANK]); p_g = ps("pe_gate", [P, BANK]); p_u = ps("pe_up", [P, BANK])
        p_hT = ps("pe_hT", [P, BANK]); p_y = ps("pe_y", [P, 2, BANK])

        s_plg = sem("E_w_pl_gate"); ended = sem("E_blocks_ended")
        x_in = [sem(f"E_x_in{s}") for s in range(2)]; xT_psum = sem("E_xT_psum"); xT_a = sem("E_xT_lo"); xT_d = sem("E_xT_hi")
        g_done = sem("E_gate"); u_done = sem("E_up"); silu_done = sem("E_silu"); h_done = sem("E_h")
        hT_psum = sem("E_hT_psum"); hT_sb = sem("E_hT"); y_psum = sem("E_y_psum"); y_half = [sem(f"E_y_half{k}") for k in range(2)]
        y_out = [sem(f"E_y_store{s}") for s in range(2)]; idx_ready = sem("E_idx"); passed = sem("E_passed"); passed_pe = sem("E_passed_pe")
        block = ctx.enter_context(nc.Block())

        @block.sync
        def _(sp):
            def load(e, s):
                sp.wait_ge(ended, sp.value_load(ends[0:1, bass.ds(e - SLOTS, 1)], min_val=1, max_val=BLOCKS))
                load_expert(sp, t, weights, e, s, s_w)
            with sp.Fori(1, EXPERTS // SLOTS) as j:
                for s in range(SLOTS):
                    load(j * SLOTS + s, s)
            for e in range(EXPERTS // SLOTS * SLOTS, EXPERTS):
                load(e, e % SLOTS)
            sp.dma_start(w_plg[:], t["w_pl_gate"].rearrange("(k p) n -> p k n", p=P)).then_inc(s_plg, 16)
            for s in range(SLOTS):
                sp.wait_ge(s_w[s], 3 * 16 * len(range(s, EXPERTS, SLOTS)))
            sp.wait_ge(s_plg, 16)

        def steps(eng, body):
            last = eng.value_load(ends[0:1, EXPERTS - 1:EXPERTS], min_val=BLOCKS // 2 + 1, max_val=BLOCKS)
            for i in range(4):
                body(i, i % 2)
            with eng.Fori(2, BLOCKS // 4) as j:
                body(j * 2, 0)
                body(j * 2 + 1, 1)
            with eng.Fori(BLOCKS // 4, BLOCKS // 2) as j:
                for s in range(2):
                    with eng.If(last > j * 2 + s):
                        body(j * 2 + s, s)

        @block.gpsimd
        def _(pool):
            def gather(i, s):
                if known(i) is None or i >= 2:
                    pool.wait_ge(xT_psum, i - 1)
                pool.sem_inc(passed, 1)
                pool.tensor_copy(idx[s][:], ids[:, bass.ds(i, 1)]).then_inc(idx_ready, 1)
                pool.wait_ge(idx_ready, i + 1)
                pool.sem_inc(passed, 1)
                pool.indirect_dma_start(x[s][:], None, t["h2"], bass.IndirectOffsetOnAxis(ap=idx[s][:], axis=0)).then_inc(x_in[s], 16)
            gather(0, 0)

            def step(i, s):
                gather(i + 1, 1 - s)
            steps(pool, step)
            counts = [pool.value_load(ends[0:1, EXPERTS + k:EXPERTS + k + 1], min_val=16, max_val=8 * BLOCKS + 16) for k in range(4)]
            for s in range(2):
                pool.wait_ge(y_out[s], counts[s])
                pool.sem_inc(passed, 1)
                pool.wait_ge(x_in[s], counts[2 + s])
                pool.sem_inc(passed, 1)

        def store_free(eng, i, s):
            if known(i) is None or i >= 2:
                eng.wait_ge(y_out[s], 8 * (i - s))

        @block.scalar
        def _(act):
            def copy_xT(i):
                act.wait_ge(xT_psum, i + 1)
                nc.scalar.copy(xT[:, 0:4, :], p_xT[:, 0, :].rearrange("p (k n) -> p k n", k=4)).then_inc(xT_a, 1)
            copy_xT(0)

            def step(i, s):
                act.wait_ge(g_done, i + 1)
                act.wait_ge(h_done, i)
                nc.scalar.activation(sg[:], p_g[:], ACT.Silu).then_inc(silu_done, 1)
                copy_xT(i + 1)
                if known(i) != 0:
                    copy_y(i - 1, 1 - s)
                    for k in range(2):
                        act.wait_ge(y_half[k], i)
                    act.dma_start(t["y"][bass.ds((i - 1) * P, P), :], y[1 - s][:]).then_inc(y_out[1 - s], 16)

            def copy_y(i, s):
                act.wait_ge(y_psum, i + 1)
                store_free(act, i, s)
                nc.scalar.copy(y[s][:, 0:BANK], p_y[:, 0, :]).then_inc(y_half[0], 1)
            steps(act, step)

        @block.vector
        def _(dve):
            def copy_xT(i):
                dve.wait_ge(xT_psum, i + 1)
                nc.vector.tensor_copy(xT[:, 4:8, :], p_xT[:, 1, :].rearrange("p (k n) -> p k n", k=4)).then_inc(xT_d, 1)

            def copy_hT(i):
                dve.wait_ge(hT_psum, i + 1)
                nc.vector.tensor_copy(hT[:], p_hT[:].rearrange("p (k n) -> p k n", k=KX)).then_inc(hT_sb, 1)

            def copy_y(i, s):
                dve.wait_ge(y_psum, i + 1)
                dve.sem_inc(ended, 1)
                store_free(dve, i, s)
                nc.vector.tensor_copy(y[s][:, BANK:D], p_y[:, 1, :]).then_inc(y_half[1], 1)
            dve.sem_inc(ended, 1)
            copy_xT(0)

            def step(i, s):
                if known(i) != 0:
                    copy_hT(i - 1)
                dve.wait_ge(silu_done, i + 1)
                dve.wait_ge(u_done, i + 1)
                dve.wait_ge(hT_psum, i)
                nc.vector.tensor_tensor(h[:], sg[:], p_u[:], ALU.mult).then_inc(h_done, 1)
                copy_xT(i + 1)
                if known(i) != 0:
                    copy_y(i - 1, 1 - s)
            steps(dve, step)

        @block.tensor
        def _(pe):
            def x_transposes(i, s):
                pe.wait_ge(x_in[s], 8 * (i + 2 - s))
                pe.wait_ge(xT_a, i)
                pe.wait_ge(xT_d, i)
                for k in range(KD):
                    last = nc.tensor.transpose(p_xT[:, k // 4, (k % 4) * P:(k % 4 + 1) * P], x[s][:, k * P:(k + 1) * P], ident[:])
                last.then_inc(xT_psum, 1)

            def h_transposes(i):
                pe.wait_ge(h_done, i + 1)
                pe.wait_ge(hT_sb, i)
                for k in range(KX):
                    last = nc.tensor.transpose(p_hT[:, k * P:(k + 1) * P], h[:, k * P:(k + 1) * P], ident[:])
                last.then_inc(hT_psum, 1)

            def slot_of(i):
                return pe.value_load(tab[0:1, 0, bass.ds(i, 1)], min_val=0, max_val=SLOTS - 1)

            def gate_up(i, s):
                slot = slot_of(i)
                loads = [pe.value_load(tab[0:1, 1 + k, bass.ds(i, 1)], min_val=48, max_val=48 * EXPERTS) for k in range(SLOTS)]
                for k in range(SLOTS):
                    pe.wait_ge(s_w[k], loads[k])
                    pe.sem_inc(passed_pe, 1)
                pe.wait_ge(xT_a, i + 1)
                pe.wait_ge(xT_d, i + 1)
                pe.wait_ge(silu_done, i)
                for w, bank, done in ((wg, p_g, g_done), (wu, p_u, u_done)):
                    if done is u_done:
                        pe.wait_ge(h_done, i)
                    for k in range(KD):
                        last = nc.tensor.matmul(bank[:], xT[:, k, :], w[:, bass.ds(slot, 1), k, :].rearrange("p o n -> p (o n)"),
                                                start=(k == 0), stop=(k == KD - 1))
                    last.then_inc(done, 1)

            def down(i):
                slot = slot_of(i)
                pe.wait_ge(hT_sb, i + 1)
                for half in range(2):
                    pe.wait_ge(y_half[half], i)
                    for k in range(KX):
                        last = nc.tensor.matmul(p_y[:, half, :], hT[:, k, :],
                                                wd[:, bass.ds(slot, 1), k, half * BANK:(half + 1) * BANK].rearrange("p o n -> p (o n)"),
                                                start=(k == 0), stop=(k == KX - 1))
                last.then_inc(y_psum, 1)
            x_transposes(0, 0)

            def step(i, s):
                if known(i) != 0:
                    h_transposes(i - 1)
                gate_up(i, s)
                x_transposes(i + 1, 1 - s)
                if known(i) != 0:
                    down(i - 1)
            steps(pe, step)


def phase_final(nc, t, ident, wq, wts, dest):
    with ExitStack() as ctx:
        sb = lambda n, s, d=F32: ctx.enter_context(nc.sbuf_tensor(n, s, d))
        sem = lambda n: t["semctx"].enter_context(nc.semaphore(n))
        wp = sb("f_w_pl", [P, PL // P, D]); g_gain = sb("f_gate_gain", [P, D]); p_gain = sb("f_pl_gain", [P, D])
        idx = [[sb(f"f_idx{s}{k}", [P, 1], U32) for k in range(2)] for s in range(2)]
        y = [[sb(f"f_y{s}{k}", [P, D]) for k in range(2)] for s in range(2)]
        pe_in = [sb(f"f_p{s}", [P, PL]) for s in range(2)]; pT = [sb(f"f_pT{s}", [P, PL // P, P]) for s in range(2)]
        x1 = [sb(f"f_x1{s}", [P, D]) for s in range(2)]; x2 = [sb(f"f_x2{s}", [P, D]) for s in range(2)]; hg = sb("f_hg", [P, D]); hgT = sb("f_hgT", [P, KD, P])
        junk = sb("f_junk", [P, D]); junk2 = sb("f_junk2", [P, D]); gate = sb("f_gate", [P, D]); pl = sb("f_pl", [P, D]); out = [sb(f"f_out{s}", [P, D]) for s in range(2)]
        ss = sb("f_ss", [P, 2]); rstd = sb("f_rstd", [P, 2]); pss = sb("f_pl_ss", [P, 2]); prstd = sb("f_pl_rstd", [P, 2])
        ps = lambda n, s: ctx.enter_context(nc.psum_tensor(n, s, F32))
        p_hT = ps("pf_hgT", [P, 2, BANK]); p_g = ps("pf_gate", [P, 2, BANK]); p_pT = ps("pf_pT", [P, BANK]); p_pl = ps("pf_pl", [P, 2, BANK])

        x1_in = [sem(f"F_x1_in{s}") for s in range(2)]; s_wp = sem("F_w_pl"); s_par = sem("F_gains"); p_in = [sem(f"F_p_in{s}") for s in range(2)]
        y_in = [sem(f"F_y_in{s}") for s in range(2)]; part = sem("F_x2_part"); x2_done = sem("F_x2"); ss_done = sem("F_ss"); rstd_done = sem("F_rstd"); hg_done = sem("F_hg")
        hT_psum = sem("F_hgT_psum"); hT_a = sem("F_hgT_lo"); hT_d = sem("F_hgT_hi"); pT_psum = sem("F_pT_psum"); pT_sb = sem("F_pT")
        g_psum = sem("F_gate_psum"); gate_done = sem("F_gate"); pl_psum = sem("F_pl_psum"); pss_done = sem("F_pl_ss"); prstd_done = sem("F_pl_rstd")
        pl_read = sem("F_pl_read"); out_done = sem("F_out_ready"); stored = [sem(f"F_store{s}") for s in range(2)]; idx_ready = sem("F_idx"); passed = sem("F_passed")
        block = ctx.enter_context(nc.Block())

        @block.sync
        def _(sp):
            def load_p(i, s):
                sp.dma_start(pe_in[s][:], t["p"][bass.ds(i * P, P), :]).then_inc(p_in[s], 16)

            def load_x1(i, s):
                sp.dma_start(x1[s][:], t["x1"][bass.ds(i * P, P), :]).then_inc(x1_in[s], 16)
            load_x1(0, 0)
            load_p(0, 0)
            load_x1(1, 1)
            load_p(1, 1)
            sp.dma_start(g_gain[:], t["pl_gate_norm_g"].partition_broadcast(P)).then_inc(s_par, 16)
            sp.dma_start(wp[:], t["w_pl"].rearrange("(k p) n -> p k n", p=P)).then_inc(s_wp, 16)
            sp.dma_start(p_gain[:], t["pl_norm_g"].partition_broadcast(P)).then_inc(s_par, 16)

            def step(i, s):
                if known(i) is None or i < TILES - 2:
                    sp.wait_ge(pT_psum, i + 1)
                    load_p(i + 2, s)
                    sp.wait_ge(x2_done, i + 1)
                    load_x1(i + 2, s)
                sp.wait_ge(out_done, i + 1)
                sp.dma_start(t["out"][bass.ds(i * P, P), :], out[s][:]).then_inc(stored[s], 16)
            first_pairs_last(sp, TILES, step)
            for s in range(2):
                sp.wait_ge(stored[s], 16 * (TILES // 2))

        @block.gpsimd
        def _(pool):
            rsqrt = Rsqrt(pool, sb, "f_rsqrt", (D,))

            def gather(i, s):
                if known(i) is None or i >= 2:
                    pool.wait_ge(x2_done, i - 1)
                pool.sem_inc(passed, 1)
                for k in range(2):
                    pool.tensor_copy(idx[s][k][:], dest[:, k, bass.ds(i, 1)]).then_inc(idx_ready, 1)
                pool.wait_ge(idx_ready, i * 2 + 2)
                pool.sem_inc(passed, 1)
                for k in range(2):
                    pool.indirect_dma_start(y[s][k][:], None, t["y"], bass.IndirectOffsetOnAxis(ap=idx[s][k][:], axis=0)).then_inc(y_in[s], 16)

            def norm(i, s):
                pool.wait_ge(ss_done, i + 1)
                pool.sem_inc(passed, 1)
                rsqrt(rstd[:, s:s + 1], ss[:, s:s + 1], D).then_inc(rstd_done, 1)

            def norm_pl(i, s):
                pool.wait_ge(pss_done, i + 1)
                pool.sem_inc(passed, 1)
                rsqrt(prstd[:, s:s + 1], pss[:, s:s + 1], D).then_inc(prstd_done, 1)
            gather(0, 0)
            gather(1, 1)
            norm(0, 0)

            def step(i, s, more=True):
                if more:
                    gather(i + 2, s)
                if known(i) != TILES - 1:
                    norm(i + 1, 1 - s)
                norm_pl(i, s)
            with pool.Fori(0, TILES // 2 - 1) as j:
                step(j * 2, 0)
                step(j * 2 + 1, 1)
            step(TILES - 2, 0, False)
            step(TILES - 1, 1, False)

        @block.scalar
        def _(act):
            def square(i, s):
                act.wait_ge(ss_done, i)
                act.wait_ge(x2_done, i + 1)
                nc.scalar.activation(junk[:], x2[s][:], ACT.Square, accum_out=ss[:, s:s + 1]).then_inc(ss_done, 1)

            def copies(i, s):
                act.wait_ge(hT_psum, i + 1)
                nc.scalar.copy(hgT[:, 0:4, :], p_hT[:, 0, :].rearrange("p (k n) -> p k n", k=4)).then_inc(hT_a, 1)
                act.wait_ge(pT_psum, i + 1)
                nc.scalar.copy(pT[s][:], p_pT[:, 0:PL].rearrange("p (k n) -> p k n", k=PL // P)).then_inc(pT_sb, 1)
            square(0, 0)
            copies(0, 0)

            def step(i, s):
                if known(i) != TILES - 1:
                    square(i + 1, 1 - s)
                act.wait_ge(g_psum, i + 1)
                act.wait_ge(out_done, i)
                nc.scalar.activation(gate[:].rearrange("p (a n) -> p a n", a=2), p_g[:], ACT.Sigmoid).then_inc(gate_done, 1)
                if known(i) != TILES - 1:
                    copies(i + 1, 1 - s)
                act.wait_ge(pl_psum, i + 1)
                act.wait_ge(pss_done, i)
                nc.scalar.activation(junk2[:].rearrange("p (a n) -> p a n", a=2), p_pl[:], ACT.Square,
                                     accum_out=pss[:, s:s + 1]).then_inc(pss_done, 1)
            first_pairs_last(act, TILES, step)

        @block.vector
        def _(dve):
            def combine(i, s):
                dve.wait_ge(y_in[s], 16 * (i + 2 - s))
                dve.wait_ge(x1_in[s], 8 * (i + 2 - s))
                if known(i) is None or i >= 2:
                    dve.wait_ge(out_done, i - 1)
                nc.vector.scalar_tensor_tensor(x2[s][:], y[s][0][:], wts[:, bass.ds(i, 1), 0], x1[s][:], ALU.mult, ALU.add)
                dve.drain()
                nc.vector.scalar_tensor_tensor(x2[s][:], y[s][1][:], wts[:, bass.ds(i, 1), 1], x2[s][:], ALU.mult, ALU.add).then_inc(x2_done, 1)

            def make_hg(i, s):
                dve.wait_ge(rstd_done, i + 1)
                dve.wait_ge(hT_psum, i)
                dve.wait_ge(x2_done, i + 1)
                nc.vector.scalar_tensor_tensor(hg[:], x2[s][:], rstd[:, s:s + 1], g_gain[:], ALU.mult, ALU.mult).then_inc(hg_done, 1)

            def copy_hT(i):
                dve.wait_ge(hT_psum, i + 1)
                nc.vector.tensor_copy(hgT[:, 4:8, :], p_hT[:, 1, :].rearrange("p (k n) -> p k n", k=4)).then_inc(hT_d, 1)
            dve.wait_ge(s_par, 32)
            combine(0, 0)
            make_hg(0, 0)
            copy_hT(0)

            def step(i, s):
                if known(i) != TILES - 1:
                    combine(i + 1, 1 - s)
                    make_hg(i + 1, 1 - s)
                    copy_hT(i + 1)
                dve.wait_ge(prstd_done, i + 1)
                nc.vector.scalar_tensor_tensor(pl[:].rearrange("p (a n) -> p a n", a=2), p_pl[:], prstd[:, s:s + 1],
                                               p_gain[:].rearrange("p (a n) -> p a n", a=2), ALU.mult, ALU.mult).then_inc(pl_read, 1)
                dve.wait_ge(gate_done, i + 1)
                dve.wait_ge(pl_read, i + 1)
                nc.vector.tensor_tensor(pl[:], pl[:], gate[:], ALU.mult)
                dve.drain()
                if known(i) is None or i >= 2:
                    dve.wait_ge(stored[s], 8 * (i - s))
                nc.vector.tensor_tensor(out[s][:], pl[:], x2[s][:], ALU.add).then_inc(out_done, 1)
            first_pairs_last(dve, TILES, step)

        @block.tensor
        def _(pe):
            def transposes(i, s):
                pe.wait_ge(hg_done, i + 1)
                for k in range(KD):
                    last = nc.tensor.transpose(p_hT[:, k // 4, (k % 4) * P:(k % 4 + 1) * P], hg[:, k * P:(k + 1) * P], ident[:])
                last.then_inc(hT_psum, 1)
                pe.wait_ge(p_in[s], 8 * (i + 2 - s))
                pe.wait_ge(pT_sb, i)
                for k in range(PL // P):
                    last = nc.tensor.transpose(p_pT[:, k * P:(k + 1) * P], pe_in[s][:, k * P:(k + 1) * P], ident[:])
                last.then_inc(pT_psum, 1)
            transposes(0, 0)

            def step(i, s):
                pe.wait_ge(hT_a, i + 1)
                pe.wait_ge(hT_d, i + 1)
                pe.wait_ge(gate_done, i)
                for h in range(2):
                    for k in range(KD):
                        last = nc.tensor.matmul(p_g[:, h, :], hgT[:, k, :], wq[:, k, h * BANK:(h + 1) * BANK], start=(k == 0), stop=(k == KD - 1))
                last.then_inc(g_psum, 1)
                if known(i) != TILES - 1:
                    transposes(i + 1, 1 - s)
                pe.wait_ge(s_wp, 16)
                pe.wait_ge(pT_sb, i + 1)
                pe.wait_ge(pl_read, i)
                for h in range(2):
                    for k in range(PL // P):
                        last = nc.tensor.matmul(p_pl[:, h, :], pT[s][:, k, :], wp[:, k, h * BANK:(h + 1) * BANK], start=(k == 0), stop=(k == PL // P - 1))
                last.then_inc(pl_psum, 1)
            first_pairs_last(pe, TILES, step)


def block_kernel(nc, a):
    with ExitStack() as ctx:
        sb = lambda n, s, d=F32: ctx.enter_context(nc.sbuf_tensor(n, s, d))
        dram = lambda n, s, d=F32: nc.dram_tensor(n, s, d).ap()
        t = {name: ap[0] for name, ap in a.items()}
        t["p"] = t["p"][0]
        t["semctx"] = ctx
        t["v"] = dram("s_v", [SEQ, RW]); t["qT"] = dram("s_qT", [SEQ, RW]); t["kT"] = dram("s_kT", [SEQ, RW])
        t["zr"] = dram("s_zr", [SEQ + 1, QKV]); t["lo"] = dram("s_lora", [3, SEQ, RW]); t["mix"] = dram("s_mix", [SEQ, D])
        t["x1"] = dram("s_x1", [SEQ, D]); t["h2"] = dram("s_h2", [SEQ, D]); t["y"] = dram("s_y", [BLOCKS * P, D]); t["ids"] = dram("s_ids", [BLOCKS * P, 1], U32)
        ident = sb("ident", [P, P])
        phase_constants(nc, t, ident)
        with ExitStack() as early:
            t["semctx"] = early
            spent = phase_project(nc, t, ident)
            t["semctx"] = ctx
            phase_attention(nc, t, ident, spent)
        phase_rwkv(nc, t, ident)
        wts = sb("expert_weights", [P, TILES, 2]); dest = sb("expert_rows", [P, 2, TILES], U32)
        ids = sb("row_tokens", [P, BLOCKS + 1], U32); tab = sb("block_table", [1, 1 + SLOTS, BLOCKS], I32); ends = sb("expert_ends", [1, EXPERTS + 4], I32)
        w_in = [ctx.enter_context(nc.semaphore(f"E_weights_in{s}")) for s in range(SLOTS)]
        w_plg = sb("w_pl_gate_sb", [P, KD, D])
        with ExitStack() as moe:
            msb = lambda n, s, d=F32: moe.enter_context(nc.sbuf_tensor(n, s, d))
            logits = msb("router_logits", [P, TILES, GROUPS + EXPERTS])
            phase_out(nc, t, ident, logits)
            weights = [msb("w_gate_sb", [P, SLOTS, KD, DX]), msb("w_up_sb", [P, SLOTS, KD, DX]), msb("w_down_sb", [P, SLOTS, KX, D])]
            phase_route(nc, t, logits, wts, dest, ids, tab, ends, weights, w_in)
            phase_experts(nc, t, ident, ids, tab, ends, weights, w_in, w_plg)
        phase_final(nc, t, ident, w_plg, wts, dest)


INPUTS = ["x", "p", "positions", "attn_norm_g", "w_in", "q_norm_g", "k_norm_g", "lambda_q1", "lambda_k1", "lambda_q2", "lambda_k2",
          "diff_out_g", "mu_rkv", "mu_wag", "w0", "w_lora_a", "w_lora_b", "a0", "a_lora_a", "a_lora_b", "g_lora_a", "g_lora_b",
          "k_k", "k_a", "r_k", "gn_w", "gn_b", "w_out", "moe_norm_g", "w_group", "w_expert_router", "w_gate", "w_up", "w_down",
          "w_pl", "pl_norm_g", "pl_gate_norm_g", "w_pl_gate"]


def kernel(**inputs):
    import numpy as _np
    import concourse.bacc as _bacc
    from concourse import mybir as _mybir
    from concourse.bass_utils import run_bass_kernel_spmd as _run

    nc = _bacc.Bacc("TRN2", target_bir_lowering=False, num_devices=1)
    arrays, aps = {}, {}
    for name in INPUTS:
        arr = _np.ascontiguousarray(inputs[name])
        arrays[f"in_{name}_dram"] = arr
        aps[name] = nc.dram_tensor(f"in_{name}_dram", arr.shape, _mybir.dt.from_np(arr.dtype), kind="ExternalInput").ap()
    aps["out"] = nc.dram_tensor("out_dram", (1, SEQ, D), F32, kind="ExternalOutput").ap()
    block_kernel(nc, aps)
    return _run(nc, [arrays], core_ids=[0]).results[0]["out_dram"]
```

```python
import math
from contextlib import ExitStack, nullcontext
import numpy as np
import concourse.bass as bass
from concourse import mybir

F32 = mybir.dt.float32
I32 = mybir.dt.int32
U32 = mybir.dt.uint32
ALU = mybir.AluOpType
ACT = mybir.ActivationFunctionType
AX = mybir.AxisListType

P = 128
SEQ, D = 2048, 1024
TILES = SEQ // P
KD = D // P
QKV = 1536
RW = 512
NORM_EPS = 1e-6
R_W, R_A, R_G = 64, 64, 160
R_ALL = R_W + R_A + R_G
DH = 64
ROPE_THETA = 10000.0
ROUND = 1.5 * 2.0 ** 23
TWO_PI = (6.28125, 1.9350051879882812e-03, 3.019916050561733e-07)
BANK = 512


def two_by_two(eng, n, body):
    body(0, 0, 0, False)
    body(1, 0, 1, False)
    with eng.Fori(1, n // 2 - 1) as j:
        body(j * 2, j, 0, False)
        body(j * 2 + 1, j, 1, False)
    body(n - 2, n // 2 - 1, 0, False)
    body(n - 1, n // 2 - 1, 1, True)


def phase_project(nc, t, ident):
    with ExitStack() as ctx:
        sb = lambda n, s, d=F32: ctx.enter_context(nc.sbuf_tensor(n, s, d))
        sems = []

        def sem(name):
            sems.append(t["semctx"].enter_context(nc.semaphore(name)))
            return sems[-1]
        w_sb = sb("w_in_sb", [P, KD, 2 * QKV])
        wl = sb("lora_in", [P, KD, 2, R_ALL])
        wab = sb("lora_out_wa", [P, RW])
        wg0 = sb("lora_out_g0", [P, RW])
        wg1 = sb("lora_out_g1", [R_G - P, RW])
        mu = sb("mu_cols", [P, 3, KD])
        gain = sb("attn_gain", [P, D])
        bias = sb("lora_bias", [P, 2, RW])
        x_sb = [sb(f"x_tile{s}", [P, D]) for s in range(2)]
        hn = [sb(f"hn_tile{s}", [P, D]) for s in range(2)]
        hT = [sb(f"hnT{s}", [P, KD, P + 1]) for s in range(2)]
        ss = sb("sumsq", [P, 2])
        rstd = sb("rstd", [P, 2])
        pw = sb("rsqrt_consts", [P, 4, 16])
        ms = sb("meansq", [P, 16])
        l1 = sb("lora_mid", [P, R_ALL])
        l1T = sb("lora_midT", [P, 3, P])
        qk = sb("qk_stage", [P, 2, BANK])
        stage = [qk[:, 0, :], qk[:, 1, :]] + [sb(f"z_stage{c}", [P, BANK])[:] for c in range(2, 9)]
        qk_g = sb("qk_gain", [P, 2, 8, DH])
        qn = sb("qk_normed", [P, 16, DH])
        by_cos = sb("qk_cos", [P, 16, DH])
        by_sin = sb("qk_sin", [P, 16, DH])
        qss = sb("qk_sumsq", [P, 16])
        qrs = sb("qk_rstd", [P, 16])
        qkT = sb("qkT_stage", [P, 8, P])
        cos_t = sb("cos_table", [P, TILES, DH // 2])
        sin_t = sb("sin_table", [P, TILES, DH // 2])
        pos_i = sb("positions_i", [P, TILES], I32)
        pos_f = sb("positions_f", [P, TILES])
        freq = sb("inv_freq", [P, DH // 2])
        turns = by_sin[:, 0:8, :].rearrange("p a b -> p (a b)").rearrange("p (t f) -> p t f", t=TILES)
        ang = by_cos[:, 0:8, :].rearrange("p a b -> p (a b)").rearrange("p (t f) -> p t f", t=TILES)
        half_pi = sb("half_pi", [P, 1])
        ps = lambda n, s: ctx.enter_context(nc.psum_tensor(n, s, F32))
        pT = ps("p_hT", [P, 2, BANK])
        pZ = ps("p_z", [P, 3, BANK])
        pL = ps("p_l1", [P, BANK])
        pLT = ps("p_l1T", [P, BANK])

        x_in = [sem(f"A_x_in{s}") for s in range(2)]
        w_in = [sem(f"A_w_in{c}") for c in range(6)]
        s_par = sem("A_params"); s_wl = sem("A_lora_w_in"); s_wl_rdy = sem("A_lora_scaled")
        s_const = sem("A_const")
        ss_done = sem("A_ss"); rstd_done = sem("A_rstd"); hn_done = sem("A_hn")
        hT_psum = sem("A_hT_psum"); hTa = sem("A_hT_lo"); hTd = sem("A_hT_hi")
        z_done = sem("A_z"); ev = [sem(f"A_evac{c}") for c in range(9)]
        staged = [sem(f"A_staged{c}") for c in range(9)]
        out_dma = [sem(f"A_out{c}") for c in range(9)]
        s_pos = sem("A_positions"); s_freq = sem("A_inv_freq"); s_ang = sem("A_angles"); s_trig = sem("A_trig")
        sq_done = sem("A_qk_sq"); qss_done = sem("A_qk_ss"); qrs_done = sem("A_qk_rstd"); rot_done = sem("A_rot")
        qkT_psum = sem("A_qkT_psum"); qkTa = sem("A_qT"); qkTd = sem("A_kT"); qT_out = sem("A_qT_out"); kT_out = sem("A_kT_out")
        l1_done = sem("A_l1"); l1_act = sem("A_l1_act"); l1T_psum = sem("A_l1T_psum"); l1T_sb = sem("A_l1T")
        block = ctx.enter_context(nc.Block())

        @block.sync
        def _(sp):
            for s in range(2):
                sp.dma_start(x_sb[s][:], t["x"][s * P:(s + 1) * P, :]).then_inc(x_in[s], 16)
            sp.dma_start(gain[:], t["attn_norm_g"].partition_broadcast(P)).then_inc(s_par, 16)
            with nc.allow_non_contiguous_dma(reason="8 KB of positions, once"):
                sp.dma_start(pos_i[:], t["positions"].rearrange("(t p) -> p t", p=P)).then_inc(s_pos, 16)
            with nc.allow_non_contiguous_dma(reason="12 KB of per-channel mixes, once"):
                for m in range(3):
                    sp.dma_start(mu[:, m, :], t["mu_wag"][m].rearrange("(k p) -> p k", p=P)).then_inc(s_wl, 16)
            for name, a, b in (("w_lora_a", 0, R_W), ("a_lora_a", R_W, R_W + R_A), ("g_lora_a", R_W + R_A, R_ALL)):
                sp.dma_start(wl[:, :, 0, a:b], t[name].rearrange("(k p) r -> p k r", p=P)).then_inc(s_wl, 16)
            sp.dma_start(wab[0:R_W, :], t["w_lora_b"]).then_inc(s_par, 16)
            sp.dma_start(wab[R_W:P, :], t["a_lora_b"]).then_inc(s_par, 16)
            sp.dma_start(wg0[:], t["g_lora_b"][0:P, :]).then_inc(s_par, 16)
            sp.dma_start(wg1[:], t["g_lora_b"][P:R_G, :]).then_inc(s_par, 16)
            sp.dma_start(bias[:, 0, :], t["w0"].partition_broadcast(P)).then_inc(s_par, 16)
            sp.dma_start(bias[:, 1, :], t["a0"].partition_broadcast(P)).then_inc(s_par, 16)
            for c in range(6):
                sp.dma_start(w_sb[:, :, c * BANK:(c + 1) * BANK],
                             t["w_in"][:, c * BANK:(c + 1) * BANK].rearrange("(k p) n -> p k n", p=P)).then_inc(w_in[c], 16)

            def tile(i, j, s, last, load):
                if load:
                    sp.wait_ge(hn_done, i + 1)
                    sp.dma_start(x_sb[s][:], t["x"][bass.ds(i * P + 2 * P, P), :]).then_inc(x_in[s], 16)
                for c in range(2, 9):
                    if c == 2:
                        dst = t["v"][bass.ds(i * P, P), :]
                    elif c < 6:
                        dst = t["zr"][bass.ds(i * P + 1, P), (c - 3) * BANK:(c - 2) * BANK]
                    else:
                        dst = t["lo"][c - 6, bass.ds(i * P, P), :]
                    sp.wait_ge(staged[c], i + 1)
                    sp.dma_start(dst, stage[c]).then_inc(out_dma[c], 16)
                for n, name, rdy, out in ((0, "qT", qkTa, qT_out), (4, "kT", qkTd, kT_out)):
                    sp.wait_ge(rdy, i + 1)
                    sp.dma_start(t[name][bass.ds(i * P, P), :], qkT[:, n:n + 4, :].rearrange("p h n -> p (h n)")).then_inc(out, 16)
            tile(0, 0, 0, False, True)
            tile(1, 0, 1, False, True)
            with sp.Fori(1, TILES // 2 - 1) as j:
                tile(j * 2, j, 0, False, True)
                tile(j * 2 + 1, j, 1, False, True)
            tile(TILES - 2, None, 0, False, False)
            tile(TILES - 1, None, 1, True, False)
            for c in range(2, 9):
                sp.wait_ge(out_dma[c], 16 * TILES)
            sp.wait_ge(qT_out, 16 * TILES)
            sp.wait_ge(kT_out, 16 * TILES)

        @block.gpsimd
        def _(pool):
            for n, v in enumerate((1.0 / D, 1.0 / DH, NORM_EPS, -0.5)):
                pool.memset(pw[:, n, :], v)
            for n in range(DH // 2):
                pool.memset(freq[:, n:n + 1], float(ROPE_THETA ** (np.float32(-n) / np.float32(DH // 2))))
            pool.memset(half_pi[:], math.pi / 2).then_inc(s_freq, 1)
            pool.memset(hT[1][:], 0.0).then_inc(s_const, 1)
            pool.drain()

            def rsqrt(out, sums, mean):
                n = out.shape[1]
                pool.tensor_tensor(ms[:, 0:n], sums, pw[:, mean, 0:n], ALU.mult)
                pool.drain()
                pool.tensor_tensor(ms[:, 0:n], ms[:, 0:n], pw[:, 2, 0:n], ALU.add)
                pool.drain()
                return pool.tensor_tensor(out, ms[:, 0:n], pw[:, 3, 0:n], ALU.pow)

            def head(i, s):
                pool.wait_ge(ss_done, i + 1)
                rsqrt(rstd[:, s:s + 1], ss[:, s:s + 1], 0).then_inc(rstd_done, 1)
            head(0, 0)

            def tile(i, j, s, last):
                if not last:
                    head(i + 1, 1 - s)
                pool.wait_ge(qss_done, i + 1)
                rsqrt(qrs[:], qss[:], 1).then_inc(qrs_done, 1)
            two_by_two(pool, TILES, tile)

        @block.scalar
        def _(act):
            def square(i, jj, s):
                act.wait_ge(x_in[s], 16 * jj + 16)
                nc.scalar.activation(hn[s][:], x_sb[s][:], ACT.Square, accum_out=ss[:, s:s + 1]).then_inc(ss_done, 1)

            def copy_hT(i, s):
                act.wait_ge(hT_psum, i + 1)
                nc.scalar.copy(hT[s][:, 0:4, 1:P + 1], pT[:, 0, :].rearrange("p (k n) -> p k n", k=4))
                nc.scalar.copy(hT[s][:, 0:4, 0:1], hT[1 - s][:, 0:4, P:P + 1]).then_inc(hTa, 1)

            for n, name in enumerate(("q_norm_g", "k_norm_g")):
                for g in range(8):
                    act.dma_start(qk_g[:, n, g, :], t[name].partition_broadcast(P)).then_inc(s_par, 16)
            act.wait_ge(s_const, 1)
            act.wait_ge(s_ang, 1)
            nc.scalar.activation(sin_t[:], ang, ACT.Sin)
            act.wait_ge(s_ang, 2)
            nc.scalar.activation(cos_t[:], turns, ACT.Sin, bias=half_pi[:], scale=-1.0).then_inc(s_trig, 1)
            square(0, 0, 0)
            copy_hT(0, 0)

            def tile(i, j, s, last):
                if not last:
                    square(i + 1, j + s, 1 - s)
                act.wait_ge(l1_done, i + 1)
                act.wait_ge(l1T_psum, i)
                nc.scalar.activation(l1[:, 0:R_W], pL[:, 0:R_W], ACT.Tanh)
                nc.scalar.copy(l1[:, R_W:P], pL[:, R_W:P])
                nc.scalar.activation(l1[:, P:R_ALL], pL[:, P:R_ALL], ACT.Sigmoid).then_inc(l1_act, 1)

                def evac(c):
                    act.wait_ge(z_done, 9 * i + (c + 1))
                    if c >= 2:
                        act.wait_ge(out_dma[c], 16 * i)
                    nc.scalar.copy(stage[c], pZ[:, c % 3, :]).then_inc(ev[c], 1)
                    if c >= 2:
                        act.wait_ge(ev[c], i + 1)
                        act.sem_inc(staged[c], 1)
                evac(0)
                evac(2)
                act.wait_ge(ev[0], i + 1)
                act.wait_ge(ev[1], i + 1)
                nc.scalar.activation(qn[:].rearrange("p g d -> p (g d)"), qk[:].rearrange("p a n -> p (a n)"),
                                     ACT.Square).then_inc(sq_done, 1)
                if not last:
                    copy_hT(i + 1, 1 - s)
                evac(4)
                for c in (6, 7):
                    act.wait_ge(ev[c], i + 1)
                    nc.scalar.activation(stage[c], stage[c], ACT.Sigmoid).then_inc(staged[c], 1)
                evac(8)
                act.wait_ge(qkT_psum, i + 1)
                act.wait_ge(qT_out, 16 * i)
                nc.scalar.copy(qkT[:, 0:4, :], pT[:, 0, :].rearrange("p (k n) -> p k n", k=4)).then_inc(qkTa, 1)
            two_by_two(act, TILES, tile)

        @block.vector
        def _(dve):
            dve.wait_ge(s_pos, 16)
            dve.wait_ge(s_freq, 1)
            nc.vector.tensor_copy(pos_f[:], pos_i[:])
            dve.drain()
            shape = [P, TILES, DH // 2]
            nc.vector.tensor_tensor(ang, pos_f[:].unsqueeze(2).broadcast_to(shape), freq[:].unsqueeze(1).broadcast_to(shape), ALU.mult)
            dve.drain()
            nc.vector.tensor_scalar(turns, ang, 1.0 / (2 * math.pi), ROUND, ALU.mult, ALU.add)
            dve.drain()
            nc.vector.tensor_scalar(turns, turns, ROUND, None, ALU.subtract)
            for part in TWO_PI:
                dve.drain()
                nc.vector.scalar_tensor_tensor(ang, turns, -part, ang, ALU.mult, ALU.add)
            dve.drain()
            nc.vector.tensor_scalar(ang, ang, math.pi, -math.pi, ALU.min, ALU.max).then_inc(s_ang, 1)
            dve.drain()
            nc.vector.scalar_tensor_tensor(turns, ang, -1.0, ang, ALU.mult, ALU.max).then_inc(s_ang, 1)
            dve.wait_ge(s_wl, 6 * 16)
            for k in range(KD):
                for m, (a, b) in enumerate(((0, R_W), (R_W, R_W + R_A), (R_W + R_A, R_ALL))):
                    nc.vector.tensor_scalar(wl[:, k, 1, a:b], wl[:, k, 0, a:b], mu[:, m, k:k + 1], None, ALU.mult)
            dve.drain()
            nc.vector.tensor_tensor(wl[:, :, 0, :], wl[:, :, 0, :], wl[:, :, 1, :], ALU.subtract).then_inc(s_wl_rdy, 1)
            dve.wait_ge(s_par, 23 * 16)
            dve.wait_ge(s_const, 1)
            dve.wait_ge(s_trig, 1)
            nc.vector.tensor_scalar(qk_g[:, 0, :, :], qk_g[:, 0, :, :], float(DH) ** -0.5, None, ALU.mult)
            dve.drain()

            def make_hn(i, jj, s):
                dve.wait_ge(x_in[s], 16 * jj + 16)
                dve.wait_ge(rstd_done, i + 1)
                nc.vector.scalar_tensor_tensor(hn[s][:], x_sb[s][:], rstd[:, s:s + 1], gain[:],
                                               ALU.mult, ALU.mult).then_inc(hn_done, 1)

            def copy_hT(i, s):
                dve.wait_ge(hT_psum, i + 1)
                nc.vector.tensor_copy(hT[s][:, 4:8, 1:P + 1], pT[:, 1, :].rearrange("p (k n) -> p k n", k=4))
                nc.vector.tensor_copy(hT[s][:, 4:8, 0:1], hT[1 - s][:, 4:8, P:P + 1]).then_inc(hTd, 1)
            make_hn(0, 0, 0)
            copy_hT(0, 0)

            def tile(i, j, s, last):
                if not last:
                    make_hn(i + 1, j + s, 1 - s)

                def evac(c):
                    dve.wait_ge(z_done, 9 * i + (c + 1))
                    if c >= 2:
                        dve.wait_ge(out_dma[c], 16 * i)
                    if c < 6:
                        nc.vector.tensor_copy(stage[c], pZ[:, c % 3, :]).then_inc(ev[c], 1)
                        if c >= 2:
                            dve.wait_ge(ev[c], i + 1)
                            dve.sem_inc(staged[c], 1)
                    else:
                        nc.vector.tensor_tensor(stage[c], pZ[:, c % 3, :], bias[:, c - 6, :], ALU.add).then_inc(ev[c], 1)
                evac(1)
                if not last:
                    copy_hT(i + 1, 1 - s)
                dve.wait_ge(l1T_psum, i + 1)
                nc.vector.tensor_copy(l1T[:, 0:2, :], pLT[:, 0:2 * P].rearrange("p (k n) -> p k n", k=2))
                nc.vector.tensor_copy(l1T[0:R_G - P, 2, :], pLT[0:R_G - P, 2 * P:3 * P]).then_inc(l1T_sb, 1)
                dve.wait_ge(sq_done, i + 1)
                nc.vector.tensor_reduce(qss[:], qn[:], AX.X, ALU.add).then_inc(qss_done, 1)
                evac(3)
                dve.wait_ge(qrs_done, i + 1)
                shape = [P, 16, DH]
                nc.vector.tensor_tensor(qn[:], qk[:].rearrange("p a (g d) -> p (a g) d", d=DH),
                                        qrs[:].unsqueeze(2).broadcast_to(shape), ALU.mult)
                dve.drain()
                nc.vector.tensor_tensor(qn[:], qn[:], qk_g[:].rearrange("p a g d -> p (a g) d"), ALU.mult)
                dve.drain()
                half = [P, 32, DH // 2]
                c_t = cos_t[:, bass.ds(i, 1), :].broadcast_to(half)
                s_t = sin_t[:, bass.ds(i, 1), :].broadcast_to(half)
                nc.vector.tensor_tensor(by_cos[:].rearrange("p g (h d) -> p (g h) d", h=2), qn[:].rearrange("p g (h d) -> p (g h) d", h=2), c_t, ALU.mult)
                nc.vector.tensor_tensor(by_sin[:].rearrange("p g (h d) -> p (g h) d", h=2), qn[:].rearrange("p g (h d) -> p (g h) d", h=2), s_t, ALU.mult)
                dve.drain()
                h = DH // 2
                nc.vector.tensor_tensor(qn[:, :, 0:h], by_cos[:, :, 0:h], by_sin[:, :, h:DH], ALU.subtract)
                nc.vector.tensor_tensor(qn[:, :, h:DH], by_cos[:, :, h:DH], by_sin[:, :, 0:h], ALU.add).then_inc(rot_done, 1)
                evac(5)
                evac(6)
                evac(7)
                dve.wait_ge(qkT_psum, i + 1)
                dve.wait_ge(kT_out, 16 * i)
                nc.vector.tensor_copy(qkT[:, 4:8, :], pT[:, 1, :].rearrange("p (k n) -> p k n", k=4)).then_inc(qkTd, 1)
            two_by_two(dve, TILES, tile)

        @block.tensor
        def _(pe):
            def transposes(i, s, first=1):
                pe.wait_ge(hn_done, i + 1)
                pe.wait_ge(qkTa, i - first)
                pe.wait_ge(qkTd, i - first)
                for k in range(KD):
                    last = nc.tensor.transpose(pT[:, k // 4, (k % 4) * P:(k % 4 + 1) * P], hn[s][:, k * P:(k + 1) * P], ident[:])
                last.then_inc(hT_psum, 1)
            transposes(0, 0, 0)
            pe.wait_ge(s_wl_rdy, 1)
            pe.wait_ge(s_par, 23 * 16)

            def tile(i, j, s, last_tile):
                pe.wait_ge(hTa, i + 1)
                pe.wait_ge(hTd, i + 1)
                pe.wait_ge(l1_act, i)
                for shifted in (0, 1):
                    for k in range(KD):
                        last = nc.tensor.matmul(pL[:, 0:R_ALL], hT[s][:, k, 1 - shifted:P + 1 - shifted], wl[:, k, shifted, :],
                                                start=(k == 0 and not shifted), stop=(k == KD - 1 and shifted == 1))
                last.then_inc(l1_done, 1)

                def free_bank(c):
                    if c < 3:
                        pe.wait_ge(ev[c + 6], i)
                    else:
                        pe.wait_ge(ev[c - 3], i + 1)

                def chunk(c):
                    pe.wait_ge(w_in[c], 16)
                    free_bank(c)
                    for k in range(KD):
                        last = nc.tensor.matmul(pZ[:, c % 3, :], hT[s][:, k, 1:P + 1], w_sb[:, k, c * BANK:(c + 1) * BANK],
                                                start=(k == 0), stop=(k == KD - 1))
                    last.then_inc(z_done, 1)
                for c in range(3):
                    chunk(c)
                if not last_tile:
                    transposes(i + 1, 1 - s)
                pe.wait_ge(l1_act, i + 1)
                pe.wait_ge(l1T_sb, i)
                nc.tensor.transpose(pLT[:, 0:P], l1[:, 0:P], ident[:])
                nc.tensor.transpose(pLT[:, P:2 * P], l1[:, P:2 * P], ident[:])
                nc.tensor.transpose(pLT[0:R_G - P, 2 * P:3 * P], l1[:, 2 * P:R_ALL], ident[:]).then_inc(l1T_psum, 1)
                for c in range(3, 6):
                    chunk(c)
                pe.wait_ge(l1T_sb, i + 1)
                free_bank(6)
                nc.tensor.matmul(pZ[:, 0, :], l1T[0:R_W, 0, :], wab[0:R_W, :], start=True, stop=True).then_inc(z_done, 1)
                free_bank(7)
                nc.tensor.matmul(pZ[:, 1, :], l1T[R_W:P, 0, :], wab[R_W:P, :], start=True, stop=True).then_inc(z_done, 1)
                free_bank(8)
                nc.tensor.matmul(pZ[:, 2, :], l1T[:, 1, :], wg0[:], start=True, stop=False)
                nc.tensor.matmul(pZ[:, 2, :], l1T[0:R_G - P, 2, :], wg1[:], start=False, stop=True).then_inc(z_done, 1)
                pe.wait_ge(rot_done, i + 1)
                if not last_tile:
                    pe.wait_ge(hTa, i + 2)
                    pe.wait_ge(hTd, i + 2)
                for g in range(8):
                    last = nc.tensor.transpose(pT[:, g // 4, (g % 4) * P:(g % 4 + 1) * P],
                                               qn[:, 2 * g:2 * g + 2, :].rearrange("p a d -> p (a d)"), ident[:])
                last.then_inc(qkT_psum, 1)
            two_by_two(pe, TILES, tile)
    return sems


def phase_constants(nc, t, ident):
    with ExitStack() as ctx:
        s_id = t["semctx"].enter_context(nc.semaphore("C_ident"))
        s_z = t["semctx"].enter_context(nc.semaphore("C_zero_row"))
        zero = ctx.enter_context(nc.sbuf_tensor("zero_row", [1, QKV], F32))
        block = ctx.enter_context(nc.Block())

        @block.gpsimd
        def _(pool):
            pool.memset(zero[:], 0.0)
            pool.memset(ident[:], 0.0)
            pool.drain()
            pool.affine_select(out=ident[:], in_=ident[:], compare_op=ALU.not_equal, fill=1.0, base=0,
                               pattern=[[-1, P]], channel_multiplier=1).then_inc(s_id, 1)
            pool.drain()
            pool.dma_start(t["zr"][0:1, :], zero[:]).then_inc(s_z, 16)
            pool.wait_ge(s_z, 16)
            pool.wait_ge(s_id, 1)


HEADS = 4
SUBLN_EPS = 1e-5
LAM_INIT = 0.8 - 0.6 * math.exp(0.0)
MASKED = -1e30


def phase_attention(nc, t, ident, spent=()):
    CH = [i // 4 + 1 for i in range(TILES)]
    W = [[min(BANK, (i + 1) * P - c * BANK) for c in range(CH[i])] for i in range(TILES)]
    C0 = [sum(CH[:i]) for i in range(TILES + 1)]
    NCH = C0[TILES]
    with ExitStack() as ctx:
        sb = lambda n, s, d=F32: ctx.enter_context(nc.sbuf_tensor(n, s, d))
        sem = lambda n: t["semctx"].enter_context(nc.semaphore(n))
        ps = lambda n, s: ctx.enter_context(nc.psum_tensor(n, s, F32))
        kT = sb("kT_all", [P, TILES, HEADS * P])
        v = sb("v_all", [P, TILES, HEADS * P])
        qz = [sb(f"q_maps{s}", [P, 2, P]) for s in range(2)]
        prob = [[sb(f"prob{s}{m}", [P, TILES * P]) for m in range(2)] for s in range(2)]
        aT = [sb(f"attnT{s}", [P, BANK]) for s in range(2)]
        o_st = [sb(f"o_stage{s}", [P, P]) for s in range(2)]
        sq_junk = sb("o_sq", [P, 2, P])
        mask = sb("causal_mask", [P, P])
        nmax = [sb(f"neg_max{s}", [P, 2, 4]) for s in range(2)]
        sums = [sb(f"prob_sums{s}", [P, 2, 4]) for s in range(2)]
        nrow = sb("neg_row_max", [P, 2])
        fac = sb("chunk_factor", [P, 2, 4])
        tmp = sb("stat_tmp", [P, 2, 4])
        den = sb("denominator", [P, 2])
        coef = sb("coef", [P, 2, 4])
        oss = sb("o_sumsq", [P, 2]); ors = sb("o_rstd", [P, 2]); oms = sb("o_ms", [P, 1])
        pw = sb("o_consts", [P, 3])
        lamv = sb("lam_sign", [P, 2])
        lp = sb("lam_params", [P, 4, DH]); lprod = sb("lam_prod", [P, 2, DH]); lsum = sb("lam_sum", [P, 2]); lexp = sb("lam_exp", [P, 2])
        og = sb("o_gain", [P, P])
        pS = ps("p_scores", [P, 4, BANK]); pT = ps("p_attnT", [P, 2, BANK]); pO = ps("p_o", [P, 2, BANK])

        kv_in = [sem(f"B_kv{n}") for n in range(4)]; par_in = sem("B_par"); q_in = [sem(f"B_q{s}") for s in range(2)]
        consts = sem("B_consts"); lam_s = sem("B_lam_sum"); lam_e = sem("B_lam_exp")
        s_done = sem("B_scores")
        max_done = sem("B_max"); exp_done = sem("B_exp")
        coef_done = sem("B_coef"); scaled = sem("B_scaled"); passed = sem("B_passed")
        d_done = sem("B_max_diff"); f_done = sem("B_factor")
        attn_done = sem("B_attn"); T_done = sem("B_attnT_psum"); Tc_done = sem("B_attnT")
        pv_done = sem("B_pv")
        oss_done = sem("B_oss"); ors_done = sem("B_ors"); o_done = sem("B_o")
        o_out = [sem(f"B_out{s}") for s in range(2)]
        block = ctx.enter_context(nc.Block())

        def load_kv(eng, n):
            rows = slice(n * 4 * P, (n + 1) * 4 * P)
            eng.dma_start(kT[:, 4 * n:4 * n + 4, :], t["kT"][rows, :].rearrange("(t p) n -> p t n", p=P)).then_inc(kv_in[n], 16)
            eng.dma_start(v[:, 4 * n:4 * n + 4, :], t["v"][rows, :].rearrange("(t p) n -> p t n", p=P)).then_inc(kv_in[n], 16)

        @block.sync
        def _(sp):
            load_kv(sp, 0)
            for k, name in enumerate(("lambda_q1", "lambda_k1", "lambda_q2", "lambda_k2")):
                sp.dma_start(lp[:, k, :], t[name].partition_broadcast(P)).then_inc(par_in, 16)
            sp.dma_start(og[:], t["diff_out_g"].partition_broadcast(P)).then_inc(par_in, 16)
            sp.wait_ge(consts, 1)
            for s in range(2):
                sp.sem_inc(o_out[s], 16)
            with sp.Fori(0, HEADS) as h:
                def load_q(i):
                    sp.wait_ge(s_done, h * (2 * NCH) + (2 * C0[TILES - 2 + i + 1] if i < 2 else 2 * NCH + 2 * C0[i - 1]))
                    for m in range(2):
                        r = slice(DH * m, DH * m + DH)
                        sp.dma_start(qz[i % 2][r, m, :], t["qT"][i * P + DH * m:i * P + DH * m + DH, bass.ds(h * P, P)]).then_inc(q_in[i % 2], 16)

                def store(i):
                    sp.wait_ge(o_done, h * TILES + (i + 3))
                    sp.dma_start(t["mix"][i * P:(i + 1) * P, bass.ds(h * P, P)], o_st[i % 2][:]).then_inc(o_out[i % 2], 16)
                load_q(0)
                load_q(1)
                for i in range(TILES):
                    if i + 2 < TILES:
                        load_q(i + 2)
                    if i >= 1:
                        store(i - 1)
                store(TILES - 1)
            for s in spent:
                sp.sem_clear(s)
            for s in range(2):
                sp.wait_ge(o_out[s], 16 * (HEADS * TILES // 2 + 1))

        @block.gpsimd
        def _(pool):
            pool.memset(qz[0][:], 0.0)
            pool.memset(qz[1][:], 0.0)
            pool.memset(lamv[:], 1.0)
            for n, c in enumerate((1.0 / P, SUBLN_EPS, -0.5)):
                pool.memset(pw[:, n:n + 1], c)
            pool.memset(mask[:], 0.0)
            pool.drain()
            pool.affine_select(out=mask[:], in_=mask[:], compare_op=ALU.is_ge, fill=MASKED, base=0,
                               pattern=[[-1, P]], channel_multiplier=1).then_inc(consts, 1)
            with pool.Fori(0, HEADS) as h:
                def rsqrt(i):
                    s = i % 2
                    pool.wait_ge(oss_done, h * TILES + i + 1)
                    pool.sem_inc(passed, 1)
                    pool.tensor_tensor(oms[:], oss[:, s:s + 1], pw[:, 0:1], ALU.mult)
                    pool.drain()
                    pool.tensor_tensor(oms[:], oms[:], pw[:, 1:2], ALU.add)
                    pool.drain()
                    pool.tensor_tensor(ors[:, s:s + 1], oms[:], pw[:, 2:3], ALU.pow).then_inc(ors_done, 1)
                    pool.drain()
                for i in range(TILES):
                    pool.wait_ge(coef_done, h * TILES + i + 1)
                    pool.sem_inc(passed, 1)
                    for c in range(CH[i]):
                        if c > 0:
                            p1 = prob[i % 2][1][:, c * BANK:c * BANK + W[i][c]]
                            pool.tensor_scalar(p1, p1, coef[:, 1, c:c + 1], None, ALU.mult).then_inc(scaled, 1)
                        if c == min(1, CH[i] - 1) and i >= 1:
                            rsqrt(i - 1)
                rsqrt(TILES - 1)

        @block.scalar
        def _(act):
            act.sem_inc(exp_done, 4)
            act.sem_inc(Tc_done, 2)
            act.wait_ge(lam_s, 1)
            nc.scalar.activation(lexp[:], lsum[:], ACT.Exp).then_inc(lam_e, 1)
            for n in range(1, 4):
                load_kv(act, n)
            with act.Fori(0, HEADS) as h:
                def exp(i, c, m):
                    n = 2 * (C0[i] + c) + m
                    act.wait_ge(max_done, h * (2 * NCH) + n + 1)
                    nc.scalar.activation(prob[i % 2][m][:, c * BANK:c * BANK + W[i][c]], pS[:, n % 4, 0:W[i][c]], ACT.Exp,
                                         bias=nmax[i % 2][:, m, c:c + 1], accum_out=sums[i % 2][:, m, c:c + 1]).then_inc(exp_done, 1)

                def square_o(i):
                    act.wait_ge(pv_done, h * NCH + (C0[i + 1] + 1))
                    nc.scalar.activation(sq_junk[:, i % 2, :], pO[:, i % 2, 0:P], ACT.Square, accum_out=oss[:, i % 2:i % 2 + 1]).then_inc(oss_done, 1)
                exp(0, 0, 0)
                exp(0, 0, 1)
                for i in range(TILES):
                    act.wait_ge(d_done, h * TILES + i + 1)
                    nc.scalar.activation(fac[:], tmp[:], ACT.Exp, scale=-1.0).then_inc(f_done, 1)
                    if i + 1 < TILES:
                        exp(i + 1, 0, 0)
                        exp(i + 1, 0, 1)
                    for c in range(CH[i]):
                        n = C0[i] + c
                        act.wait_ge(T_done, h * NCH + n + 1)
                        act.wait_ge(pv_done, h * NCH + n) if n > 0 else None
                        nc.scalar.copy(aT[n % 2][:, 0:W[i][c]], pT[:, n % 2, 0:W[i][c]]).then_inc(Tc_done, 1)
                        if c == 0 and i >= 1:
                            square_o(i - 1)
                        if i + 1 < TILES and c + 1 < CH[i + 1]:
                            exp(i + 1, c + 1, 0)
                            exp(i + 1, c + 1, 1)
                square_o(TILES - 1)

        @block.vector
        def _(dve):
            dve.sem_inc(o_done, 2)
            dve.wait_ge(par_in, 16 * 5)
            dve.wait_ge(consts, 1)
            nc.vector.tensor_tensor(lprod[:, 0, :], lp[:, 0, :], lp[:, 1, :], ALU.mult)
            nc.vector.tensor_tensor(lprod[:, 1, :], lp[:, 2, :], lp[:, 3, :], ALU.mult)
            nc.vector.tensor_scalar(og[:], og[:], 1.0 - LAM_INIT, None, ALU.mult)
            nc.vector.memset(nmax[0][:], 0.0)
            nc.vector.memset(nmax[1][:], 0.0)
            nc.vector.memset(tmp[:], 0.0)
            dve.drain()
            nc.vector.tensor_reduce(lsum[:], lprod[:], AX.X, ALU.add).then_inc(lam_s, 1)
            dve.wait_ge(lam_e, 1)
            nc.vector.tensor_tensor(lamv[:, 1:2], lexp[:, 1:2], lexp[:, 0:1], ALU.subtract)
            dve.drain()
            nc.vector.tensor_scalar(lamv[:, 1:2], lamv[:, 1:2], -LAM_INIT, None, ALU.add)
            dve.drain()
            with dve.Fori(0, HEADS) as h:
                def chunk_max(i, c, m):
                    n = 2 * (C0[i] + c) + m
                    dve.wait_ge(s_done, h * (2 * NCH) + 2 * NCH + n + 1)
                    nc.vector.tensor_reduce(nmax[i % 2][:, m, c:c + 1], pS[:, n % 4, 0:W[i][c]], AX.X, ALU.max, negate=True).then_inc(max_done, 1)

                def output(i):
                    dve.wait_ge(ors_done, h * TILES + i + 1)
                    dve.wait_ge(o_out[i % 2], h * (8 * 16) + (i // 2 + 1) * 16)
                    nc.vector.scalar_tensor_tensor(o_st[i % 2][:], pO[:, i % 2, 0:P], ors[:, i % 2:i % 2 + 1], og[:],
                                                   ALU.mult, ALU.mult).then_inc(o_done, 1)
                def coefficients(i):
                    k, s = CH[i], i % 2
                    three = [P, 2, k]
                    dve.wait_ge(exp_done, h * (2 * NCH) + (4 + 2 * C0[i + 1]))
                    nc.vector.tensor_reduce(nrow[:], nmax[s][:, :, 0:k], AX.X, ALU.min)
                    dve.drain()
                    nc.vector.tensor_tensor(tmp[:, :, 0:k], nmax[s][:, :, 0:k], nrow[:].unsqueeze(2).broadcast_to(three), ALU.subtract).then_inc(d_done, 1)
                    dve.wait_ge(f_done, h * TILES + i + 1)
                    nc.vector.tensor_tensor(coef[:, :, 0:k], fac[:, :, 0:k], sums[s][:, :, 0:k], ALU.mult)
                    dve.drain()
                    nc.vector.tensor_reduce(den[:], coef[:, :, 0:k], AX.X, ALU.add)
                    dve.drain()
                    nc.vector.reciprocal(den[:], den[:])
                    dve.drain()
                    nc.vector.tensor_tensor(den[:], den[:], lamv[:], ALU.mult)
                    dve.drain()
                    nc.vector.tensor_tensor(coef[:, :, 0:k], fac[:, :, 0:k], den[:].unsqueeze(2).broadcast_to(three), ALU.mult).then_inc(coef_done, 1)
                    dve.drain()

                def combine(i, c):
                    cols = slice(c * BANK, c * BANK + W[i][c])
                    p0, p1 = prob[i % 2][0][:, cols], prob[i % 2][1][:, cols]
                    if c == 0:
                        nc.vector.tensor_scalar(p1, p1, coef[:, 1, c:c + 1], None, ALU.mult)
                        dve.drain()
                    else:
                        dve.wait_ge(scaled, h * (NCH - TILES) + (C0[i] - i + c))
                    nc.vector.scalar_tensor_tensor(p0, p0, coef[:, 0, c:c + 1], p1, ALU.mult, ALU.add).then_inc(attn_done, 1)
                chunk_max(0, 0, 0)
                chunk_max(0, 0, 1)
                for i in range(TILES):
                    coefficients(i)
                    if i + 1 < TILES:
                        chunk_max(i + 1, 0, 0)
                    combine(i, 0)
                    if i + 1 < TILES:
                        chunk_max(i + 1, 0, 1)
                    for c in range(CH[i]):
                        if c > 0:
                            combine(i, c)
                        if i + 1 < TILES and c + 1 < CH[i + 1]:
                            chunk_max(i + 1, c + 1, 0)
                            chunk_max(i + 1, c + 1, 1)
                        if c == min(1, CH[i] - 1) and i >= 1:
                            output(i - 1)
                output(TILES - 1)

        @block.tensor
        def _(pe):
            pe.sem_inc(s_done, 2 * NCH)
            pe.wait_ge(consts, 1)
            pe.sem_inc(pv_done, 1)
            with pe.Fori(0, HEADS) as h:
                def scores(i, c, m):
                    n = 2 * (C0[i] + c) + m
                    if c == 0 and m == 0:
                        pe.wait_ge(q_in[i % 2], h * (8 * 32) + (i // 2 + 1) * 32)
                        pe.wait_ge(kv_in[i // 4], 32)
                    pe.wait_ge(exp_done, h * (2 * NCH) + n + 1)
                    tiles = W[i][c] // P
                    diag = c == CH[i] - 1
                    last = nc.tensor.matmul(pS[:, n % 4, 0:W[i][c]], qz[i % 2][:, m, :], kT[:, 4 * c:4 * c + tiles, bass.ds(h * P, P)],
                                            start=True, stop=not diag)
                    if diag:
                        last = nc.tensor.matmul(pS[:, n % 4, W[i][c] - P:W[i][c]], ident[:], mask[:], start=False, stop=True)
                    last.then_inc(s_done, 1)

                def turn(i, c):
                    n = C0[i] + c
                    pe.wait_ge(attn_done, h * NCH + n + 1)
                    pe.wait_ge(Tc_done, h * NCH + n + 1)
                    for b in range(W[i][c] // P):
                        last = nc.tensor.transpose(pT[:, n % 2, b * P:(b + 1) * P], prob[i % 2][0][:, c * BANK + b * P:c * BANK + (b + 1) * P], ident[:])
                    last.then_inc(T_done, 1)

                def values(i, c):
                    n = C0[i] + c
                    if c == 0:
                        pe.wait_ge(o_done, h * TILES + i + 1)
                    pe.wait_ge(Tc_done, h * NCH + n + 3)
                    for b in range(W[i][c] // P):
                        kb = 4 * c + b
                        last = nc.tensor.matmul(pO[:, i % 2, 0:P], aT[n % 2][:, b * P:(b + 1) * P], v[:, kb, bass.ds(h * P, P)],
                                                start=(kb == 0), stop=(kb == i))
                    last.then_inc(pv_done, 1)
                for i in range(-1, TILES):
                    if i + 1 < TILES:
                        scores(i + 1, 0, 0)
                        scores(i + 1, 0, 1)
                    if i >= 1:
                        values(i - 1, CH[i - 1] - 1)
                    for c in range(CH[i] if i >= 0 else 0):
                        if i + 1 < TILES and c + 1 < CH[i + 1]:
                            scores(i + 1, c + 1, 0)
                            scores(i + 1, c + 1, 1)
                        turn(i, c)
                        if c > 0:
                            values(i, c - 1)
                values(TILES - 1, CH[TILES - 1] - 1)


HV = 8
CK = 64
DECAY = math.exp(-0.5)
GN_EPS = 64e-5
LEVELS = (1, 2, 4, 8, 16, 32)


class Events:

    def __init__(self, sem, names):
        self.sem, self.at = sem, {n: k + 1 for k, n in enumerate(names)}
        assert len(self.at) == len(names)
        self.n, self.seen = len(names), 0

    def value(self, name, step):
        return self.nth(self.at[name], step)

    def nth(self, k, step):
        return step * self.n + (self.n + k)

    def in_order(self, name):
        assert self.at[name] == self.seen % self.n + 1, (name, self.seen % self.n)
        self.seen += 1


AB = "ab"
PE_JOBS = (["cum", "G3a", "G3b", "G1_0", "G1_1", "Tr0a", "G1_2", "G1_3", "Tr0b", "G2_0", "G2_1", "X1a", "X1b", "Wa", "Wb",
            "TX1a", "G2_2", "TX1b", "G2_3", "Tr1a", "MN0", "Tr1b", "MN1", "X2a", "RT", "X2b", "Y0", "TX2a", "S0", "TX2b",
            "Tr2a", "S1", "Tr2b", "X3a", "Ya", "X3b", "Yb", "TX3a", "Da", "TX3b", "Db", "Tr3a", "Tr3b", "pc", "X4a", "X4b", "TX4a", "TX4b",
            "Tr4a", "T0", "Tr4b", "T1", "X5a", "T2", "X5b", "T3", "TX5a", "TX5b", "Tr5a", "Tr5b"])
PREP_JOBS = ("cum", "pc", "T0", "T1", "T2", "T3")
TAIL = ("Wa", "Wb", "MN0", "MN1", "RT", "Y0", "S0", "S1", "Ya", "Yb", "sqy", "s1", "yc", "s2", "yn", "ysum", "rsy", "out")
PREP = PREP_JOBS + ("P", "cumsb", "Pex", "sqk", "vcopy", "kp", "ssk", "kkn", "Ah", "Bh", "bon", "T_init", "rkv", "kk0", "rsk", "ex", "b", "Kh", "Rh", "rk", "bv")
ACT_EV = ["P", "cumsb", "Tr0a", "Tr0b", "X1a", "X1b", "Wa", "Wb", "sqk", "Tr1a", "Tr1b", "Pex", "X2a", "X2b", "Y0", "Tr2a", "Tr2b",
          "X3a", "X3b", "Da", "Db", "Tr3a", "Tr3b", "sqy", "pc", "X4a", "X4b", "vcopy", "Tr4a", "T0", "Tr4b", "T1", "X5a", "T2", "X5b", "T3", "Tr5a", "Tr5b"]
DVE_EV = ["G3a", "G3b", "G1_0", "G1_1", "G1_2", "G1_3", "G2_0", "G2_1", "TX1a", "G2_2", "TX1b", "G2_3", "kp", "ssk", "MN0", "MN1", "kkn", "RT", "TX2a", "S0", "TX2b",
          "S1", "Ya", "Yb", "s1", "yc", "TX3a", "TX3b", "Ah", "Bh", "s2", "TX4a", "TX4b", "bon", "yn", "TX5a", "TX5b"]
POOL_EV = ["rkv", "kk0", "rsk", "ex", "b", "Kh", "Rh", "rk", "T_init", "rsy", "bv", "out"]
MAIN_JOBS = [n for n in PE_JOBS if n not in PREP_JOBS]
BANKS = 6
FIRST_OF = (0, 4, 1, 5)


def phase_rwkv(nc, t, ident):
    with ExitStack() as ctx:
        sb = lambda n, s, d=F32: ctx.enter_context(nc.sbuf_tensor(n, s, d))
        sem = lambda n: t["semctx"].enter_context(nc.semaphore(n))
        two = lambda n, s, d=F32: [sb(f"{n}{k}", s, d) for k in range(2)]
        assert len(MAIN_JOBS) % BANKS == 0
        z = two("c_z", [P, 3 * RW]); rkv = two("c_rkv", [P, 3 * RW])
        sig = two("c_sig", [P, RW]); a = two("c_a", [P, RW]); g = two("c_g", [P, RW])
        mu = sb("c_mu", [P, 3 * RW]); k_k = sb("c_kk", [P, RW]); k_a = sb("c_ka", [P, RW]); r_k = sb("c_rk", [P, RW])
        gn_w = sb("c_gnw", [P, RW]); gn_b = sb("c_gnb", [P, RW])
        Pt = sb("c_P", [P, RW]); iP = sb("c_invP", [P, RW]); cumsb = sb("c_cum", [P, RW]); Pex = sb("c_Pex", [P, RW])
        kk0 = sb("c_kk0", [P, RW]); sq = sb("c_sq", [P, RW]); kp = sb("c_kp", [P, RW]); kkn = sb("c_kkn", [P, RW]); bb = sb("c_b", [P, RW])
        rk = sb("c_rkp", [P, RW]); bon = sb("c_bon", [P, HV]); ssk = sb("c_ssk", [P, HV]); rsk = sb("c_rsk", [P, HV])
        AD = two("c_AD", [P, 2, HV, DH])
        Bh = two("c_Bh", [P, RW]); Kh = two("c_Kh", [P, RW]); Rh = sb("c_Rh", [P, RW]); V = two("c_V", [P, RW]); bv = two("c_bv", [P, RW])
        cT = two("c_cT", [P, 4, 4, P])
        pc = two("c_pc", [P, 4, 2])
        AR1 = two("c_AR1", [P, HV, 2, P]); AR2 = two("c_AR2", [P, HV, 2, P])
        T = two("c_T", [P, HV, CK]); TB = two("c_TB", [P, HV, P])
        TT = two("c_TT", [P, HV, P]); X = sb("c_X", [P, HV, CK])
        WU = sb("c_WU", [P, HV, 2, DH]); RpT = sb("c_RpT", [P, 4, P]); Y0 = sb("c_Y0", [P, RW])
        MT = sb("c_MT", [P, 2, 4, DH]); NN = sb("c_NN", [P, 2, 4, DH]); St = sb("c_Stmp", [P, 4, DH])
        S = [two(f"c_S{k}", [P, 4, DH]) for k in range(2)]
        y = sb("c_y", [P, RW]); s1 = sb("c_s1", [P, HV]); s2 = sb("c_s2", [P, HV]); rsy = sb("c_rsy", [P, HV]); yo = sb("c_yo", [P, RW])
        cst = sb("c_consts", [P, 4, HV]); tiny = sb("c_tiny", [P, HV])
        maskG = sb("c_maskG", [P, 2, P]); i64 = sb("c_i64", [P, CK]); ind = sb("c_ind", [P, 2])
        lv = sb("c_levels", [P, len(LEVELS), CK], I32); bits = sb("c_bits", [P, 3, CK], I32)
        ps = ctx.enter_context(nc.psum_tensor("p_ring", [P, 8, BANK], F32))

        z_in = [sem(f"C_z_in{k}") for k in range(2)]; g_in = [sem(f"C_g_in{k}") for k in range(2)]; par = sem("C_params"); o_out = sem("C_out")
        cs_p = sem("C_masks"); passed = sem("C_passed")
        PE = Events(sem("C_pe"), PE_JOBS); AC = Events(sem("C_act"), ACT_EV)
        DV = Events(sem("C_dve"), DVE_EV); PO = Events(sem("C_pool"), POOL_EV)
        block = ctx.enter_context(nc.Block())

        def bank(name):
            return ps[:, MAIN_JOBS.index(name) % BANKS, :] if name in MAIN_JOBS else ps[:, BANKS + PREP_JOBS.index(name) % 2, :]

        def owner(name):
            ev = {"cum": "cumsb"}.get(name, name)
            return (AC, ev) if ev in AC.at else (DV, ev)

        def steps(eng, body):
            body(-1, 1, {"prep"}, None)
            body(0, 0, {"main", "prep"}, None)
            with eng.Fori(0, (TILES - 2) // 2) as j:
                body(j * 2 + 1, 1, {"main", "tail", "prep"}, j)
                body(j * 2 + 2, 0, {"main", "tail", "prep"}, j)
            body(TILES - 1, 1, {"main", "tail"}, None)
            body(TILES, 0, {"tail"}, None)

        def nth(tile, j, ahead):
            return tile // 2 if isinstance(tile, int) else j + ahead

        def group(name):
            return "tail" if name in TAIL else "prep" if name in PREP else "main"

        def heads(ap):
            return ap.rearrange("p (h d) -> p h d", d=DH)

        @block.sync
        def _(sp):
            sp.dma_start(mu[:], t["mu_rkv"].rearrange("m n -> (m n)").partition_broadcast(P)).then_inc(par, 16)
            for dst, name in ((k_k, "k_k"), (k_a, "k_a"), (r_k, "r_k"), (gn_w, "gn_w"), (gn_b, "gn_b")):
                src = t[name].rearrange("h n -> (h n)") if name == "r_k" else t[name]
                sp.dma_start(dst[:], src.partition_broadcast(P)).then_inc(par, 16)

            def load(i, s):
                sp.dma_start(z[s][:], t["zr"][bass.ds(i * P + 1, P), :]).then_inc(z_in[s], 16)
                sp.dma_start(rkv[s][:], t["zr"][bass.ds(i * P, P), :]).then_inc(z_in[s], 16)
                sp.dma_start(sig[s][:], t["lo"][0, bass.ds(i * P, P), :]).then_inc(z_in[s], 16)
                sp.dma_start(a[s][:], t["lo"][1, bass.ds(i * P, P), :]).then_inc(z_in[s], 16)
            load(0, 0)
            load(1, 1)
            sp.sem_inc(o_out, 16)
            sp.dma_start(g[0][:], t["lo"][2, 0:P, :]).then_inc(g_in[0], 16)
            sp.dma_start(g[1][:], t["lo"][2, P:2 * P, :]).then_inc(g_in[1], 16)

            def step(i, s, what, j):
                if "tail" in what:
                    sp.wait_ge(PO.sem, PO.value("out", i))
                    sp.dma_start(t["mix"][bass.ds((i - 1) * P, P), RW:2 * RW], yo[:]).then_inc(o_out, 16)
                    if "prep" in what:
                        sp.dma_start(g[1 - s][:], t["lo"][2, bass.ds((i + 1) * P, P), :]).then_inc(g_in[1 - s], 16)
            def reload(i, s):
                sp.wait_ge(PO.sem, PO.value("bv", i - 1))
                sp.wait_ge(DV.sem, DV.value("bon", i - 1))
                sp.wait_ge(AC.sem, AC.value("vcopy", i - 1))
                load(i + 2, s)
            reload(0, 0)
            reload(1, 1)
            with sp.Fori(0, (TILES - 2) // 2 - 1) as j:
                step(j * 2 + 1, 1, {"main", "tail", "prep"}, j)
                reload(j * 2 + 2, 0)
                step(j * 2 + 2, 0, {"main", "tail", "prep"}, j)
                reload(j * 2 + 3, 1)
            step(TILES - 3, 1, {"main", "tail", "prep"}, None)
            step(TILES - 2, 0, {"main", "tail", "prep"}, None)
            step(TILES - 1, 1, {"main", "tail"}, None)
            step(TILES, 0, {"tail"}, None)
            sp.wait_ge(o_out, 16 * (TILES + 1))

        @block.gpsimd
        def _(pool):
            for n, c in enumerate((1.0 / DH, GN_EPS, -0.5)):
                pool.memset(cst[:, n, :], c)
            pool.memset(maskG[:], 1.0)
            pool.memset(ind[:], 0.0)
            pool.memset(i64[:], 0.0)
            for k in range(2):
                pool.memset(S[k][0][:], 0.0)
            pool.iota(bits[:, 0, :], pattern=[[0, CK]], base=0, channel_multiplier=1)
            pool.iota(bits[:, 1, :], pattern=[[1, CK]], base=0, channel_multiplier=0)
            pool.drain()
            for c in range(2):
                r = slice(c * CK, c * CK + CK)
                pool.memset(ind[r, c:c + 1], 1.0)
                pool.memset(maskG[r, :, (1 - c) * CK:(1 - c) * CK + CK], 0.0)
                pool.affine_select(out=i64[r, :], in_=i64[r, :], compare_op=ALU.not_equal, fill=1.0, base=0,
                                   pattern=[[-1, CK]], channel_multiplier=1)
            pool.drain()
            for kind in range(2):
                pool.affine_select(out=maskG[:, kind, :], in_=maskG[:, kind, :], compare_op=ALU.is_ge, fill=0.0,
                                   base=kind - 1, pattern=[[1, P]], channel_multiplier=-1)
            pool.drain()
            pool.tensor_copy(tiny[:], cst[:, 0, :]).then_inc(cs_p, 1)
            pool.wait_ge(par, 16 * 6)

            def step(i, s, what, j):
                n = 1 - s

                def ev(name, make):
                    if group(name) in what:
                        PO.in_order(name)
                        make().then_inc(PO.sem, 1)
                    else:
                        PO.in_order(name)
                        pool.drain().then_inc(PO.sem, 1)

                def mul(out, x0, x1, op=ALU.mult):
                    return lambda: pool.tensor_tensor(out, x0, x1, op)
                real = "prep" in what
                if real:
                    pool.wait_ge(z_in[n], nth(i + 1, j, 1) * 64 + 64)
                    pool.tensor_tensor(rkv[n][:], rkv[n][:], z[n][:], ALU.subtract)
                    pool.drain()
                    pool.tensor_tensor(rkv[n][:], rkv[n][:], mu[:], ALU.mult)
                    pool.drain()
                ev("rkv", mul(rkv[n][:], rkv[n][:], z[n][:], ALU.add))
                pool.drain()
                ev("kk0", mul(kk0[:], rkv[n][:, RW:2 * RW], k_k[:]))
                if real:
                    pool.wait_ge(DV.sem, DV.value("ssk", i))
                ev("rsk", mul(rsk[:], ssk[:], cst[:, 2, :], ALU.pow))
                if real:
                    pool.wait_ge(AC.sem, AC.value("cumsb", i))
                ev("ex", mul(cumsb[:], cumsb[:], sig[n][:], ALU.subtract))
                if real:
                    pool.wait_ge(DV.sem, DV.value("kkn", i))
                ev("b", mul(bb[:], kkn[:], a[n][:]))
                if real:
                    pool.wait_ge(DV.sem, DV.value("kp", i))
                    pool.wait_ge(AC.sem, AC.value("P", i))
                    pool.wait_ge(PE.sem, PE.value("MN1", i))
                ev("Kh", mul(Kh[n][:], kp[:], iP[:]))
                ev("Rh", mul(Rh[:], rkv[n][:, 0:RW], Pt[:]))
                if real:
                    pool.tensor_tensor(rk[:], rkv[n][:, 0:RW], kp[:], ALU.mult)
                    pool.drain()
                ev("rk", mul(rk[:], rk[:], r_k[:]))
                if real:
                    pool.wait_ge(PE.sem, PE.value("Tr5b", i - 1)) if not (isinstance(i, int) and i < 0) else None
                    pool.sem_inc(passed, 1)
                    pool.tensor_copy(T[n][:], i64[:].unsqueeze(1).broadcast_to([P, HV, CK]))
                ev("T_init", lambda: pool.tensor_copy(TB[n][:], ident[:].unsqueeze(1).broadcast_to([P, HV, P])))
                if "tail" in what:
                    pool.wait_ge(DV.sem, DV.value("s2", i))
                    pool.tensor_tensor(tiny[:], s2[:], cst[:, 0, :], ALU.mult)
                    pool.drain()
                    pool.tensor_tensor(tiny[:], tiny[:], cst[:, 1, :], ALU.add)
                    pool.drain()
                ev("rsy", mul(rsy[:], tiny[:], cst[:, 2, :], ALU.pow))
                if "tail" in what:
                    pool.wait_ge(DV.sem, DV.value("yn", i))
                    pool.wait_ge(g_in[n], nth(i - 1, j, 0) * 16 + 16)
                    pool.wait_ge(o_out, i * 16)
                    pool.tensor_tensor(yo[:], y[:], gn_w[:], ALU.mult)
                    pool.drain()
                    pool.tensor_tensor(yo[:], yo[:], gn_b[:], ALU.add)
                    pool.drain()
                    pool.tensor_tensor(yo[:], yo[:], bv[n][:], ALU.add)
                    pool.drain()
                if real:
                    pool.wait_ge(DV.sem, DV.value("bon", i))
                ev("bv", lambda: pool.tensor_tensor(heads(bv[n][:]), heads(rkv[n][:, 2 * RW:3 * RW]), bon[:].unsqueeze(2).broadcast_to([P, HV, DH]), ALU.mult))
                ev("out", mul(yo[:], yo[:], g[n][:]))

            steps(pool, step)

        @block.scalar
        def _(act):
            act.wait_ge(cs_p, 1)

            def step(i, s, what, j):
                n = 1 - s

                def ev(name, make, *waits):
                    if group(name) in what:
                        for e, other in waits:
                            act.wait_ge(e.sem, e.value(other, i))
                        AC.in_order(name)
                        make().then_inc(AC.sem, 1)
                    else:
                        AC.in_order(name)
                        act.drain().then_inc(AC.sem, 1)

                def evac(name, out, src=None, waits=()):
                    b = bank(name)
                    ev(name, lambda: nc.scalar.copy(out, src(b) if src else b), (PE, name), *waits)

                def four(b):
                    return b.rearrange("p (h n) -> p h n", h=4)

                def tr(level, f):
                    evac(f"Tr{level}{f}", TT[s][:, half(f), :], four)

                def x_(level, f):
                    evac(f"X{level}{f}", X[:, half(f), :], lambda b: b[:, 0:4 * CK].rearrange("p (h n) -> p h n", h=4))
                if "prep" in what:
                    act.wait_ge(PE.sem, PE.value("cum", i))
                    act.wait_ge(PO.sem, PO.value("Rh", i - 1)) if not (isinstance(i, int) and i < 0) else None
                    act.wait_ge(DV.sem, DV.value("Bh", i - 1)) if not (isinstance(i, int) and i < 0) else None
                    nc.scalar.activation(Pt[:], bank("cum"), ACT.Exp, scale=-DECAY)
                ev("P", lambda: nc.scalar.activation(iP[:], bank("cum"), ACT.Exp, scale=DECAY))
                ev("cumsb", lambda: nc.scalar.copy(cumsb[:], bank("cum")))
                tr(0, "a")
                tr(0, "b")
                x_(1, "a")
                x_(1, "b")
                for f in AB:
                    evac(f"W{f}", WU[:, half(f), :, :].rearrange("p h a d -> p h (a d)"), four)
                ev("sqk", lambda: nc.scalar.activation(sq[:], kk0[:], ACT.Square), (PO, "kk0"))
                tr(1, "a")
                tr(1, "b")
                ev("Pex", lambda: nc.scalar.activation(Pex[:], cumsb[:], ACT.Exp, scale=-DECAY), (PO, "ex"))
                x_(2, "a")
                x_(2, "b")
                evac("Y0", Y0[:])
                tr(2, "a")
                tr(2, "b")
                x_(3, "a")
                x_(3, "b")
                for f in AB:
                    evac(f"D{f}", AD[s][:, 1, half(f), :], lambda b: b[:, 0:4 * DH].rearrange("p (h n) -> p h n", h=4))
                tr(3, "a")
                tr(3, "b")
                ev("sqy", lambda: nc.scalar.activation(sq[:], y[:], ACT.Square), (DV, "yc"))
                ev("pc", lambda: nc.scalar.activation(pc[n][:], bank("pc")[:, 0:8].rearrange("p (a c) -> p a c", c=2), ACT.Exp, scale=-DECAY),
                   (PE, "pc"), (DV, "S1"))
                x_(4, "a")
                x_(4, "b")
                ev("vcopy", lambda: nc.scalar.copy(V[n][:], rkv[n][:, 2 * RW:3 * RW]), (PO, "rkv"), (PE, "Y0"))

                def t_(p):
                    evac(f"T{p}", cT[n][:, p, :, :], lambda b: b.rearrange("p (k n) -> p k n", k=4), ((DV, "RT"),))
                tr(4, "a")
                t_(0)
                tr(4, "b")
                t_(1)
                x_(5, "a")
                t_(2)
                x_(5, "b")
                t_(3)
                tr(5, "a")
                tr(5, "b")
            steps(act, step)

        @block.vector
        def _(dve):
            dve.wait_ge(cs_p, 1)
            nc.vector.tensor_scalar(bits[:, 0, :], bits[:, 0, :], CK - 1, None, ALU.bitwise_and)
            dve.drain()
            nc.vector.tensor_tensor(bits[:, 2, :], bits[:, 0, :], bits[:, 1, :], ALU.bitwise_xor)
            dve.drain()
            for b in range(len(LEVELS)):
                nc.vector.tensor_scalar(lv[:, b, :], bits[:, 2, :], b, None, ALU.logical_shift_right)
                nc.vector.tensor_scalar(bits[:, 1, :], bits[:, 0, :], b, 1, ALU.logical_shift_right, ALU.bitwise_and)
                dve.drain()
                nc.vector.tensor_scalar(lv[:, b, :], lv[:, b, :], 1.0, None, ALU.is_equal)
                dve.drain()
                nc.vector.tensor_tensor(lv[:, b, :], lv[:, b, :], bits[:, 1, :], ALU.mult)
                dve.drain()
            dve.wait_ge(par, 16 * 6)

            def step(i, s, what, j):
                n = 1 - s
                started = not (isinstance(i, int) and i < 0)

                def ev(name, make, *waits):
                    if group(name) in what:
                        for e, other in waits:
                            dve.wait_ge(e.sem, e.value(other, i))
                        if name[:2] in ("G3", "TX"):
                            dve.sem_inc(passed, 1)
                        DV.in_order(name)
                        make().then_inc(DV.sem, 1)
                    else:
                        DV.in_order(name)
                        dve.drain().then_inc(DV.sem, 1)

                def fill_T(name, level, f):
                    def make():
                        src = bank(name)[:, 0:4 * CK].rearrange("p (h n) -> p h n", h=4)
                        m = lv[:, level, :].unsqueeze(1).broadcast_to([P, 4, CK])
                        nc.vector.copy_predicated(T[s][:, half(f), :], m, src)
                        nc.vector.copy_predicated(TB[s][0:CK, half(f), 0:CK], m[0:CK], src[0:CK])
                        return nc.vector.copy_predicated(TB[s][CK:P, half(f), CK:P], m[CK:P], src[CK:P])
                    ev(name, make, (PE, name))

                def masked(name, dst, p):
                    h0 = FIRST_OF[p]
                    ev(name, lambda: nc.vector.tensor_tensor(dst[s][:, h0:h0 + 3:2, :, :].rearrange("p h k n -> p h (k n)"),
                                                             bank(name).rearrange("p (h n) -> p h n", h=2),
                                                             maskG[:].rearrange("p k n -> p (k n)").unsqueeze(1).broadcast_to([P, 2, 2 * P]), ALU.mult),
                       (PE, name))
                if "main" in what:
                    dve.wait_ge(PO.sem, PO.value("T_init", i - 1))
                for f in AB:
                    fill_T(f"G3{f}", 0, f)
                for p in range(4):
                    masked(f"G1_{p}", AR1, p)
                masked("G2_0", AR2, 0)
                masked("G2_1", AR2, 1)
                fill_T("TX1a", 1, "a")
                masked("G2_2", AR2, 2)
                fill_T("TX1b", 1, "b")
                masked("G2_3", AR2, 3)
                if "prep" in what:
                    dve.wait_ge(PO.sem, PO.value("kk0", i))
                    dve.wait_ge(z_in[n], nth(i + 1, j, 1) * 64 + 64)
                    nc.vector.scalar_tensor_tensor(kp[:], a[n][:], -1.0, k_a[:], ALU.add, ALU.mult)
                    dve.drain()
                ev("kp", lambda: nc.vector.scalar_tensor_tensor(kp[:], kp[:], 1.0, rkv[n][:, RW:2 * RW], ALU.add, ALU.mult))
                if "prep" in what:
                    dve.wait_ge(AC.sem, AC.value("sqk", i))
                    nc.vector.tensor_reduce(ssk[:], heads(sq[:]), AX.X, ALU.add)
                    dve.drain()
                ev("ssk", lambda: nc.vector.tensor_scalar(ssk[:], ssk[:], 1e-24, None, ALU.max))
                for c in range(2):
                    def mn():
                        b = bank(f"MN{c}")
                        nc.vector.tensor_tensor(MT[:, c, :, :], b[:, 0:4 * DH].rearrange("p (a d) -> p a d", d=DH),
                                                i64[:].unsqueeze(1).broadcast_to([P, 4, DH]), ALU.add)
                        return nc.vector.tensor_copy(NN[:, c, :, :], b[:, 4 * DH:8 * DH].rearrange("p (a d) -> p a d", d=DH))
                    ev(f"MN{c}", mn, (PE, f"MN{c}"))
                ev("kkn", lambda: nc.vector.tensor_tensor(heads(kkn[:]), heads(kk0[:]), rsk[:].unsqueeze(2).broadcast_to([P, HV, DH]), ALU.mult),
                   (PO, "rsk"))
                ev("RT", lambda: nc.vector.tensor_tensor(RpT[:], bank("RT").rearrange("p (a n) -> p a n", a=4), cT[n][:, :, 1, :], ALU.add), (PE, "RT"))

                def state(c):
                    def make():
                        nc.vector.tensor_tensor(St[:], bank(f"S{c}")[:, 0:4 * DH].rearrange("p (a d) -> p a d", d=DH), NN[:, c, :, :], ALU.add)
                        dve.drain()
                        dst = S[n][1] if c == 0 else S[s][0]
                        return nc.vector.tensor_tensor(dst[:], St[:], pc[n][:, :, c:c + 1].broadcast_to([P, 4, DH]), ALU.mult)
                    ev(f"S{c}", make, (PE, f"S{c}"))
                fill_T("TX2a", 2, "a")
                state(0)
                fill_T("TX2b", 2, "b")
                state(1)
                if "tail" in what:
                    dve.wait_ge(PO.sem, PO.value("out", i - 1))
                for f in AB:
                    ev(f"Y{f}", lambda: nc.vector.tensor_tensor(heads(y[:])[:, half(f), :], bank(f"Y{f}")[:, 0:4 * DH].rearrange("p (h n) -> p h n", h=4),
                                                                heads(Y0[:])[:, half(f), :], ALU.add), (PE, f"Y{f}"), (AC, "Y0"))
                dve.drain()

                def mean():
                    nc.vector.tensor_reduce(s1[:], heads(y[:]), AX.X, ALU.add)
                    dve.drain()
                    return nc.vector.tensor_scalar(s1[:], s1[:], 1.0 / DH, None, ALU.mult)
                ev("s1", mean)
                dve.drain()
                ev("yc", lambda: nc.vector.tensor_tensor(heads(y[:]), heads(y[:]), s1[:].unsqueeze(2).broadcast_to([P, HV, DH]), ALU.subtract))
                fill_T("TX3a", 3, "a")
                fill_T("TX3b", 3, "b")
                ev("Ah", lambda: nc.vector.scalar_tensor_tensor(AD[n][:, 0, :, :], heads(kkn[:]), -1.0, heads(Pex[:]), ALU.mult, ALU.mult), (AC, "Pex"), (PE, "Wb"))
                ev("Bh", lambda: nc.vector.tensor_tensor(Bh[n][:], bb[:], iP[:], ALU.mult), (PO, "b"), (PE, "MN1"))
                ev("s2", lambda: nc.vector.tensor_reduce(s2[:], heads(sq[:]), AX.X, ALU.add), (AC, "sqy"))
                fill_T("TX4a", 4, "a")
                fill_T("TX4b", 4, "b")
                ev("bon", lambda: nc.vector.tensor_reduce(bon[:], heads(rk[:]), AX.X, ALU.add), (PO, "rk"))
                ev("yn", lambda: nc.vector.tensor_tensor(heads(y[:]), heads(y[:]), rsy[:].unsqueeze(2).broadcast_to([P, HV, DH]), ALU.mult), (PO, "rsy"))
                fill_T("TX5a", 5, "a")
                fill_T("TX5b", 5, "b")

            steps(dve, step)

        @block.tensor
        def _(pe):
            pe.wait_ge(cs_p, 1)

            def step(i, s, what, j):
                n = 1 - s
                first = isinstance(i, int) and i < 0

                def job(name, make, *waits):
                    if group(name) not in what:
                        PE.in_order(name)
                        pe.drain().then_inc(PE.sem, 1)
                        return
                    ring, size = (MAIN_JOBS, BANKS) if name in MAIN_JOBS else (PREP_JOBS, 2)
                    k = ring.index(name)
                    e, other = owner(ring[k - size])
                    free = [(e, other, 0 if k >= size else 1)] if k >= size or not first else []
                    for e in (AC, DV, PO):
                        asked = [(-back, e.at[other]) for who, other, back in (*free, *waits) if who is e]
                        if asked:
                            back, at_ = max(asked)
                            pe.wait_ge(e.sem, e.nth(at_, i + back))
                    if name[:2] in ("G3", "MN", "S0", "S1", "Ya", "Yb"):
                        pe.sem_inc(passed, 1)
                    PE.in_order(name)
                    make(bank(name)).then_inc(PE.sem, 1)

                def each(name, hs, mm, *waits):
                    def make(b):
                        for h in hs:
                            last = mm(b, h)
                        return last
                    job(name, make, *waits)

                def cols(b, h, w):
                    return b[:, h * w:(h + 1) * w]

                def at(h):
                    return slice(DH * (h % 2), DH * (h % 2) + DH)

                def cum(b):
                    return nc.tensor.matmul(b, maskG[:, 1, :], sig[n][:], start=True, stop=True)

                def chunk_ends(b):
                    for p in range(4):
                        last = nc.tensor.matmul(b[:, 2 * p:2 * p + 2], sig[n][:, p * P:(p + 1) * P], ind[:], start=True, stop=True)
                    return last
                if "prep" in what:
                    pe.wait_ge(z_in[n], nth(i + 1, j, 1) * 64 + 64)
                job("cum", cum)

                def g3(b, h):
                    for c in range(2):
                        r = slice(c * CK, c * CK + CK)
                        last = nc.tensor.matmul(b[r, (h // 2) * CK:(h // 2 + 1) * CK], cT[s][at(h), h // 2, 0, r], cT[s][at(h), h // 2, 2, r], start=True, stop=True)
                    return last

                def g12(kind):
                    return lambda b, h: nc.tensor.matmul(b[:, (h // 2 % 2) * 2 * P:(h // 2 % 2 + 1) * 2 * P], cT[s][at(h), h // 2, kind, :],
                                                         cT[s][at(h), h // 2, 0:2, :], start=True, stop=True)

                def g1(p):
                    each(f"G1_{p}", (FIRST_OF[p], FIRST_OF[p] + 2), g12(2))

                def g2(p):
                    each(f"G2_{p}", (FIRST_OF[p], FIRST_OF[p] + 2), g12(3))

                def tr(level, f):
                    each(f"Tr{level}{f}", hs_of(f), lambda b, h: nc.tensor.transpose(cols(b, h // 2, P), TB[s][:, h, :], ident[:]),
                         (DV, ("G3" if level == 0 else f"TX{level}") + f, 0))

                def x_(level, f):
                    each(f"X{level}{f}", hs_of(f), lambda b, h: nc.tensor.matmul(cols(b, h // 2, CK), AR1[s][:, h, 0, :], T[s][:, h, :], start=True, stop=True),
                         (DV, ("G3" if level == 1 else f"TX{level - 1}") + f, 0), (DV, "G1_3" if f == "b" else "G1_1", 0))

                def tx(level, f):
                    each(f"TX{level}{f}", hs_of(f), lambda b, h: nc.tensor.matmul(cols(b, h // 2, CK), TT[s][:, h, :], X[:, h, :], start=True, stop=True),
                         (AC, f"X{level}{f}", 0), (AC, f"Tr{level - 1}{f}", 0))

                def w_(f):
                    each(f"W{f}", hs_of(f), lambda b, h: nc.tensor.matmul(cols(b, h // 2, P), TT[n][:, h, :], AD[n][:, :, h, :], start=True, stop=True),
                         (AC, f"Tr5{f}", 1), (AC, "Db", 1))

                def mn(c):
                    r = slice(c * CK, c * CK + CK)

                    def mm(b, h):
                        o, col = at(h), (h // 2) * DH
                        hc = slice(h * DH, h * DH + DH)
                        nc.tensor.matmul(b[o, col:col + DH], WU[r, h, 0, :], Bh[n][r, hc], start=True, stop=True)
                        nc.tensor.matmul(b[o, 4 * DH + col:4 * DH + col + DH], Bh[n][r, hc], WU[r, h, 1, :], start=True, stop=False)
                        return nc.tensor.matmul(b[o, 4 * DH + col:4 * DH + col + DH], Kh[n][r, hc], V[n][r, hc], start=False, stop=True)
                    each(f"MN{c}", range(HV), mm, (AC, "Wb", 0))

                def rt(b, h):
                    return nc.tensor.matmul(b[at(h), (h // 2) * P:(h // 2 + 1) * P], WU[:, h, 0, :], AR1[n][:, h, 1, :], start=True, stop=True)

                def y0(b, h):
                    nc.tensor.matmul(cols(b, h, DH), AR1[n][:, h, 1, :], WU[:, h, 1, :], start=True, stop=False)
                    return nc.tensor.matmul(cols(b, h, DH), AR2[n][:, h, 1, :], V[n][:, h * DH:(h + 1) * DH], start=False, stop=True)

                def s_(c):
                    each(f"S{c}", range(HV), lambda b, h: nc.tensor.matmul(b[at(h), (h // 2) * DH:(h // 2 + 1) * DH], MT[at(h), c, h // 2, :], S[n][c][at(h), h // 2, :], start=True, stop=True),
                         (DV, f"MN{c}", 0), *(((DV, "S0", 0),) if c else ((DV, "S1", 1),)))

                def y_(b, h):
                    for c in range(2):
                        r = slice(c * CK, c * CK + CK)
                        last = nc.tensor.matmul(b[r, (h // 2) * DH:(h // 2 + 1) * DH], RpT[at(h), h // 2, r], S[n][c][at(h), h // 2, :], start=True, stop=True)
                    return last

                def d_(b, h):
                    return nc.tensor.matmul(cols(b, h // 2, DH), AR2[s][:, h, 0, :], V[s][:, h * DH:(h + 1) * DH], start=True, stop=True)

                def t_(p):
                    def make(b):
                        for k, src in enumerate((AD[n][:, 0, 2 * p:2 * p + 2, :].rearrange("p h d -> p (h d)"), Rh[:, p * P:(p + 1) * P], Bh[n][:, p * P:(p + 1) * P], Kh[n][:, p * P:(p + 1) * P])):
                            last = nc.tensor.transpose(b[:, k * P:(k + 1) * P], src, ident[:])
                        return last
                    job(f"T{p}", make, (DV, "Bh", 0), (PO, "Rh", 0))
                each("G3a", hs_of("a"), g3, (AC, "T3", 1))
                each("G3b", hs_of("b"), g3)
                g1(0); g1(1); tr(0, "a"); g1(2); g1(3); tr(0, "b"); g2(0); g2(1)
                x_(1, "a"); x_(1, "b"); w_("a"); w_("b")
                tx(1, "a"); g2(2); tx(1, "b"); g2(3)
                tr(1, "a"); mn(0); tr(1, "b"); mn(1)
                x_(2, "a"); each("RT", range(HV), rt); x_(2, "b"); each("Y0", range(HV), y0); tx(2, "a"); s_(0)
                tx(2, "b"); tr(2, "a"); s_(1); tr(2, "b")
                x_(3, "a"); each("Ya", hs_of("a"), y_, (DV, "RT", 0), (DV, "S0", 0)); x_(3, "b"); each("Yb", hs_of("b"), y_)
                tx(3, "a"); each("Da", hs_of("a"), d_, (DV, "G2_3", 0), (AC, "vcopy", 1)); tx(3, "b"); each("Db", hs_of("b"), d_)
                tr(3, "a"); tr(3, "b")
                job("pc", chunk_ends)
                x_(4, "a"); x_(4, "b"); tx(4, "a"); tx(4, "b")
                tr(4, "a"); t_(0); tr(4, "b"); t_(1)
                x_(5, "a"); t_(2); x_(5, "b"); t_(3); tx(5, "a"); tx(5, "b"); tr(5, "a"); tr(5, "b")
            steps(pe, step)


def half(f):
    return slice(AB.index(f), HV, 2)


def hs_of(f):
    return range(AB.index(f), HV, 2)


GROUPS, PER_GROUP = 4, 8
EXPERTS = GROUPS * PER_GROUP
DX = 512
KX = DX // P
BLOCKS = 2 * SEQ // P + EXPERTS
SLOTS = 3
PRELOADED = SLOTS - 1
LOW = -3e38
PL = 256


def first_pairs_last(eng, n, body):
    body(0, 0)
    body(1, 1)
    with eng.Fori(1, n // 2 - 1) as j:
        body(j * 2, 0)
        body(j * 2 + 1, 1)
    body(n - 2, 0)
    body(n - 1, 1)


def known(i):
    return i if isinstance(i, int) else None


def load_expert(sp, t, weights, e, s, w_in):
    for w, name in zip(weights, ("w_gate", "w_up", "w_down")):
        sp.dma_start(w[:, s], t[name][bass.ds(e, 1)].rearrange("o (k p) n -> p (o k) n", p=P)).then_inc(w_in[s], 16)


F32R = mybir.dt.float32r
PARTS = ((0, 0), (0, 1), (1, 0))


def split_high(nc, high, src):
    return nc.scalar.copy(high, src)


def split_low(nc, low, src, high):
    return nc.vector.tensor_tensor(low, src, high, ALU.subtract)


def matmul_split(nc, out, lhsT, rhs, steps, start=True, stop=True):
    for k in range(steps):
        for n, (a, b) in enumerate(PARTS):
            last = nc.tensor.matmul(out, lhsT(a, k), rhs(b, k), start=(start and k == 0 and n == 0),
                                    stop=(stop and k == steps - 1 and n == len(PARTS) - 1))
    return last


class Rsqrt:

    def __init__(self, pool, sb, name, steps_done):
        self.pool, self.steps_done = pool, steps_done
        self.c = sb(name + "_consts", [P, 3])
        self.ms = sb(name + "_mean", [P, 1])
        for n, v in enumerate((1.0 / D, NORM_EPS, -0.5)):
            pool.memset(self.c[:, n:n + 1], v)
        pool.drain()

    def __call__(self, out, total, i, done):
        pool = self.pool
        if known(i) != 0:
            pool.wait_ge(done, i)
        pool.tensor_tensor(self.ms[:], total, self.c[:, 0:1], ALU.mult).then_inc(self.steps_done, 1)
        pool.wait_ge(self.steps_done, i * 2 + 1)
        pool.tensor_tensor(self.ms[:], self.ms[:], self.c[:, 1:2], ALU.add).then_inc(self.steps_done, 1)
        pool.wait_ge(self.steps_done, i * 2 + 2)
        pool.tensor_tensor(out, self.ms[:], self.c[:, 2:3], ALU.pow).then_inc(done, 1)


def phase_out(nc, t, ident, logits):
    with ExitStack() as ctx:
        sb = lambda n, s, d=F32: ctx.enter_context(nc.sbuf_tensor(n, s, d))
        sem = lambda n: t["semctx"].enter_context(nc.semaphore(n))
        w_sb = sb("d_w_out", [P, KD, D]); w2 = [sb(f"d_w_out_part{k}", [P, KD, D], F32R) for k in range(2)]; wr = sb("d_w_router", [P, KD, GROUPS + EXPERTS]); gain = sb("d_gain", [P, D])
        mix = [sb(f"d_mix{s}", [P, D]) for s in range(2)]; x = [sb(f"d_x{s}", [P, D]) for s in range(2)]
        mixT = [[sb(f"d_mixT{s}{k}", [P, KD, P], F32R) for k in range(2)] for s in range(2)]
        h2T = sb("d_h2T", [P, KD, P])
        h2 = [sb(f"d_h2{s}", [P, D]) for s in range(2)]; x1 = [sb(f"d_x1{s}", [P, D]) for s in range(2)]
        zeros = sb("d_zeros", [P, D]); ss = sb("d_ss", [P, 2]); rstd = sb("d_rstd", [P, 2])
        ps = lambda n, s: ctx.enter_context(nc.psum_tensor(n, s, F32))
        p_mT = ps("pd_mixT", [P, 2, BANK]); p_o = ps("pd_out", [P, 2, BANK]); p_hT = ps("pd_h2T", [P, 2, BANK]); p_l = ps("pd_logits", [P, BANK])

        s_w = [sem(f"D_w_out{h}") for h in range(2)]; w_high = sem("D_w_high"); w_low = sem("D_w_low"); s_par = sem("D_params")
        mix_in = [sem(f"D_mix_in{s}") for s in range(2)]; x_in = [sem(f"D_x_in{s}") for s in range(2)]
        mT_psum = sem("D_mixT_psum"); mT_a = sem("D_mixT_lo"); mT_d = sem("D_mixT_hi"); out_done = sem("D_out")
        x1_half = [sem(f"D_x1_half{h}") for h in range(2)]; x1_done = sem("D_x1"); ss_done = sem("D_ss"); rstd_done = sem("D_rstd"); h2_done = sem("D_h2"); h2_out = [sem(f"D_h2_store{s}") for s in range(2)]; x1_out = [sem(f"D_x1_store{s}") for s in range(2)]; zeroed = sem("D_zeros"); z_out = sem("D_zero_blocks")
        hT_psum = sem("D_h2T_psum"); hT_a = sem("D_h2T_lo"); hT_d = sem("D_h2T_hi"); lg_psum = sem("D_logits_psum"); lg_sb = sem("D_logits")
        passed = sem("D_passed")
        block = ctx.enter_context(nc.Block())

        @block.sync
        def _(sp):
            def load_mix(i, s):
                sp.dma_start(mix[s][:], t["mix"][bass.ds(i * P, P), :]).then_inc(mix_in[s], 16)

            def load_x(i, s):
                sp.dma_start(x[s][:], t["x"][bass.ds(i * P, P), :]).then_inc(x_in[s], 16)
            load_mix(0, 0)
            for h in range(2):
                sp.dma_start(w_sb[:, :, h * BANK:(h + 1) * BANK],
                             t["w_out"][:, h * BANK:(h + 1) * BANK].rearrange("(k p) n -> p k n", p=P)).then_inc(s_w[h], 16)
            load_mix(1, 1)
            load_x(0, 0)
            load_x(1, 1)
            sp.dma_start(gain[:], t["moe_norm_g"].partition_broadcast(P)).then_inc(s_par, 16)
            with nc.allow_non_contiguous_dma(reason="144 KB of router weights, once"):
                sp.dma_start(wr[:, :, 0:GROUPS], t["w_group"].rearrange("(k p) g -> p k g", p=P)).then_inc(s_par, 16)
                for g in range(GROUPS):
                    a = GROUPS + g * PER_GROUP
                    sp.dma_start(wr[:, :, a:a + PER_GROUP], t["w_expert_router"][g].rearrange("(k p) e -> p k e", p=P)).then_inc(s_par, 16)

            def step(i, s):
                more = known(i) is None or i < TILES - 2
                if more:
                    sp.wait_ge(mT_psum, i + 1)
                    load_mix(i + 2, s)
                sp.dma_start(t["y"][bass.ds(i * 2 * P + BLOCKS // 2 * P, 2 * P), :].rearrange("(b p) n -> p b n", p=P),
                             zeros[:].unsqueeze(1).broadcast_to([P, 2, D])).then_inc(z_out, 16)
                sp.wait_ge(x1_done, i + 1)
                sp.dma_start(t["x1"][bass.ds(i * P, P), :], x1[s][:]).then_inc(x1_out[s], 16)
                if more:
                    load_x(i + 2, s)
                sp.wait_ge(h2_done, i + 1)
                sp.dma_start(t["h2"][bass.ds(i * P, P), :], h2[s][:]).then_inc(h2_out[s], 16)
            sp.wait_ge(zeroed, 1)
            first_pairs_last(sp, TILES, step)
            sp.wait_ge(z_out, 16 * TILES)
            for s in range(2):
                sp.wait_ge(h2_out[s], 8 * TILES)
                sp.wait_ge(x1_out[s], 8 * TILES)

        @block.gpsimd
        def _(pool):
            pool.memset(zeros[:], 0.0).then_inc(zeroed, 1)
            rsqrt = Rsqrt(pool, sb, "d_rsqrt", sem("D_rsqrt"))

            def step(i, s):
                pool.wait_ge(ss_done, i + 1)
                pool.sem_inc(passed, 1)
                rsqrt(rstd[:, s:s + 1], ss[:, s:s + 1], i, rstd_done)
            first_pairs_last(pool, TILES, step)

        @block.scalar
        def _(act):
            def copy_mT(i, s):
                act.wait_ge(mT_psum, i + 1)
                split_high(nc, mixT[s][0][:].rearrange("p (a k) n -> p a (k n)", a=2), p_mT[:]).then_inc(mT_a, 1)

            def copy_hT(i):
                act.wait_ge(hT_psum, i + 1)
                nc.scalar.copy(h2T[:, 0:4, :], p_hT[:, 0, :].rearrange("p (k n) -> p k n", k=4)).then_inc(hT_a, 1)
            copy_mT(0, 0)
            for h in range(2):
                half = slice(h * BANK, (h + 1) * BANK)
                act.wait_ge(s_w[h], 16)
                split_high(nc, w2[0][:, :, half], w_sb[:, :, half]).then_inc(w_high, 1)

            def step(i, s):
                if known(i) != TILES - 1:
                    copy_mT(i + 1, 1 - s)
                if known(i) != 0:
                    copy_hT(i - 1)
                act.wait_ge(x1_done, i + 1)
                if known(i) is None or i >= 2:
                    act.wait_ge(h2_out[s], 8 * (i - s))
                    act.wait_ge(hT_psum, i - 1)
                nc.scalar.activation(h2[s][:], x1[s][:], ACT.Square, accum_out=ss[:, s:s + 1]).then_inc(ss_done, 1)
            first_pairs_last(act, TILES, step)
            copy_hT(TILES - 1)

        @block.vector
        def _(dve):
            def copy_mT(i, s):
                dve.wait_ge(mT_a, i + 1)
                flat = lambda k: mixT[s][k][:].rearrange("p (a k) n -> p a (k n)", a=2)
                split_low(nc, flat(1), p_mT[:], flat(0)).then_inc(mT_d, 1)

            def copy_hT(i):
                dve.wait_ge(hT_psum, i + 1)
                nc.vector.tensor_copy(h2T[:, 4:8, :], p_hT[:, 1, :].rearrange("p (k n) -> p k n", k=4)).then_inc(hT_d, 1)

            def copy_logits(i):
                dve.wait_ge(lg_psum, i + 1)
                nc.vector.tensor_copy(logits[:, bass.ds(i, 1), :], p_l[:, 0:GROUPS + EXPERTS].unsqueeze(1)).then_inc(lg_sb, 1)
            copy_mT(0, 0)
            for h in range(2):
                half = slice(h * BANK, (h + 1) * BANK)
                dve.wait_ge(w_high, h + 1)
                split_low(nc, w2[1][:, :, half], w_sb[:, :, half], w2[0][:, :, half]).then_inc(w_low, 1)
            def step(i, s):
                if known(i) != TILES - 1:
                    copy_mT(i + 1, 1 - s)
                if known(i) != 0:
                    copy_hT(i - 1)
                dve.wait_ge(x_in[s], 8 * (i + 2 - s))
                if known(i) is None or i >= 2:
                    dve.wait_ge(x1_out[s], 8 * (i - s))
                for h in range(2):
                    dve.wait_ge(out_done, i * 2 + (h + 1))
                    half = slice(h * BANK, (h + 1) * BANK)
                    nc.vector.tensor_tensor(x1[s][:, half], p_o[:, h, :], x[s][:, half], ALU.add).then_inc(x1_half[h], 1)
                dve.wait_ge(x1_half[1], i + 1)
                dve.sem_inc(x1_done, 1)
                if known(i) != 0:
                    copy_logits(i - 1)
                dve.wait_ge(rstd_done, i + 1)
                if known(i) == 0:
                    dve.wait_ge(s_par, 16 * (2 + GROUPS))
                nc.vector.scalar_tensor_tensor(h2[s][:], x1[s][:], rstd[:, s:s + 1], gain[:], ALU.mult, ALU.mult).then_inc(h2_done, 1)
            first_pairs_last(dve, TILES, step)
            copy_hT(TILES - 1)
            copy_logits(TILES - 1)

        @block.tensor
        def _(pe):
            def mix_transposes(i, s):
                pe.wait_ge(mT_d, i)
                pe.wait_ge(mix_in[s], 8 * (i + 2 - s))
                for k in range(KD):
                    last = nc.tensor.transpose(p_mT[:, k // 4, (k % 4) * P:(k % 4 + 1) * P], mix[s][:, k * P:(k + 1) * P], ident[:])
                last.then_inc(mT_psum, 1)

            def h2_transposes(i, s):
                pe.wait_ge(h2_done, i + 1)
                for k in range(KD):
                    last = nc.tensor.transpose(p_hT[:, k // 4, (k % 4) * P:(k % 4 + 1) * P], h2[s][:, k * P:(k + 1) * P], ident[:])
                last.then_inc(hT_psum, 1)

            def route(i):
                if known(i) == 0:
                    pe.wait_ge(s_par, 16 * (2 + GROUPS))
                pe.wait_ge(hT_a, i + 1)
                pe.wait_ge(hT_d, i + 1)
                pe.wait_ge(lg_sb, i)
                for k in range(KD):
                    last = nc.tensor.matmul(p_l[:, 0:GROUPS + EXPERTS], h2T[:, k, :], wr[:, k, :], start=(k == 0), stop=(k == KD - 1))
                last.then_inc(lg_psum, 1)
            mix_transposes(0, 0)

            def step(i, s):
                pe.wait_ge(mT_a, i + 1)
                pe.wait_ge(mT_d, i + 1)
                for h in range(2):
                    if known(i) != 0:
                        pe.wait_ge(x1_half[h], i)
                    pe.wait_ge(w_low, h + 1)
                    matmul_split(nc, p_o[:, h, :], lambda part, k: mixT[s][part][:, k, :],
                                 lambda part, k: w2[part][:, k, h * BANK:(h + 1) * BANK], KD).then_inc(out_done, 1)
                    if h == 0 and known(i) != TILES - 1:
                        mix_transposes(i + 1, 1 - s)
                    if h == 0 and known(i) != 0:
                        h2_transposes(i - 1, 1 - s)
                if known(i) != 0:
                    route(i - 1)
            first_pairs_last(pe, TILES, step)
            h2_transposes(TILES - 1, (TILES - 1) % 2)
            route(TILES - 1)


def phase_route(nc, t, logits, wts, dest, ids, tab, ends, order, weights, w_in, scratch):
    with ExitStack() as ctx:
        sb = lambda n, s, d=F32: ctx.enter_context(nc.sbuf_tensor(n, s, d))
        sem = lambda n: t["semctx"].enter_context(nc.semaphore(n))
        E = EXPERTS
        g8 = sb("r_group_logits", [P, TILES, 8]); gmax = sb("r_group_max", [P, TILES, 8]); gidx = sb("r_group_idx", [P, TILES, 8], U32)
        gsel = sb("r_group", [P, TILES]); goh = sb("r_group_onehot", [P, TILES, GROUPS]); goff = sb("r_group_off", [P, TILES, GROUPS])
        iota_i = sb("r_iota_i", [P, P], I32); iota = sb("r_iota", [P, P])
        gex = sb("r_group_exp", [P, TILES, GROUPS]); gsum = sb("r_group_sum", [P, TILES])
        em = sb("r_masked", [P, TILES, E]); emax = sb("r_top", [P, TILES, 8]); eidx = sb("r_top_idx", [P, TILES, 8], U32)
        esel = sb("r_experts", [P, TILES, 2]); diff = sb("r_diff", [P, TILES]); den = sb("r_den", [P, TILES])
        oh = [sb(f"r_onehot{k}", [P, TILES, E]) for k in range(2)]; both = sb("r_both", [P, TILES, E])
        before = sb("r_before", [P, P]); ones = sb("r_ones", [P, P])
        pos = sb("r_pos", [P, TILES, E]); base = sb("r_base", [P, TILES + 1, E])
        nb_i = sb("r_nblocks_i", [P, E], I32); nb = sb("r_nblocks", [P, E]); bend = sb("r_block_end", [P, E]); pstart = sb("r_row_start", [P, E])
        dest_f = sb("r_dest_f", [P, 2, TILES]); lo = sb("r_dest_lo", [P, 2, TILES], U32); hi = sb("r_dest_hi", [P, 2, TILES], U32)
        lo_f = sb("r_row_f", [P, 2, TILES]); hi_f = sb("r_block_f", [P, 2, TILES]); half = sb("r_half", [1, 4], I32)
        tok_i = sb("r_tokens_i", [P, TILES], I32); tok = sb("r_tokens", [P, TILES])
        row_oh = scratch[:, 0:4, :].rearrange("p k n -> p (k n)").rearrange("p (a r) -> p a r", r=P)
        block_tok = scratch[:, 4:6, :].rearrange("p k n -> p (k n)").rearrange("p (a b) -> p a b", b=BLOCKS)
        past = scratch[0:1, 6:8, :].rearrange("p k n -> p (k n)").rearrange("p (b e) -> p b e", e=E); be = sb("r_block_expert", [1, BLOCKS]); be_i = sb("r_block_expert_i", [1, BLOCKS], I32)
        used = sb("r_used", [1, E]); bend1 = sb("r_bend1", [1, E]); turn = sb("r_turn", [1, E])
        order_f = sb("r_order_f", [1, E]); ends_f = sb("r_ends_f", [1, E])
        hit = scratch[0:1, 6, :].rearrange("p (r e) -> p r e", e=E); looked = scratch[0:1, 7, :].rearrange("p (r e) -> p r e", e=E)
        ps_i = ctx.enter_context(nc.psum_tensor("pr_ids", [P, BANK], F32))
        ps_r = ctx.enter_context(nc.psum_tensor("pr_rank", [P, BANK], F32)); ps_t = ctx.enter_context(nc.psum_tensor("pr_total", [P, BANK], F32))
        s_c = sem("R_consts"); s_gm = sem("R_group_max"); s_ge = sem("R_group_exp"); s_d = sem("R_diff"); s_de = sem("R_diff_exp")
        s_oh = sem("R_onehots"); s_rk = sem("R_ranks"); s_ohs = sem("R_row_onehots"); s_ids = sem("R_ids")
        block = ctx.enter_context(nc.Block())

        @block.sync
        def _(sp):
            for s in range(SLOTS):
                sp.sem_inc(w_in[s], 16)
            for e in range(PRELOADED):
                load_expert(sp, t, weights, e, e, w_in)

        @block.gpsimd
        def _(pool):
            pool.iota(iota_i[:], [[1, P]], base=0, channel_multiplier=0)
            pool.iota(tok_i[:], [[P, TILES]], base=0, channel_multiplier=1)
            pool.memset(ids[:, BLOCKS:BLOCKS + 1], 0)
            pool.memset(ones[:], 1.0)
            pool.memset(before[:], 1.0)
            pool.drain()
            pool.affine_select(out=before[:], in_=before[:], compare_op=ALU.is_gt, fill=0.0, base=0,
                               pattern=[[1, P]], channel_multiplier=-1)
            pool.drain()
            pool.sem_inc(s_c, 1)

        @block.scalar
        def _(act):
            act.wait_ge(s_gm, 1)
            nc.scalar.activation(gex[:], gex[:], ACT.Exp).then_inc(s_ge, 1)
            act.wait_ge(s_d, 1)
            nc.scalar.activation(diff[:], diff[:], ACT.Exp).then_inc(s_de, 1)

        @block.tensor
        def _(pe):
            pe.wait_ge(s_c, 1)
            pe.wait_ge(s_oh, 1)
            flat = both[:].rearrange("p t e -> p (t e)")
            nc.tensor.matmul(ps_t[:], ones[:], flat, start=True, stop=True)
            nc.tensor.matmul(ps_r[:], before[:], flat, start=True, stop=True).then_inc(s_rk, 1)
            for a in range(2 * TILES):
                if a % 8 == 0:
                    pe.wait_ge(s_ohs, a // 8 + 1)
                last = nc.tensor.matmul(ps_i[:, 0:BLOCKS], row_oh[:, a, :], block_tok[:, a, :], start=(a == 0), stop=(a == 2 * TILES - 1))
            last.then_inc(s_ids, 1)

        @block.vector
        def _(dve):
            v = nc.vector
            tt = lambda o, a, b, op: v.tensor_tensor(o, a, b, op)
            v.memset(g8[:], LOW)
            dve.wait_ge(s_c, 1)
            dve.drain()
            v.tensor_copy(g8[:, :, 0:GROUPS], logits[:, :, 0:GROUPS])
            v.tensor_copy(iota[:], iota_i[:])
            v.tensor_copy(tok[:], tok_i[:])
            dve.drain()
            for i in range(TILES):
                v.max(gmax[:, i, :], g8[:, i, :])
            dve.drain()
            for i in range(TILES):
                v.max_index(gidx[:, i, :], gmax[:, i, :], g8[:, i, :])
            s4 = [P, TILES, GROUPS]
            tt(gex[:], logits[:, :, 0:GROUPS], gmax[:, :, 0:1].broadcast_to(s4), ALU.subtract).then_inc(s_gm, 1)
            dve.drain()
            v.tensor_copy(gsel[:].unsqueeze(2), gidx[:, :, 0:1])
            dve.drain()
            tt(goh[:], gsel[:].unsqueeze(2).broadcast_to(s4), iota[:, 0:GROUPS].unsqueeze(1).broadcast_to(s4), ALU.is_equal)
            dve.drain()
            v.tensor_scalar(goff[:], goh[:], 1.0, -LOW, ALU.subtract, ALU.mult)
            for g in range(GROUPS):
                a = GROUPS + g * PER_GROUP
                tt(em[:, :, g * PER_GROUP:(g + 1) * PER_GROUP], logits[:, :, a:a + PER_GROUP],
                   goh[:, :, g:g + 1].broadcast_to([P, TILES, PER_GROUP]), ALU.mult)
            dve.drain()
            for g in range(GROUPS):
                part = em[:, :, g * PER_GROUP:(g + 1) * PER_GROUP]
                tt(part, part, goff[:, :, g:g + 1].broadcast_to([P, TILES, PER_GROUP]), ALU.add)
            dve.drain()
            for i in range(TILES):
                v.max(emax[:, i, :], em[:, i, :])
            dve.drain()
            for i in range(TILES):
                v.max_index(eidx[:, i, :], emax[:, i, :], em[:, i, :])
            tt(diff[:].unsqueeze(2), emax[:, :, 1:2], emax[:, :, 0:1], ALU.subtract).then_inc(s_d, 1)
            dve.drain()
            v.tensor_copy(esel[:], eidx[:, :, 0:2])
            dve.drain()
            sE = [P, TILES, E]
            for k in range(2):
                tt(oh[k][:], esel[:, :, k:k + 1].broadcast_to(sE), iota[:, 0:E].unsqueeze(1).broadcast_to(sE), ALU.is_equal)
            dve.drain()
            tt(both[:], oh[0][:], oh[1][:], ALU.add).then_inc(s_oh, 1)
            dve.wait_ge(s_ge, 1)
            v.tensor_reduce(gsum[:], gex[:], AX.X, ALU.add)
            dve.wait_ge(s_de, 1)
            dve.drain()
            v.scalar_tensor_tensor(den[:], diff[:], 1.0, gsum[:], ALU.add, ALU.mult)
            dve.drain()
            v.reciprocal(wts[:, :, 0], den[:])
            dve.drain()
            tt(wts[:, :, 1], wts[:, :, 0], diff[:], ALU.mult)
            v.memset(base[:, 0, :], 0.0)
            dve.wait_ge(s_rk, 1)
            dve.drain()
            for i in range(TILES):
                tt(base[:, i + 1, :], base[:, i, :], ps_t[:, i * E:(i + 1) * E], ALU.add)
                dve.drain()
            v.tensor_copy(nb_i[:], base[:, TILES, :])
            dve.drain()
            v.tensor_scalar(nb_i[:], nb_i[:], P - 1, None, ALU.add)
            dve.drain()
            v.tensor_scalar(nb_i[:], nb_i[:], 7, None, ALU.arith_shift_right)
            dve.drain()
            v.tensor_copy(nb[:], nb_i[:])
            dve.drain()
            v.tensor_tensor_scan(bend[:], ones[:, 0:E], nb[:], 0.0, ALU.mult, ALU.add)
            dve.drain()
            v.tensor_scalar(used[:], nb[0:1, :], 1.0, None, ALU.min)
            v.tensor_scalar(bend1[:], bend[0:1, :], 1.0, None, ALU.add)
            tt(pstart[:], bend[:], nb[:], ALU.subtract)
            dve.drain()
            v.memset(used[:, 0:PRELOADED], 1.0)
            v.tensor_scalar(pstart[:], pstart[:], float(P), None, ALU.mult)
            tt(pos[:], base[:, 0:TILES, :], ps_r[:].rearrange("p (t e) -> p t e", e=E), ALU.add)
            dve.drain()
            tt(pos[:], pos[:], pstart[:].unsqueeze(1).broadcast_to(sE), ALU.add)
            dve.drain()
            for k in range(2):
                tt(oh[k][:], oh[k][:], pos[:], ALU.mult)
            dve.drain()
            for k in range(2):
                v.tensor_reduce(dest_f[:, k, :], oh[k][:], AX.X, ALU.add)
            dve.drain()
            v.tensor_copy(dest[:], dest_f[:])
            dve.drain()
            v.tensor_scalar(lo[:], dest[:], P - 1, None, ALU.bitwise_and)
            v.tensor_scalar(hi[:], dest[:], 7, None, ALU.logical_shift_right)
            dve.drain()
            v.tensor_copy(lo_f[:], lo[:])
            v.tensor_copy(hi_f[:], hi[:])
            dve.drain()
            flat2 = lambda ap: ap.rearrange("p k t -> p (k t)")
            sT = [P, 2 * TILES, BLOCKS]
            tt(block_tok, flat2(hi_f[:]).unsqueeze(2).broadcast_to(sT), iota[:, 0:BLOCKS].unsqueeze(1).broadcast_to(sT), ALU.is_equal)
            dve.drain()
            for k in range(2):
                part = block_tok[:, k * TILES:(k + 1) * TILES, :]
                tt(part, part, tok[:].unsqueeze(2).broadcast_to([P, TILES, BLOCKS]), ALU.mult)
            for q in range(4):
                s8 = [P, 8, P]
                tt(row_oh[:, q * 8:(q + 1) * 8, :], flat2(lo_f[:])[:, q * 8:(q + 1) * 8].unsqueeze(2).broadcast_to(s8),
                   iota[:].unsqueeze(1).broadcast_to(s8), ALU.is_equal)
                dve.drain()
                dve.sem_inc(s_ohs, 1)
            sR = [1, E, E]
            v.tensor_tensor_scan(turn[:], ones[0:1, 0:E], used[:], 0.0, ALU.mult, ALU.add)
            dve.drain()
            tt(turn[:], turn[:], used[:], ALU.subtract)
            dve.drain()
            tt(hit, turn[:].unsqueeze(1).broadcast_to(sR), iota[0:1, 0:E].unsqueeze(2).broadcast_to(sR), ALU.is_equal)
            dve.drain()
            tt(hit, hit, used[:].unsqueeze(1).broadcast_to(sR), ALU.mult)
            dve.drain()
            for table, values in ((order_f, iota[0:1, 0:E]), (ends_f, bend1[:])):
                tt(looked, hit, values.unsqueeze(1).broadcast_to(sR), ALU.mult)
                dve.drain()
                v.tensor_reduce(table[:], looked, AX.X, ALU.add)
                dve.drain()
            v.tensor_tensor_scan(bend1[:], ones[0:1, 0:E], ends_f[:], 0.0, ALU.mult, ALU.max)
            v.tensor_copy(order[:], order_f[:])
            dve.drain()
            v.tensor_copy(ends[0:1, 0:EXPERTS], bend1[:])
            dve.drain()
            for s in range(4):
                v.tensor_scalar(half[:, s:s + 1], ends[0:1, EXPERTS - 1:EXPERTS], (0, -1, 1, 0)[s], None, ALU.add)
            dve.drain()
            v.tensor_scalar(half[:], half[:], 1, 4, ALU.arith_shift_right, ALU.logical_shift_left)
            dve.drain()
            v.tensor_copy(ends[0:1, EXPERTS:EXPERTS + 4], half[:])
            sB = [1, BLOCKS, E]
            tt(past[:], bend[0:1, :].unsqueeze(1).broadcast_to(sB), iota[0:1, 0:BLOCKS].unsqueeze(2).broadcast_to(sB), ALU.is_le)
            dve.drain()
            tt(past[:], past[:], used[:].unsqueeze(1).broadcast_to(sB), ALU.mult)
            dve.drain()
            v.tensor_reduce(be[:], past[:], AX.X, ALU.add)
            dve.drain()
            v.tensor_scalar(be[:], be[:], float(E - 1), None, ALU.min)
            dve.drain()
            v.tensor_copy(be_i[:], be[:])
            dve.drain()
            for s in range(SLOTS):
                v.tensor_scalar(tab[:, 1 + s, :], be_i[:], SLOTS - s, None, ALU.add)
            v.tensor_scalar(tab[:, 0, :], be_i[:], 43, None, ALU.mult)
            dve.drain()
            v.tensor_scalar(tab[:, 1:, :], tab[:, 1:, :], 43, None, ALU.mult)
            v.tensor_scalar(tab[:, 0, :], tab[:, 0, :], 7, None, ALU.arith_shift_right)
            dve.drain()
            v.tensor_scalar(tab[:, 1:, :], tab[:, 1:, :], 7, None, ALU.arith_shift_right)
            v.scalar_tensor_tensor(tab[:, 0, :], tab[:, 0, :], -SLOTS, be_i[:], ALU.mult, ALU.add)
            dve.drain()
            v.tensor_scalar(tab[:, 1:, :], tab[:, 1:, :], 3 * 16, 16, ALU.mult, ALU.add)
            dve.wait_ge(s_ids, 1)
            v.tensor_copy(ids[:, 0:BLOCKS], ps_i[:, 0:BLOCKS])
            dve.drain()


def phase_experts(nc, t, ident, ids, tab, ends, order, weights, s_w, w_plg):
    with ExitStack() as ctx:
        sb = lambda n, s, d=F32: ctx.enter_context(nc.sbuf_tensor(n, s, d))
        sem = lambda n: t["semctx"].enter_context(nc.semaphore(n))
        wg, wu, wd = weights
        idx = [sb(f"e_idx{s}", [P, 1], U32) for s in range(2)]
        x = [sb(f"e_x{s}", [P, D]) for s in range(2)]; xT = sb("e_xT", [P, KD, P])
        sg = sb("e_silu", [P, DX]); h = sb("e_h", [P, DX]); hT = sb("e_hT", [P, KX, P]); y = [sb(f"e_y{s}", [P, D]) for s in range(2)]
        ps = lambda n, s: ctx.enter_context(nc.psum_tensor(n, s, F32))
        p_xT = ps("pe_xT", [P, 2, BANK]); p_g = ps("pe_gate", [P, BANK]); p_u = ps("pe_up", [P, BANK])
        p_hT = ps("pe_hT", [P, BANK]); p_y = ps("pe_y", [P, 2, BANK])

        s_plg = sem("E_w_pl_gate"); ended = sem("E_blocks_ended")
        x_in = [sem(f"E_x_in{s}") for s in range(2)]; xT_psum = sem("E_xT_psum"); xT_a = sem("E_xT_lo"); xT_d = sem("E_xT_hi")
        g_done = sem("E_gate"); u_done = sem("E_up"); silu_done = sem("E_silu"); h_done = sem("E_h")
        hT_psum = sem("E_hT_psum"); hT_sb = sem("E_hT"); y_psum = sem("E_y_psum"); y_half = [sem(f"E_y_half{k}") for k in range(2)]
        y_out = [sem(f"E_y_store{s}") for s in range(2)]; idx_ready = sem("E_idx"); passed = sem("E_passed"); passed_pe = sem("E_passed_pe"); passed_sp = sem("E_passed_sp")
        block = ctx.enter_context(nc.Block())

        @block.sync
        def _(sp):
            def load(turn, s, before):
                e = sp.value_load(order[0:1, bass.ds(turn, 1)], min_val=0, max_val=EXPERTS - 1)
                if known(turn) is None or turn >= SLOTS:
                    blocks = sp.value_load(ends[0:1, bass.ds(turn - SLOTS, 1)], min_val=1, max_val=BLOCKS)
                    sp.wait_ge(s_w[s], before * (3 * 16) + 16)
                    sp.sem_inc(passed_sp, 1)
                    sp.wait_ge(ended, blocks)
                    sp.sem_inc(passed_sp, 1)
                load_expert(sp, t, weights, e, s, s_w)
            for turn in range(PRELOADED, SLOTS):
                load(turn, turn, 0)
            with sp.Fori(1, EXPERTS // SLOTS) as j:
                for s in range(SLOTS):
                    load(j * SLOTS + s, s, j)
            for turn in range(EXPERTS // SLOTS * SLOTS, EXPERTS):
                load(turn, turn % SLOTS, EXPERTS // SLOTS)
            sp.dma_start(w_plg[:], t["w_pl_gate"].rearrange("(k p) n -> p k n", p=P)).then_inc(s_plg, 16)
            for s in range(SLOTS):
                sp.wait_ge(s_w[s], 3 * 16 * len(range(s, EXPERTS, SLOTS)) + 16)
            sp.wait_ge(s_plg, 16)

        def steps(eng, body):
            last = eng.value_load(ends[0:1, EXPERTS - 1:EXPERTS], min_val=BLOCKS // 2 + 1, max_val=BLOCKS)
            for i in range(4):
                body(i, i % 2, nullcontext)
            with eng.Fori(2, BLOCKS // 4) as j:
                body(j * 2, 0, nullcontext)
                body(j * 2 + 1, 1, nullcontext)
            with eng.Fori(BLOCKS // 4, BLOCKS // 2) as j:
                for s in range(2):
                    with eng.If(last > j * 2 + s):
                        body(j * 2 + s, s, lambda: eng.If(last > j * 2 + (s + 1)))

        @block.gpsimd
        def _(pool):
            def gather(i, s):
                if known(i) is None or i >= 2:
                    pool.wait_ge(xT_psum, i - 1)
                pool.sem_inc(passed, 1)
                pool.tensor_copy(idx[s][:], ids[:, bass.ds(i, 1)]).then_inc(idx_ready, 1)
                pool.wait_ge(idx_ready, i + 1)
                pool.sem_inc(passed, 1)
                pool.indirect_dma_start(x[s][:], None, t["h2"], bass.IndirectOffsetOnAxis(ap=idx[s][:], axis=0)).then_inc(x_in[s], 16)
            gather(0, 0)

            def step(i, s, fresh):
                with fresh():
                    gather(i + 1, 1 - s)
            steps(pool, step)
            counts = [pool.value_load(ends[0:1, EXPERTS + k:EXPERTS + k + 1], min_val=16, max_val=8 * BLOCKS + 16) for k in range(4)]
            for s in range(2):
                pool.wait_ge(y_out[s], counts[s])
                pool.sem_inc(passed, 1)
                pool.wait_ge(x_in[s], counts[2 + s])
                pool.sem_inc(passed, 1)

        def store_free(eng, i, s):
            if known(i) is None or i >= 2:
                eng.wait_ge(y_out[s], 8 * (i - s))

        @block.scalar
        def _(act):
            def copy_xT(i):
                act.wait_ge(xT_psum, i + 1)
                nc.scalar.copy(xT[:, 0:4, :], p_xT[:, 0, :].rearrange("p (k n) -> p k n", k=4)).then_inc(xT_a, 1)
            copy_xT(0)

            def step(i, s, fresh):
                with fresh():
                    act.wait_ge(g_done, i + 1)
                    act.wait_ge(h_done, i)
                    nc.scalar.activation(sg[:], p_g[:], ACT.Silu).then_inc(silu_done, 1)
                    copy_xT(i + 1)
                if known(i) != 0:
                    copy_y(i - 1, 1 - s)
                    for k in range(2):
                        act.wait_ge(y_half[k], i)
                    act.dma_start(t["y"][bass.ds((i - 1) * P, P), :], y[1 - s][:]).then_inc(y_out[1 - s], 16)

            def copy_y(i, s):
                act.wait_ge(y_psum, i + 1)
                store_free(act, i, s)
                nc.scalar.copy(y[s][:, 0:BANK], p_y[:, 0, :]).then_inc(y_half[0], 1)
            steps(act, step)

        @block.vector
        def _(dve):
            def copy_xT(i):
                dve.wait_ge(xT_psum, i + 1)
                nc.vector.tensor_copy(xT[:, 4:8, :], p_xT[:, 1, :].rearrange("p (k n) -> p k n", k=4)).then_inc(xT_d, 1)

            def copy_hT(i):
                dve.wait_ge(hT_psum, i + 1)
                nc.vector.tensor_copy(hT[:], p_hT[:].rearrange("p (k n) -> p k n", k=KX)).then_inc(hT_sb, 1)

            def copy_y(i, s):
                dve.wait_ge(y_psum, i + 1)
                dve.sem_inc(ended, 1)
                store_free(dve, i, s)
                nc.vector.tensor_copy(y[s][:, BANK:D], p_y[:, 1, :]).then_inc(y_half[1], 1)
            dve.sem_inc(ended, 1)
            copy_xT(0)

            def step(i, s, fresh):
                if known(i) != 0:
                    copy_hT(i - 1)
                with fresh():
                    dve.wait_ge(silu_done, i + 1)
                    dve.wait_ge(u_done, i + 1)
                    dve.wait_ge(hT_psum, i)
                    nc.vector.tensor_tensor(h[:], sg[:], p_u[:], ALU.mult).then_inc(h_done, 1)
                    copy_xT(i + 1)
                if known(i) != 0:
                    copy_y(i - 1, 1 - s)
            steps(dve, step)

        @block.tensor
        def _(pe):
            def x_transposes(i, s):
                pe.wait_ge(x_in[s], 8 * (i + 2 - s))
                pe.wait_ge(xT_a, i)
                pe.wait_ge(xT_d, i)
                for k in range(KD):
                    last = nc.tensor.transpose(p_xT[:, k // 4, (k % 4) * P:(k % 4 + 1) * P], x[s][:, k * P:(k + 1) * P], ident[:])
                last.then_inc(xT_psum, 1)

            def h_transposes(i):
                pe.wait_ge(h_done, i + 1)
                pe.wait_ge(hT_sb, i)
                for k in range(KX):
                    last = nc.tensor.transpose(p_hT[:, k * P:(k + 1) * P], h[:, k * P:(k + 1) * P], ident[:])
                last.then_inc(hT_psum, 1)

            def slot_of(i):
                return pe.value_load(tab[0:1, 0, bass.ds(i, 1)], min_val=0, max_val=SLOTS - 1)

            def gate_up(i, s):
                slot = slot_of(i)
                loads = [pe.value_load(tab[0:1, 1 + k, bass.ds(i, 1)], min_val=16, max_val=48 * EXPERTS) for k in range(SLOTS)]
                for k in range(SLOTS):
                    pe.wait_ge(s_w[k], loads[k])
                    pe.sem_inc(passed_pe, 1)
                pe.wait_ge(xT_a, i + 1)
                pe.wait_ge(xT_d, i + 1)
                pe.wait_ge(silu_done, i)
                for w, bank, done in ((wg, p_g, g_done), (wu, p_u, u_done)):
                    if done is u_done:
                        pe.wait_ge(h_done, i)
                    for k in range(KD):
                        last = nc.tensor.matmul(bank[:], xT[:, k, :], w[:, bass.ds(slot, 1), k, :].rearrange("p o n -> p (o n)"),
                                                start=(k == 0), stop=(k == KD - 1))
                    last.then_inc(done, 1)

            def down(i):
                slot = slot_of(i)
                pe.wait_ge(hT_sb, i + 1)
                for half in range(2):
                    pe.wait_ge(y_half[half], i)
                    for k in range(KX):
                        last = nc.tensor.matmul(p_y[:, half, :], hT[:, k, :],
                                                wd[:, bass.ds(slot, 1), k, half * BANK:(half + 1) * BANK].rearrange("p o n -> p (o n)"),
                                                start=(k == 0), stop=(k == KX - 1))
                last.then_inc(y_psum, 1)
            x_transposes(0, 0)

            def step(i, s, fresh):
                if known(i) != 0:
                    h_transposes(i - 1)
                with fresh():
                    gate_up(i, s)
                    x_transposes(i + 1, 1 - s)
                if known(i) != 0:
                    down(i - 1)
            steps(pe, step)


def phase_final(nc, t, ident, wq, wts, dest):
    with ExitStack() as ctx:
        sb = lambda n, s, d=F32: ctx.enter_context(nc.sbuf_tensor(n, s, d))
        sem = lambda n: t["semctx"].enter_context(nc.semaphore(n))
        wp = sb("f_w_pl", [P, PL // P, D]); g_gain = sb("f_gate_gain", [P, D]); p_gain = sb("f_pl_gain", [P, D])
        idx = [[sb(f"f_idx{s}{k}", [P, 1], U32) for k in range(2)] for s in range(2)]
        y = [[sb(f"f_y{s}{k}", [P, D]) for k in range(2)] for s in range(2)]
        pe_in = [sb(f"f_p{s}", [P, PL]) for s in range(2)]; pT = [[sb(f"f_pT{s}{k}", [P, PL // P, P], F32R) for k in range(2)] for s in range(2)]
        x1 = [sb(f"f_x1{s}", [P, D]) for s in range(2)]; x2 = [sb(f"f_x2{s}", [P, D]) for s in range(2)]; hg = sb("f_hg", [P, D]); hgT = [sb(f"f_hgT{k}", [P, KD, P], F32R) for k in range(2)]
        wq2 = [sb(f"f_w_gate{k}", [P, KD, D], F32R) for k in range(2)]; wp2 = [sb(f"f_w_pl{k}", [P, PL // P, D], F32R) for k in range(2)]
        junk = sb("f_junk", [P, D]); junk2 = sb("f_junk2", [P, D], mybir.dt.bfloat16); gate = sb("f_gate", [P, D]); pl = [sb(f"f_pl{s}", [P, D]) for s in range(2)]; out = [sb(f"f_out{s}", [P, D]) for s in range(2)]
        ss = sb("f_ss", [P, 2]); rstd = sb("f_rstd", [P, 2]); pss = sb("f_pl_ss", [P, 2]); prstd = sb("f_pl_rstd", [P, 2])
        ps = lambda n, s: ctx.enter_context(nc.psum_tensor(n, s, F32))
        p_hT = ps("pf_hgT", [P, 2, BANK]); p_g = ps("pf_gate", [P, 2, BANK]); p_pT = ps("pf_pT", [P, BANK]); p_pl = ps("pf_pl", [P, 2, BANK])

        x1_in = [sem(f"F_x1_in{s}") for s in range(2)]; s_wp = sem("F_w_pl"); s_par = [sem(f"F_gain{k}") for k in range(2)]; p_in = [sem(f"F_p_in{s}") for s in range(2)]
        y_in = [sem(f"F_y_in{s}") for s in range(2)]; part = sem("F_x2_part"); x2_done = sem("F_x2"); ss_done = sem("F_ss"); rstd_done = sem("F_rstd"); hg_done = sem("F_hg")
        hT_psum = sem("F_hgT_psum"); hT_a = sem("F_hgT_lo"); hT_d = sem("F_hgT_hi"); pT_psum = sem("F_pT_psum"); pT_a = sem("F_pT_high"); pT_sb = sem("F_pT_low"); w_high = sem("F_w_high"); w_low = sem("F_w_low")
        g_psum = sem("F_gate_psum"); gate_done = sem("F_gate"); pl_psum = sem("F_pl_psum"); pss_done = sem("F_pl_ss"); prstd_done = sem("F_pl_rstd")
        pl_read = sem("F_pl_read"); out_done = sem("F_out_ready"); stored = [sem(f"F_store{s}") for s in range(2)]; idx_ready = sem("F_idx"); passed = sem("F_passed")
        block = ctx.enter_context(nc.Block())

        @block.sync
        def _(sp):
            def load_p(i, s):
                sp.dma_start(pe_in[s][:], t["p"][bass.ds(i * P, P), :]).then_inc(p_in[s], 16)

            def load_x1(i, s):
                sp.dma_start(x1[s][:], t["x1"][bass.ds(i * P, P), :]).then_inc(x1_in[s], 16)
            load_p(0, 0)
            load_p(1, 1)
            load_x1(0, 0)
            sp.dma_start(wp[:], t["w_pl"].rearrange("(k p) n -> p k n", p=P)).then_inc(s_wp, 16)
            sp.dma_start(g_gain[:], t["pl_gate_norm_g"].partition_broadcast(P)).then_inc(s_par[0], 16)
            load_x1(1, 1)
            sp.dma_start(p_gain[:], t["pl_norm_g"].partition_broadcast(P)).then_inc(s_par[1], 16)

            def step(i, s):
                if known(i) is None or i < TILES - 2:
                    sp.wait_ge(pT_psum, i + 1)
                    load_p(i + 2, s)
                    sp.wait_ge(x2_done, i + 1)
                    load_x1(i + 2, s)
                sp.wait_ge(out_done, i + 1)
                sp.dma_start(t["out"][bass.ds(i * P, P), :], out[s][:]).then_inc(stored[s], 16)
            first_pairs_last(sp, TILES, step)
            for s in range(2):
                sp.wait_ge(stored[s], 16 * (TILES // 2))

        @block.gpsimd
        def _(pool):
            rsqrt = Rsqrt(pool, sb, "f_rsqrt", sem("F_rsqrt"))
            rsqrt_pl = Rsqrt(pool, sb, "f_rsqrt_pl", sem("F_rsqrt_pl"))

            def gather(i, s):
                if known(i) is None or i >= 2:
                    pool.wait_ge(x2_done, i - 1)
                pool.sem_inc(passed, 1)
                for k in range(2):
                    pool.tensor_copy(idx[s][k][:], dest[:, k, bass.ds(i, 1)]).then_inc(idx_ready, 1)
                pool.wait_ge(idx_ready, i * 2 + 2)
                pool.sem_inc(passed, 1)
                for k in range(2):
                    pool.indirect_dma_start(y[s][k][:], None, t["y"], bass.IndirectOffsetOnAxis(ap=idx[s][k][:], axis=0)).then_inc(y_in[s], 16)

            def norm(i, s):
                pool.wait_ge(ss_done, i + 1)
                pool.sem_inc(passed, 1)
                rsqrt(rstd[:, s:s + 1], ss[:, s:s + 1], i, rstd_done)

            def norm_pl(i, s):
                pool.wait_ge(pss_done, i + 1)
                pool.sem_inc(passed, 1)
                rsqrt_pl(prstd[:, s:s + 1], pss[:, s:s + 1], i, prstd_done)
            gather(0, 0)
            gather(1, 1)
            norm_pl(0, 0)
            norm(0, 0)

            def step(i, s, more=True):
                if more:
                    gather(i + 2, s)
                if known(i) != TILES - 1:
                    norm(i + 1, 1 - s)
                    norm_pl(i + 1, 1 - s)
            with pool.Fori(0, TILES // 2 - 1) as j:
                step(j * 2, 0)
                step(j * 2 + 1, 1)
            step(TILES - 2, 0, False)
            step(TILES - 1, 1, False)

        @block.scalar
        def _(act):
            def square(i, s):
                act.wait_ge(ss_done, i)
                act.wait_ge(x2_done, i + 1)
                nc.scalar.activation(junk[:], x2[s][:], ACT.Square, accum_out=ss[:, s:s + 1]).then_inc(ss_done, 1)

            def copy_hT(i):
                act.wait_ge(hT_psum, i + 1)
                split_high(nc, hgT[0][:].rearrange("p (a k) n -> p a (k n)", a=2), p_hT[:]).then_inc(hT_a, 1)

            def copy_pT(i, s):
                act.wait_ge(pT_psum, i + 1)
                split_high(nc, pT[s][0][:].rearrange("p k n -> p (k n)"), p_pT[:, 0:PL]).then_inc(pT_a, 1)

            def square_pl(i, s):
                act.wait_ge(pl_psum, i + 1)
                act.wait_ge(pss_done, i)
                nc.scalar.activation(junk2[:].rearrange("p (a n) -> p a n", a=2), p_pl[:], ACT.Square,
                                     accum_out=pss[:, s:s + 1]).then_inc(pss_done, 1)
            copy_pT(0, 0)
            copy_pT(1, 1)
            act.wait_ge(s_wp, 16)
            split_high(nc, wp2[0][:], wp[:]).then_inc(w_high, 1)
            for h in range(2):
                half = slice(h * BANK, (h + 1) * BANK)
                split_high(nc, wq2[0][:, :, half], wq[:, :, half]).then_inc(w_high, 1)
            square_pl(0, 0)
            square(0, 0)
            copy_hT(0)

            def step(i, s):
                if known(i) != TILES - 1:
                    square(i + 1, 1 - s)
                act.wait_ge(g_psum, i + 1)
                act.wait_ge(out_done, i)
                nc.scalar.activation(gate[:].rearrange("p (a n) -> p a n", a=2), p_g[:], ACT.Sigmoid).then_inc(gate_done, 1)
                if known(i) != TILES - 1:
                    copy_hT(i + 1)
                    if known(i) is None or i < TILES - 2:
                        copy_pT(i + 2, s)
                    square_pl(i + 1, 1 - s)
            first_pairs_last(act, TILES, step)

        @block.vector
        def _(dve):
            def combine(i, s):
                dve.wait_ge(y_in[s], 16 * (i + 2 - s))
                dve.wait_ge(x1_in[s], 8 * (i + 2 - s))
                if known(i) is None or i >= 2:
                    dve.wait_ge(out_done, i - 1)
                nc.vector.scalar_tensor_tensor(x2[s][:], y[s][0][:], wts[:, bass.ds(i, 1), 0], x1[s][:], ALU.mult, ALU.add)
                dve.drain()
                nc.vector.scalar_tensor_tensor(x2[s][:], y[s][1][:], wts[:, bass.ds(i, 1), 1], x2[s][:], ALU.mult, ALU.add).then_inc(x2_done, 1)

            def make_hg(i, s):
                dve.wait_ge(rstd_done, i + 1)
                dve.wait_ge(hT_psum, i)
                dve.wait_ge(x2_done, i + 1)
                nc.vector.scalar_tensor_tensor(hg[:], x2[s][:], rstd[:, s:s + 1], g_gain[:], ALU.mult, ALU.mult).then_inc(hg_done, 1)

            def copy_hT(i):
                dve.wait_ge(hT_a, i + 1)
                flat = lambda k: hgT[k][:].rearrange("p (a k) n -> p a (k n)", a=2)
                split_low(nc, flat(1), p_hT[:], flat(0)).then_inc(hT_d, 1)

            def copy_pT(i, s):
                dve.wait_ge(pT_a, i + 1)
                flat = lambda k: pT[s][k][:].rearrange("p k n -> p (k n)")
                split_low(nc, flat(1), p_pT[:, 0:PL], flat(0)).then_inc(pT_sb, 1)

            def norm_pl(i, s):
                dve.wait_ge(prstd_done, i + 1)
                nc.vector.scalar_tensor_tensor(pl[s][:].rearrange("p (a n) -> p a n", a=2), p_pl[:], prstd[:, s:s + 1],
                                               p_gain[:].rearrange("p (a n) -> p a n", a=2), ALU.mult, ALU.mult).then_inc(pl_read, 1)

            def finish(i, s):
                dve.wait_ge(gate_done, i + 1)
                dve.wait_ge(pl_read, i + 1)
                nc.vector.tensor_tensor(pl[s][:], pl[s][:], gate[:], ALU.mult)
                dve.drain()
                if known(i) is None or i >= 2:
                    dve.wait_ge(stored[s], 8 * (i - s))
                nc.vector.tensor_tensor(out[s][:], pl[s][:], x2[s][:], ALU.add).then_inc(out_done, 1)
            copy_pT(0, 0)
            copy_pT(1, 1)
            dve.wait_ge(w_high, 1)
            split_low(nc, wp2[1][:], wp[:], wp2[0][:]).then_inc(w_low, 1)
            for h in range(2):
                half = slice(h * BANK, (h + 1) * BANK)
                dve.wait_ge(w_high, h + 2)
                split_low(nc, wq2[1][:, :, half], wq[:, :, half], wq2[0][:, :, half]).then_inc(w_low, 1)
            combine(0, 0)
            dve.wait_ge(s_par[0], 16)
            make_hg(0, 0)
            copy_hT(0)
            dve.wait_ge(s_par[1], 16)

            def step(i, s):
                if known(i) != 0:
                    finish(i - 1, 1 - s)
                if known(i) != TILES - 1:
                    combine(i + 1, 1 - s)
                norm_pl(i, s)
                if known(i) != TILES - 1:
                    make_hg(i + 1, 1 - s)
                    copy_hT(i + 1)
                    if known(i) is None or i < TILES - 2:
                        copy_pT(i + 2, s)
            first_pairs_last(dve, TILES, step)
            finish(TILES - 1, 1)

        @block.tensor
        def _(pe):
            def hg_transposes(i):
                pe.wait_ge(hg_done, i + 1)
                for k in range(KD):
                    last = nc.tensor.transpose(p_hT[:, k // 4, (k % 4) * P:(k % 4 + 1) * P], hg[:, k * P:(k + 1) * P], ident[:])
                last.then_inc(hT_psum, 1)

            def p_transposes(i, s):
                pe.wait_ge(p_in[s], 8 * (i + 2 - s))
                pe.wait_ge(pT_sb, i)
                for k in range(PL // P):
                    last = nc.tensor.transpose(p_pT[:, k * P:(k + 1) * P], pe_in[s][:, k * P:(k + 1) * P], ident[:])
                last.then_inc(pT_psum, 1)

            def embed(i, s):
                pe.wait_ge(pT_sb, i + 1)
                pe.wait_ge(pl_read, i)
                for h in range(2):
                    last = matmul_split(nc, p_pl[:, h, :], lambda part, k: pT[s][part][:, k, :],
                                        lambda part, k: wp2[part][:, k, h * BANK:(h + 1) * BANK], PL // P)
                last.then_inc(pl_psum, 1)
            p_transposes(0, 0)
            p_transposes(1, 1)
            pe.wait_ge(w_low, 1)
            embed(0, 0)
            hg_transposes(0)

            def step(i, s):
                pe.wait_ge(hT_d, i + 1)
                pe.wait_ge(gate_done, i)
                for h in range(2):
                    pe.wait_ge(w_low, h + 2)
                    last = matmul_split(nc, p_g[:, h, :], lambda part, k: hgT[part][:, k, :],
                                        lambda part, k: wq2[part][:, k, h * BANK:(h + 1) * BANK], KD)
                last.then_inc(g_psum, 1)
                if known(i) != TILES - 1:
                    hg_transposes(i + 1)
                    if known(i) is None or i < TILES - 2:
                        p_transposes(i + 2, s)
                    embed(i + 1, 1 - s)
            first_pairs_last(pe, TILES, step)


def block_kernel(nc, a):
    with ExitStack() as ctx:
        sb = lambda n, s, d=F32: ctx.enter_context(nc.sbuf_tensor(n, s, d))
        dram = lambda n, s, d=F32: nc.dram_tensor(n, s, d).ap()
        t = {name: ap[0] for name, ap in a.items()}
        t["p"] = t["p"][0]
        t["semctx"] = ctx
        t["v"] = dram("s_v", [SEQ, RW]); t["qT"] = dram("s_qT", [SEQ, RW]); t["kT"] = dram("s_kT", [SEQ, RW])
        t["zr"] = dram("s_zr", [SEQ + 1, QKV]); t["lo"] = dram("s_lora", [3, SEQ, RW]); t["mix"] = dram("s_mix", [SEQ, D])
        t["x1"] = dram("s_x1", [SEQ, D]); t["h2"] = dram("s_h2", [SEQ, D]); t["y"] = dram("s_y", [BLOCKS * P, D]);
        ident = sb("ident", [P, P])
        phase_constants(nc, t, ident)
        with ExitStack() as early:
            t["semctx"] = early
            spent = phase_project(nc, t, ident)
            t["semctx"] = ctx
            phase_attention(nc, t, ident, spent)
        phase_rwkv(nc, t, ident)
        wts = sb("expert_weights", [P, TILES, 2]); dest = sb("expert_rows", [P, 2, TILES], U32)
        ids = sb("row_tokens", [P, BLOCKS + 1], U32); tab = sb("block_table", [1, 1 + SLOTS, BLOCKS], I32); ends = sb("turn_ends", [1, EXPERTS + 4], I32)
        order = sb("turn_experts", [1, EXPERTS], I32)
        w_in = [ctx.enter_context(nc.semaphore(f"E_weights_in{s}")) for s in range(SLOTS)]
        w_plg = sb("w_pl_gate_sb", [P, KD, D])
        with ExitStack() as moe:
            msb = lambda n, s, d=F32: moe.enter_context(nc.sbuf_tensor(n, s, d))
            logits = msb("router_logits", [P, TILES, GROUPS + EXPERTS])
            phase_out(nc, t, ident, logits)
            weights = [msb("w_gate_sb", [P, SLOTS, KD, DX]), msb("w_up_sb", [P, SLOTS, KD, DX]), msb("w_down_sb", [P, SLOTS, KX, D])]
            phase_route(nc, t, logits, wts, dest, ids, tab, ends, order, weights, w_in, w_plg)
            phase_experts(nc, t, ident, ids, tab, ends, order, weights, w_in, w_plg)
        phase_final(nc, t, ident, w_plg, wts, dest)


INPUTS = ["x", "p", "positions", "attn_norm_g", "w_in", "q_norm_g", "k_norm_g", "lambda_q1", "lambda_k1", "lambda_q2", "lambda_k2",
          "diff_out_g", "mu_rkv", "mu_wag", "w0", "w_lora_a", "w_lora_b", "a0", "a_lora_a", "a_lora_b", "g_lora_a", "g_lora_b",
          "k_k", "k_a", "r_k", "gn_w", "gn_b", "w_out", "moe_norm_g", "w_group", "w_expert_router", "w_gate", "w_up", "w_down",
          "w_pl", "pl_norm_g", "pl_gate_norm_g", "w_pl_gate"]


def kernel(**inputs):
    import numpy as _np
    import concourse.bacc as _bacc
    from concourse import mybir as _mybir
    from concourse.bass_utils import run_bass_kernel_spmd as _run

    nc = _bacc.Bacc("TRN2", target_bir_lowering=False, num_devices=1)
    arrays, aps = {}, {}
    for name in INPUTS:
        arr = _np.ascontiguousarray(inputs[name])
        arrays[f"in_{name}_dram"] = arr
        aps[name] = nc.dram_tensor(f"in_{name}_dram", arr.shape, _mybir.dt.from_np(arr.dtype), kind="ExternalInput").ap()
    aps["out"] = nc.dram_tensor("out_dram", (1, SEQ, D), F32, kind="ExternalOutput").ap()
    block_kernel(nc, aps)
    return _run(nc, [arrays], core_ids=[0]).results[0]["out_dram"]
```
